# Optimizing a Trainium2 kernel written in Bass

```python
import math
import jax, jax.numpy as jnp
from jax import lax
import numpy as np

D_MODEL = 1024
BATCH = 1
SEQ = 512
DEPTH = 2
DEC_BATCH = 8
DEC_SEQ = 4
PAST_LEN = 256
PAGE_SIZE = 128

N_A = DEPTH // 2
N_B = DEPTH - N_A
MEM_TOKENS = 256
MEM_HEADS = 4
MEM_HEAD_DIM = D_MODEL // 16
MEM_WIDTH = MEM_HEADS * MEM_HEAD_DIM
MIX_WIDTH = D_MODEL - MEM_WIDTH
POOL_WINDOWS = (2, 4, 8, 16)
POOL_GROUPS = len(POOL_WINDOWS)
GROUP_WIDTH = MIX_WIDTH // POOL_GROUPS
POOL_HIST = max(POOL_WINDOWS) - 1
DIFF_HEAD_DIM = 64
DIFF_HEADS = MIX_WIDTH // (2 * DIFF_HEAD_DIM)
DIFF_V_DIM = 2 * DIFF_HEAD_DIM
D_FF = 4 * D_MODEL
ROPE_THETA = 10000.0
Q_BLOCK = 128
RMS_EPS = 1e-6
NEG_INF = -1e30

kernel_name = "yoco_pool_diffattn_mem_decoder_step"

def rmsnorm(x, g):
    xf = x.astype(jnp.float32)
    y = xf * lax.rsqrt(jnp.mean(xf * xf, axis=-1, keepdims=True) + RMS_EPS)
    return (y * g.astype(jnp.float32)).astype(x.dtype)

def rope(x, pos):
    d = x.shape[-1]
    inv = 1.0 / (ROPE_THETA ** (jnp.arange(0, d, 2, dtype=jnp.float32) / d))
    ang = pos.astype(jnp.float32)[:, None] * inv[None, :]
    shape = (1, pos.shape[0]) + (1,) * (x.ndim - 3) + (d,)
    cos = jnp.concatenate([jnp.cos(ang), jnp.cos(ang)], axis=-1).reshape(shape)
    sin = jnp.concatenate([jnp.sin(ang), jnp.sin(ang)], axis=-1).reshape(shape)
    xf = x.astype(jnp.float32)
    rot = jnp.concatenate([-xf[..., d // 2:], xf[..., :d // 2]], axis=-1)
    return (xf * cos + rot * sin).astype(x.dtype)

def multi_scale_pool(u, pos):
    L = u.shape[1]
    c = jnp.cumsum(u.astype(jnp.float32), axis=1)
    outs = []
    for g, w in enumerate(POOL_WINDOWS):
        cg = c[:, :, g]
        prev = jnp.pad(cg, ((0, 0), (w, 0), (0, 0)))[:, :L]
        cnt = jnp.minimum(w, pos + 1).astype(jnp.float32)
        outs.append((cg - prev) / cnt[None, :, None])
    mean = jnp.stack(outs, axis=2)
    return (mean - u.astype(jnp.float32)).astype(u.dtype)

def diff_core(q, k, v, q_pos, k_pos, lam):
    s = jnp.einsum('bqhjd,bkhjd->bhjqk', q, k, preferred_element_type=jnp.float32) * (DIFF_HEAD_DIM ** -0.5)
    mask = k_pos[None, :] <= q_pos[:, None]
    s = jnp.where(mask[None, None, None], s, NEG_INF)
    p = jax.nn.softmax(s, axis=-1)
    a = p[:, :, 0] - lam * p[:, :, 1]
    return jnp.einsum('bhqk,bkhe->bqhe', a.astype(v.dtype), v)

def memory_attention(q, mk, mv):
    s = jnp.einsum('bqhd,bmhd->bhqm', q, mk, preferred_element_type=jnp.float32) * (MEM_HEAD_DIM ** -0.5)
    p = jax.nn.softmax(s, axis=-1)
    return jnp.einsum('bhqm,bmhd->bqhd', p.astype(mv.dtype), mv)

def trunk(x, pos, pool_hist, mem_k, mem_v, past_k, past_v, p):
    B, T, _ = x.shape
    pool_new = []
    k_new = v_new = k_all = v_all = None
    for l in range(DEPTH):
        if l == N_A:
            hk = rmsnorm(x, p['kv_norm'])
            k_new = rope((hk @ p['w_k']).reshape(B, T, DIFF_HEADS, 2, DIFF_HEAD_DIM), pos)
            v_new = (hk @ p['w_v']).reshape(B, T, DIFF_HEADS, DIFF_V_DIM)
            if past_k is None:
                k_all, v_all = k_new, v_new
            else:
                k_all = jnp.concatenate([past_k, k_new], axis=1)
                v_all = jnp.concatenate([past_v, v_new], axis=1)
        h = rmsnorm(x, p['norm1'][l])
        z = h @ p['w_in'][l]
        z_mix, z_mem = z[..., :MIX_WIDTH], z[..., MIX_WIDTH:]
        if l < N_A:
            u = z_mix.reshape(B, T, POOL_GROUPS, GROUP_WIDTH)
            if pool_hist is None:
                ext, pos_ext = u, pos
            else:
                hist = pool_hist[l].reshape(B, POOL_HIST, POOL_GROUPS, GROUP_WIDTH)
                ext = jnp.concatenate([hist, u], axis=1)
                pos_ext = jnp.concatenate([pos[0] - POOL_HIST + jnp.arange(POOL_HIST, dtype=pos.dtype), pos])
            pooled = multi_scale_pool(ext, pos_ext)[:, -T:]
            pool_new.append(ext[:, -POOL_HIST:].reshape(B, POOL_HIST, MIX_WIDTH))
            mix = jnp.einsum('btgc,gcd->btgd', pooled, p['w_pool'][l]).reshape(B, T, MIX_WIDTH) * p['pool_scale'][l]
        else:
            j = l - N_A
            lam_init = 0.8 - 0.6 * math.exp(-0.3 * l)
            lam = (jnp.exp(jnp.sum(p['lambda_q1'][j].astype(jnp.float32) * p['lambda_k1'][j].astype(jnp.float32)))
                   - jnp.exp(jnp.sum(p['lambda_q2'][j].astype(jnp.float32) * p['lambda_k2'][j].astype(jnp.float32)))
                   + lam_init)
            q = rope(z_mix.reshape(B, T, DIFF_HEADS, 2, DIFF_HEAD_DIM), pos)
            k_pos = jnp.arange(k_all.shape[1])
            if past_k is None and T % Q_BLOCK == 0 and T >= Q_BLOCK:
                nblk = T // Q_BLOCK
                qb = q.reshape(B, nblk, Q_BLOCK, DIFF_HEADS, 2, DIFF_HEAD_DIM).transpose(1, 0, 2, 3, 4, 5)
                pb = pos.reshape(nblk, Q_BLOCK)
                ob = lax.map(lambda a: diff_core(a[0], k_all, v_all, a[1], k_pos, lam), (qb, pb))
                o = ob.transpose(1, 0, 2, 3, 4).reshape(B, T, DIFF_HEADS, DIFF_V_DIM)
            else:
                o = diff_core(q, k_all, v_all, pos, k_pos, lam)
            o = rmsnorm(o, p['subln'][j]) * (1.0 - lam_init)
            mix = o.reshape(B, T, MIX_WIDTH)
        mem_out = memory_attention(z_mem.reshape(B, T, MEM_HEADS, MEM_HEAD_DIM), mem_k[l], mem_v[l]).reshape(B, T, MEM_WIDTH)
        x = x + jnp.concatenate([mix, mem_out], axis=-1) @ p['w_out'][l]
        h2 = rmsnorm(x, p['norm2'][l])
        x = x + jnp.square(jax.nn.relu(h2 @ p['w_mlp1'][l])) @ p['w_mlp2'][l]
    y = rmsnorm(x, p['final_norm'])
    return y, jnp.stack(pool_new, axis=0), k_new, v_new

def setup_inputs(seed: int = 0) -> dict:
    key = jax.random.key(seed)
    ks = jax.random.split(key, 32)
    f32 = jnp.float32
    n_pages = PAST_LEN // PAGE_SIZE
    n_used = DEC_BATCH * n_pages
    n_pool = n_used + n_used // 4
    page_table = jax.random.permutation(ks[0], n_pool)[:n_used].reshape(DEC_BATCH, n_pages).astype(jnp.int32)
    nrm = lambda k, s, sc: jax.random.normal(k, s, f32) * sc
    return {
        'x_prompt': nrm(ks[1], (BATCH, SEQ, D_MODEL), 1.0),
        'x_sample': nrm(ks[2], (DEC_BATCH, DEC_SEQ, D_MODEL), 1.0),
        'state_pool': nrm(ks[3], (N_A, DEC_BATCH, POOL_HIST, MIX_WIDTH), 1.0),
        'cache_mem_k': nrm(ks[4], (DEPTH, DEC_BATCH, MEM_TOKENS, MEM_HEADS, MEM_HEAD_DIM), 1.0),
        'cache_mem_v': nrm(ks[5], (DEPTH, DEC_BATCH, MEM_TOKENS, MEM_HEADS, MEM_HEAD_DIM), 1.0),
        'cache_k': nrm(ks[6], (n_pool, PAGE_SIZE, DIFF_HEADS, 2, DIFF_HEAD_DIM), 1.0),
        'cache_v': nrm(ks[7], (n_pool, PAGE_SIZE, DIFF_HEADS, DIFF_V_DIM), 1.0),
        'page_table': page_table,
        'mem_prompt': nrm(ks[8], (BATCH, MEM_TOKENS, D_MODEL), 1.0),
        'norm1': 1.0 + nrm(ks[9], (DEPTH, D_MODEL), 0.05),
        'norm2': 1.0 + nrm(ks[10], (DEPTH, D_MODEL), 0.05),
        'final_norm': 1.0 + nrm(ks[11], (D_MODEL,), 0.05),
        'kv_norm': 1.0 + nrm(ks[12], (D_MODEL,), 0.05),
        'mem_norm': 1.0 + nrm(ks[13], (D_MODEL,), 0.05),
        'w_in': nrm(ks[14], (DEPTH, D_MODEL, D_MODEL), D_MODEL ** -0.5),
        'w_out': nrm(ks[15], (DEPTH, D_MODEL, D_MODEL), D_MODEL ** -0.5),
        'w_mem_k': nrm(ks[16], (DEPTH, D_MODEL, MEM_WIDTH), D_MODEL ** -0.5),
        'w_mem_v': nrm(ks[17], (DEPTH, D_MODEL, MEM_WIDTH), D_MODEL ** -0.5),
        'w_pool': nrm(ks[18], (N_A, POOL_GROUPS, GROUP_WIDTH, GROUP_WIDTH), GROUP_WIDTH ** -0.5),
        'pool_scale': 1.0 + nrm(ks[19], (N_A, MIX_WIDTH), 0.1),
        'w_k': nrm(ks[20], (D_MODEL, MIX_WIDTH), D_MODEL ** -0.5),
        'w_v': nrm(ks[21], (D_MODEL, MIX_WIDTH), D_MODEL ** -0.5),
        'lambda_q1': nrm(ks[22], (N_B, DIFF_HEAD_DIM), 0.1),
        'lambda_k1': nrm(ks[23], (N_B, DIFF_HEAD_DIM), 0.1),
        'lambda_q2': nrm(ks[24], (N_B, DIFF_HEAD_DIM), 0.1),
        'lambda_k2': nrm(ks[25], (N_B, DIFF_HEAD_DIM), 0.1),
        'subln': 1.0 + nrm(ks[26], (N_B, DIFF_V_DIM), 0.05),
        'w_mlp1': nrm(ks[27], (DEPTH, D_MODEL, D_FF), D_MODEL ** -0.5),
        'w_mlp2': nrm(ks[28], (DEPTH, D_FF, D_MODEL), D_FF ** -0.5),
    }

def reference(x_prompt, x_sample, state_pool, cache_mem_k, cache_mem_v, cache_k, cache_v, page_table, mem_prompt,
              norm1, norm2, final_norm, kv_norm, mem_norm, w_in, w_out, w_mem_k, w_mem_v, w_pool, pool_scale,
              w_k, w_v, lambda_q1, lambda_k1, lambda_q2, lambda_k2, subln, w_mlp1, w_mlp2):
    p = dict(norm1=norm1, norm2=norm2, final_norm=final_norm, kv_norm=kv_norm, w_in=w_in, w_out=w_out,
             w_pool=w_pool, pool_scale=pool_scale, w_k=w_k, w_v=w_v, lambda_q1=lambda_q1, lambda_k1=lambda_k1,
             lambda_q2=lambda_q2, lambda_k2=lambda_k2, subln=subln, w_mlp1=w_mlp1, w_mlp2=w_mlp2)
    Bp, Tp, _ = x_prompt.shape
    Bs, Ts, _ = x_sample.shape
    hm = rmsnorm(mem_prompt, mem_norm)
    mem_k_prompt = jnp.einsum('bmd,lde->lbme', hm, w_mem_k).reshape(DEPTH, Bp, MEM_TOKENS, MEM_HEADS, MEM_HEAD_DIM)
    mem_v_prompt = jnp.einsum('bmd,lde->lbme', hm, w_mem_v).reshape(DEPTH, Bp, MEM_TOKENS, MEM_HEADS, MEM_HEAD_DIM)
    pos_p = jnp.arange(Tp, dtype=jnp.int32)
    y_prompt, pool_prompt, k_prompt, v_prompt = trunk(x_prompt, pos_p, None, mem_k_prompt, mem_v_prompt, None, None, p)
    n_pages = page_table.shape[1]
    past_k = cache_k[page_table].reshape(Bs, n_pages * PAGE_SIZE, DIFF_HEADS, 2, DIFF_HEAD_DIM)
    past_v = cache_v[page_table].reshape(Bs, n_pages * PAGE_SIZE, DIFF_HEADS, DIFF_V_DIM)
    pos_s = PAST_LEN + jnp.arange(Ts, dtype=jnp.int32)
    y_sample, pool_sample, k_sample, v_sample = trunk(x_sample, pos_s, state_pool, cache_mem_k, cache_mem_v, past_k, past_v, p)
    return (y_prompt, y_sample, pool_prompt, mem_k_prompt, mem_v_prompt, k_prompt, v_prompt, pool_sample, k_sample, v_sample)


_drawn_inputs = setup_inputs


def setup_inputs(seed=0):
    import zlib

    import numpy as np

    out = dict(_drawn_inputs(seed))
    spreads = {}
    factors = {'lambda_q1': 18.28,
     'lambda_k1': 64.0,
     'lambda_q2': 64.0,
     'lambda_k2': 64.0,
     'subln': 3.684}
    for name, (base, spread) in spreads.items():
        noise = np.random.default_rng([zlib.crc32(name.encode()), seed]).standard_normal(out[name].shape)
        drawn = base * np.exp(spread * noise) if base else spread * noise
        out[name] = __import__('jax').numpy.asarray(drawn.astype(out[name].dtype))
    for name, factor in factors.items():
        out[name] = (out[name] * factor).astype(out[name].dtype)
    return out
```

```python
import concourse.bass as bass
from concourse import mybir
from contextlib import ExitStack
import math
import numpy as np

D = 1024
P = 128
KT = D // P
PROMPT, REQS, STEPS = 512, 8, 4
SAMPLE = REQS * STEPS
TOK = PROMPT + SAMPLE
HALF = TOK // 2
PAST, PAGE = 256, 128
PAGES = PAST // PAGE
MEM, MEM_PAIRS, HD = 256, 2, 64
MIXT = 6
HIST = 15
WINDOWS = (2, 4, 8, 16)
EXT = 16 + PROMPT + REQS * (HIST + STEPS)
HEADS = 6
QT = PROMPT // P
SCALE = 64 ** -0.5
EPS = 1e-6
NEG = -1e30
CLAMP, BIG, BIG_END = 1.6e18, 2.0 ** -68, 2.0 ** -8
SUB = 2.0 ** -8
LAM_INIT = 0.8 - 0.6 * math.exp(-0.3)

U_MEM, U_IN0, U_POOL, U_OUT0, U_MLP0 = 0, 8, 16, 22, 30
U_IN1, U_K, U_V, U_OUT1, U_MLP1 = 94, 102, 108, 114, 122
N_UNITS = 186
BLOCKS = 4
RAW, HL, PS, TS = 4, 2, 2, 4
IN_ORDER = [6, 7, 0, 1, 2, 3, 4, 5]

R_MEM, R_IN0, R_MLP0, R_IN1, R_MLP1, R_FINAL = range(6)
G_MEM, G_IN0, G_MLP0, G_IN1, G_KV, G_MLP1, G_FINAL = range(7)

C_GAIN = 0
C_PSCALE = C_GAIN + 7 * KT
C_SUBLN = C_PSCALE + MIXT
C_LAM = C_SUBLN + 1
C_PARAM = C_LAM + 256
K_IDENT = 0
K_CAUSAL = K_IDENT + P
K_DMASK = K_CAUSAL + P
K_SEL = K_DMASK + 4 * SAMPLE
K_ROWJ = K_SEL + 48
K_INVW = K_ROWJ + 2
K_TAB = K_INVW + MIXT
K_CONST = K_TAB + MIXT * 16


def attention_items(layer):
    mem = [("mem", pr, i) for pr in range(MEM_PAIRS) for i in range(QT)]
    items = [("memdec", 0, 0)] + mem + [("memdec", 1, 0)]
    if layer == 1:
        for h in range(HEADS):
            items += [("diff", h, i) for i in range(QT)]
            if h < REQS // 2:
                items.append(("decode", h, 0))
    return items


ITEMS = attention_items(0) + attention_items(1)
L0_ITEMS = len(attention_items(0))


def build(nc, xT, memT, hist, params, consts, ropes, weights, memK, memV, cacheK, cacheV, pages,
          o_y, o_pool, o_memk, o_memv, o_k, o_v, o_pools, o_vs):
    F32, F32R, I32 = mybir.dt.float32, mybir.dt.float32r, mybir.dt.int32
    ALU, ACT, AX = mybir.AluOpType, mybir.ActivationFunctionType, mybir.AxisListType

    ctx = ExitStack()
    with ctx:
        base = nc.sbuf_base
        slab_bytes = 212 * 1000
        ctx.enter_context(nc.sbuf_tensor("slab", [P, slab_bytes // 4], F32))
        top = [(base + 31) // 32 * 32]
        end = base + slab_bytes

        def take(n_bytes):
            at = top[0]
            top[0] += (n_bytes + 31) // 32 * 32
            assert top[0] <= end, (top[0], end)
            return at

        def place(name, shape, dt, at):
            return nc.alloc_sbuf_tensor_at(name, shape, dt, offset=at)

        def new(name, shape, dt=F32):
            return place(name, shape, dt, take(4 * math.prod(shape[1:])))

        X = new("residual", [P, KT, TOK])
        a_at, b_at = take(8 * KT * TOK), take(8 * KT * TOK)
        A = place("operand_a", [P, 2, KT, TOK], F32R, a_at)
        B = place("operand_b", [P, 2, KT, TOK], F32R, b_at)
        Z = new("projected", [P, KT, TOK])
        raw = new("weights_raw", [P, RAW, D])
        split = new("weights_split", [P, HL, 2, D], F32R)
        T = new("staging", [P, TS, TOK])
        sq_at = take(12 * TOK)
        SQ = place("squares", [P, 2, TOK], F32, sq_at)
        sq_sum = place("squares_sum", [P, TOK], F32, sq_at + 8 * TOK)
        rms = new("inv_rms", [P, TOK])
        rms_mem = new("inv_rms_mem", [P, MEM])
        kv_at = take(2 * 12288)
        k_at = take(4 * HEADS * TOK)
        memKT = new("mem_keys", [P, 2, MEM_PAIRS, MEM])
        memVt = new("mem_values", [P, 2, 2, MEM])
        QbdM = new("mem_query_blocks", [P, REQS, MEM_PAIRS, 32])
        par = new("params", [P, C_PARAM])
        con = new("constants", [P, K_CONST])
        tiny = new("tiny", [P, 160])
        C2 = new("combine", [P, 2, 48])
        pg = new("page_table", [1, 16], I32)
        ones = new("ones", [P, P])
        Kt = place("keys", [P, HEADS, TOK], F32, k_at)
        line = place("pool_line", [P, 2, EXT], F32, k_at)
        window = place("pool_window", [P, 2, EXT], F32, k_at + 8 * EXT)
        kv = place("cache_tiles", [P, 2, 2, 2 * 768], F32, kv_at)
        swap = place("rotated", [P, MIXT, TOK], F32, kv_at)
        rope = place("cos_sin", [P, 2, TOK], F32, kv_at + 4 * MIXT * TOK)
        partial = place("window_partial", [P, 2, EXT], F32, sq_at)
        memX = place("mem_residual", [P, KT, MEM], F32, kv_at)
        histb = new("pool_history", [P, MIXT, REQS, HIST])
        Vt = place("values", [P, QT, 768], F32, a_at)
        Vn = place("values_new", [SAMPLE, 768], F32, a_at + 4 * KT * TOK)
        O = place("attention_out", [P, 24, P], F32, b_at)
        Qbd = place("query_blocks", [P, HEADS, REQS, 64], F32, b_at + 16384)
        Pr = [[place(f"probs_l{l}_{s}", [P, 2, 512], F32, b_at + at) for s, at in enumerate(ats)]
              for l, ats in enumerate([(0, 4 * KT * TOK), (12288, 28672)])]
        PT = [T[:, s, 0:512] for s in range(2)]

        ps = ctx.enter_context(nc.psum_tensor("psum", [P, 8, 512], F32))

        ident = con[:, K_IDENT:K_IDENT + P]
        causal = con[:, K_CAUSAL:K_CAUSAL + P]

        def gain(g, k):
            return par[:, C_GAIN + g * KT + k:C_GAIN + g * KT + k + 1]

        epsc, lam_n, gsub, sgn = tiny[:, 0:1], tiny[:, 1:2], tiny[:, 2:3], tiny[:, 3:4]
        lamw = tiny[:, 4:12]
        mx = tiny[:, 16:20].rearrange("p (s j) -> p s j", s=2)
        nb = tiny[:, 20:24].rearrange("p (s j) -> p s j", s=2)
        sums = tiny[:, 24:28].rearrange("p (s j) -> p s j", s=2)
        coef = tiny[:, 28:32].rearrange("p (s j) -> p s j", s=2)
        ss = tiny[:, 32:56]
        rr = tiny[:, 56:80]
        rr2 = tiny[:, 80:104]
        ss_big, keep = tiny[:, 104:128], tiny[:, 128:152]
        eps_sub = tiny[:, 12:13]
        NS = MIXT * SAMPLE
        small = [T[:, 2 + i // 2, (i % 2) * NS:(i % 2) * NS + NS] for i in range(4)]

        def sem(name):
            return ctx.enter_context(nc.semaphore(name))

        raw_loaded = [sem(f"raw_loaded{i}") for i in range(RAW)]
        weight_hi, weight_lo = sem("weight_hi"), sem("weight_lo")
        unit_done, unit_out = sem("unit_done"), sem("unit_out")
        x_loaded, memx_loaded = sem("x_loaded"), sem("memx_loaded")
        par_loaded, con_loaded = sem("par_loaded"), sem("con_loaded")
        hist_loaded, rope_loaded, pg_loaded = sem("hist_loaded"), sem("rope_loaded"), sem("pg_loaded")
        sq_ready, sq_summed = sem("sq_ready"), sem("sq_summed")
        norm_hi, norm_lo = sem("norm_hi"), sem("norm_lo")
        norm_mm, root_ready, rms_ready = sem("norm_mm"), sem("root_ready"), sem("rms_ready")
        hid_hi, hid_lo = sem("hid_hi"), sem("hid_lo")
        mix_hi, mix_lo = sem("mix_hi"), sem("mix_lo")
        cat_hi, cat_lo = sem("cat_hi"), sem("cat_lo")
        memv_turned, memv_ready = sem("memv_turned"), sem("memv_ready")
        v_turned, v_ready = sem("v_turned"), sem("v_ready")
        line_ready, window_ready, pooled = sem("line_ready"), sem("window_ready"), sem("pooled")
        kv_loaded = [sem(f"kv_loaded{i}") for i in range(2)]
        qbdm_ready, qbd_ready = sem("qbdm_ready"), sem("qbd_ready")
        q_swapped, k_swapped = sem("q_swapped"), sem("k_swapped")
        q_roped, k_roped = sem("q_roped"), sem("k_roped")
        scored, biased, exped = sem("scored"), sem("biased"), sem("exped")
        weighted, turned, copied = sem("weighted"), sem("turned"), sem("copied")
        mixed, drained = sem("mixed"), sem("drained")
        squared = sem("squared")
        sub_mean = sem("sub_mean")
        sub_root, sub_rms, sub_mm = sem("sub_root"), sem("sub_rms"), sem("sub_mm")
        sub_sample = sem("sub_sample")
        sub_scaled, sub_turned = sem("sub_scaled"), sem("sub_turned")
        const_ready = sem("const_ready")
        lam_dot, lam_exp = sem("lam_dot"), sem("lam_exp")
        y_ready = sem("y_ready")
        stored = sem("stored")
        hid_sq = sem("hid_sq")
        v_stored, k_stored = sem("v_stored"), sem("k_stored")
        memk_stored, memv_stored = sem("memk_stored"), sem("memv_stored")
        pool_stored, pools_stored = sem("pool_stored"), sem("pools_stored")
        act_order, dve_order, pool_order = sem("act_order"), sem("dve_order"), sem("pool_order")
        lo_of = lambda k: slice(k * P, (k + 1) * P)

        class Order:

            def __init__(self, eng, s):
                self.eng, self.sem, self.n = eng, s, 0

            def step(self, ins):
                self.n += 1
                ins.then_inc(self.sem, 1)

            def settle(self):
                self.eng.wait_ge(self.sem, self.n)

            def chain(self, ins):
                self.step(ins)
                self.settle()

        def halves(ap):
            return ap.rearrange("p (a b) -> p a b", a=2)

        def unit_psum(j):
            return ps[:, 2 * (j % PS):2 * (j % PS) + 2, 0:HALF]

        chunks = ([("mem", 0, c) for c in range(4)] + [("mem", 1, c) for c in range(4)]
                  + [("page", 0, b) for b in range(REQS)])

        def kv_ready(eng, n):
            done = 32 * (n // 2 + 1) if n < 8 else 32 * 4 + 64 * ((n - 8) // 2 + 1)
            eng.wait_ge(kv_loaded[n % 2], done)

        def chunk_of(n):
            kind, a, _ = ITEMS[n]
            l = int(n >= L0_ITEMS)
            return 4 * l + 2 * a if kind == "memdec" else 8 + 2 * a

        DEC = [n for n, it in enumerate(ITEMS) if it[0] in ("memdec", "decode")]

        block = ctx.enter_context(nc.Block())

        @block.sync
        def _(sp):
            def load(u, first):
                s = u % RAW if isinstance(u, int) else None
                if not first:
                    sp.wait_ge(weight_lo, u - RAW + 1)
                sp.dma_start(raw[:, s, :], weights[u]).then_inc(raw_loaded[s], 16)

            def load_units(a, b):
                while a < b and (a % RAW or a < RAW):
                    load(a, a < RAW)
                    a += 1
                turns = (b - a) // RAW
                if turns > 1:
                    with sp.Fori(0, turns) as t:
                        for s in range(RAW):
                            u = t * RAW + (a + s)
                            sp.wait_ge(weight_lo, u - RAW + 1)
                            sp.dma_start(raw[:, s, :], weights[u]).then_inc(raw_loaded[s], 16)
                    a += turns * RAW
                while a < b:
                    load(a, False)
                    a += 1

            def load_chunks(n):
                at = DEC.index(n)
                if at >= 1:
                    sp.wait_ge(mixed, DEC[at - 1] + 1)
                if n == DEC[2]:
                    sp.wait_ge(k_roped, 1)
                    sp.wait_ge(q_roped, 1)
                c0 = chunk_of(n)
                for c in (c0, c0 + 1):
                    s = c % 2
                    kind, l, i = chunks[c]
                    if kind == "mem":
                        sp.dma_start(kv[:, s, 0, 0:1024], memK[l, i]).then_inc(kv_loaded[s], 16)
                        sp.dma_start(kv[:, s, 1, 0:1024], memV[l, i]).then_inc(kv_loaded[s], 16)
                    else:
                        for g in range(PAGES):
                            page = sp.value_load(pg[0:1, PAGES * i + g:PAGES * i + g + 1], min_val=0,
                                                 max_val=cacheK.shape[0] - 1)
                            sp.dma_start(kv[:, s, 0, g * 768:(g + 1) * 768], cacheK[page]).then_inc(kv_loaded[s], 16)
                            sp.dma_start(kv[:, s, 1, g * 768:(g + 1) * 768], cacheV[page]).then_inc(kv_loaded[s], 16)

            sp.dma_start(memX[:, :, :], memT).then_inc(memx_loaded, 16)
            sp.dma_start(par[:, :], params).then_inc(par_loaded, 16)
            load_units(0, 2)
            sp.dma_start(X[:, :, :], xT).then_inc(x_loaded, 16)
            load_units(2, 4)
            sp.dma_start(con[:, :], consts).then_inc(con_loaded, 16)
            sp.dma_start(pg[:, :], pages).then_inc(pg_loaded, 16)
            load_units(4, 12)
            sp.dma_start(histb[:, :, :, :], hist).then_inc(hist_loaded, 16)
            sp.wait_ge(norm_lo, KT)
            sp.wait_ge(sq_ready, KT)
            load_chunks(DEC[0])
            load_units(12, 20)
            load_chunks(DEC[1])
            load_units(20, U_IN1)
            sp.wait_ge(mixed, DEC[1] + 1)
            sp.dma_start(rope[:, :, :], ropes).then_inc(rope_loaded, 16)
            load_units(U_IN1, U_OUT1 + HL)
            sp.wait_ge(pg_loaded, 16)
            load_chunks(DEC[2])
            load_chunks(DEC[3])
            for n in DEC[4:]:
                load_chunks(n)
            load_units(U_OUT1 + HL, N_UNITS)
            for k in range(KT):
                sp.wait_ge(y_ready, k + 1)
                sp.dma_start(o_y[:, k, :], Z[:, k, :]).then_inc(stored, 16)
            sp.wait_ge(stored, 16 * KT)

        @block.tensor
        def _(pe):
            def unit(u, j, act, kts=tuple(range(KT)), cols=TOK, ready=None, base_kt=0, first=False):
                pe.wait_ge(weight_lo, u + 1)
                if not first:
                    pe.wait_ge(unit_out, u - PS + 1)
                n = cols // 2 if cols == TOK else cols
                for q, k in enumerate(kts):
                    if ready:
                        ready(k)
                    w = lambda r: split[:, j % HL, r, lo_of(k - base_kt)]
                    for wr, ar in ((0, 0), (0, 1), (1, 0)):
                        for hf in range(cols // n):
                            mm = pe.matmul(ps[:, 2 * (j % PS) + hf, 0:n], w(wr), act[:, ar, k, hf * n:(hf + 1) * n],
                                           start=(q == 0 and wr == 0 and ar == 0),
                                           stop=(q == len(kts) - 1 and wr == 1))
                mm.then_inc(unit_done, 1)

            def norm_sum(r, cols=TOK):
                pe.wait_ge(sq_summed, (KT - 1) * (r + 1))
                n = cols // 2 if cols == TOK else cols
                for hf in range(cols // n):
                    mm = pe.matmul(ps[:, 6 + hf, 0:n], ones[:, :], sq_sum[:, hf * n:(hf + 1) * n],
                                   start=True, stop=True)
                mm.then_inc(norm_mm, 1)

            def normed(g):
                return lambda k: pe.wait_ge(norm_lo, KT * g + k + 1)

            def project(u0, act, g, r=None):
                for j in range(KT):
                    unit(u0 + j, u0 + j, act, ready=normed(g) if j == 0 else None)
                    if j == 0 and r is not None:
                        norm_sum(r)

            def mlp(u0, h2, hidden, g, r, done):
                def block_(i, u, first):
                    for j in range(KT):
                        unit(u + j, u0 + j, h2, ready=normed(g) if first and j == 0 else None)
                        if first and j == 0:
                            norm_sum(r)
                    for j in range(KT):
                        ready = (lambda k: pe.wait_ge(hid_lo, i * KT + (done + k + 1))) if j == 0 else None
                        unit(u + (KT + j), u0 + j, hidden, ready=ready)

                block_(0, u0, True)
                with pe.Fori(1, BLOCKS) as i:
                    block_(i, i * (2 * KT) + u0, False)

            def banks(n):
                return 2 * (n % 2), 4 + n % 2, 6 + n % 2

            def scores(n):
                kind, a, i = ITEMS[n]
                l = int(n >= L0_ITEMS)
                s0, _, _ = banks(n)
                if n >= 2:
                    pe.wait_ge(exped, n - 1)
                if kind == "mem":
                    for hh in range(2):
                        lane = slice(64 * hh, 64 * hh + 64)
                        mm = pe.matmul(ps[:, s0 + hh, 0:MEM], Z[lane, 6 + a, i * P:(i + 1) * P],
                                       memKT[lane, l, a, :], start=True, stop=True)
                elif kind == "memdec":
                    pe.wait_ge(qbdm_ready, l + 1)
                    for b in range(4):
                        c = chunk_of(n) + b // 2
                        kv_ready(pe, c)
                        for pr in range(MEM_PAIRS):
                            at = (b % 2) * 512 + pr * MEM
                            mm = pe.matmul(ps[32 * b:32 * b + 32, s0, 0:MEM], QbdM[:, 4 * a + b, pr, :],
                                           kv[:, c % 2, 0, at:at + MEM], start=(pr == 0), stop=(pr == 1))
                elif kind == "diff":
                    for j in range(2):
                        lane = slice(64 * j, 64 * j + 64)
                        mm = pe.matmul(ps[:, s0 + j, 0:(i + 1) * P], Z[lane, a, i * P:(i + 1) * P],
                                       Kt[lane, a, 0:(i + 1) * P], start=True, stop=True)
                else:
                    pe.wait_ge(qbd_ready, 1)
                    for o in range(2):
                        c = chunk_of(n) + o
                        kv_ready(pe, c)
                        keys = kv[:, c % 2, 0, :].rearrange("p (g h k) -> p h g k", g=PAGES, h=HEADS)
                        for h in range(HEADS):
                            pe.matmul(ps[64 * o:64 * o + 64, s0, 0:PAST].rearrange("p (g k) -> p g k", g=PAGES),
                                      Qbd[:, h, 2 * a + o, :], keys[:, h, :, :], start=(h == 0), stop=(h == 5))
                    for h in range(HEADS):
                        mm = pe.matmul(ps[:, s0, PAST:PAST + SAMPLE], Qbd[:, h, 2 * a:2 * a + 2, :],
                                       Kt[:, h, PROMPT:TOK], start=(h == 0), stop=(h == 5))
                mm.then_inc(scored, 1)

            def turn(n):
                kind, a, i = ITEMS[n]
                l = int(n >= L0_ITEMS)
                _, t0, _ = banks(n)
                pr = Pr[l][n % 2]
                pe.wait_ge(weighted, n + 1)
                if n >= 2:
                    pe.wait_ge(copied, n - 1)
                if kind == "mem":
                    for kt in range(2):
                        for hh in range(2):
                            at = (2 * kt + hh) * P
                            mm = pe.transpose(ps[:, t0, at:at + P], pr[:, hh, lo_of(kt)], ident)
                elif kind == "memdec":
                    for kt in range(2):
                        mm = pe.transpose(ps[:, t0, lo_of(kt)], pr[:, 0, lo_of(kt)], ident)
                elif kind == "diff":
                    for kt in range(i + 1):
                        mm = pe.transpose(ps[:, t0, lo_of(kt)], pr[:, 0, lo_of(kt)], ident)
                else:
                    for kt in range(2):
                        pe.matmul(ps[:, t0, 48 * kt:48 * kt + 48], pr[:, 0, lo_of(kt)], C2[:, n % 2, :],
                                  start=True, stop=True)
                    mm = pe.matmul(ps[0:SAMPLE, t0, 96:144], pr[:, 0, PAST:PAST + SAMPLE], C2[:, n % 2, :],
                                   start=True, stop=True)
                mm.then_inc(turned, 1)

            def mix(n):
                kind, a, i = ITEMS[n]
                l = int(n >= L0_ITEMS)
                _, _, m0 = banks(n)
                pt = PT[n % 2]
                pe.wait_ge(copied, n + 1)
                if n >= 2:
                    pe.wait_ge(drained, n - 1)
                if kind == "mem":
                    for hh in range(2):
                        for kt in range(2):
                            mm = pe.matmul(ps[64 * hh:64 * hh + 64, m0, 0:P],
                                           memVt[:, l, kt, a * P + 64 * hh:a * P + 64 * hh + 64],
                                           pt[:, (2 * kt + hh) * P:(2 * kt + hh + 1) * P],
                                           start=(kt == 0), stop=(kt == 1))
                elif kind == "memdec":
                    for b in range(4):
                        c = chunk_of(n) + b // 2
                        for pr in range(MEM_PAIRS):
                            for kt in range(2):
                                at = (b % 2) * 512 + kt * MEM + pr * P
                                out = (pr * 4 + b) * 8
                                mm = pe.matmul(ps[:, m0, out:out + 8], kv[:, c % 2, 1, at:at + P],
                                               pt[:, kt * P + 32 * b + 8 * pr:kt * P + 32 * b + 8 * pr + 8],
                                               start=(kt == 0), stop=(kt == 1))
                elif kind == "diff":
                    for kt in range(i + 1):
                        mm = pe.matmul(ps[:, m0, 0:P], pt[:, lo_of(kt)], Vt[:, kt, a * P:(a + 1) * P],
                                       start=(kt == 0), stop=(kt == i))
                else:
                    for o in range(2):
                        c = chunk_of(n) + o
                        for h in range(HEADS):
                            out = (h * 2 + o) * 4
                            at = o * 24 + h * 4
                            for kt in range(2):
                                pe.matmul(ps[:, m0, out:out + 4], kv[:, c % 2, 1, kt * 768 + h * P:kt * 768 + (h + 1) * P],
                                          pt[:, 48 * kt + at:48 * kt + at + 4], start=(kt == 0), stop=False)
                            mm = pe.matmul(ps[:, m0, out:out + 4], Vn[:, h * P:(h + 1) * P],
                                           pt[0:SAMPLE, 96 + at:96 + at + 4], start=False, stop=True)
                mm.then_inc(mixed, 1)

            def attention(n0, n1):
                scores(n0)
                for n in range(n0, n1):
                    if n + 1 < n1:
                        scores(n + 1)
                    turn(n)
                    if n > n0:
                        mix(n - 1)
                mix(n1 - 1)

            def cat_ready(k):
                if k >= 6:
                    pe.wait_ge(cat_lo, 1)
                else:
                    pe.wait_ge(unit_out, U_POOL + k + 1)

            pe.wait_ge(const_ready, 1)
            for u in range(8):
                unit(u, u, A, cols=MEM, ready=normed(G_MEM) if u == 0 else None, first=u < PS)
                if u == 0:
                    norm_sum(R_MEM, MEM)
            pe.wait_ge(con_loaded, 16)
            for j in range(KT):
                unit(U_IN0 + j, j, B, ready=normed(G_IN0) if j == 0 else None)
                if j == 0:
                    pe.wait_ge(root_ready, 1)
                    norm_sum(R_IN0)
                if j == 1:
                    pe.wait_ge(root_ready, 2)
                    for m in range(4):
                        for kt in range(2):
                            mm = pe.transpose(ps[:, 6 + m // 2, (kt * 2 + m % 2) * P:(kt * 2 + m % 2 + 1) * P],
                                              T[:, m, lo_of(kt)], ident)
                    mm.then_inc(memv_turned, 1)
            pe.wait_ge(unit_out, U_POOL)
            pe.wait_ge(memv_ready, 2)
            attention(0, L0_ITEMS)
            pe.wait_ge(drained, L0_ITEMS)
            for j in range(MIXT):
                pair, o = j // 3, j % 3
                kts = [3 * pair + k for k in ((0, 1), (0, 1, 2), (1, 2))[o]]
                pe.wait_ge(mix_lo, 3 * pair + 3)
                unit(U_POOL + j, j, A, kts=kts, base_kt=3 * pair)
            for j in range(KT):
                unit(U_OUT0 + j, j, B, kts=(6, 7, 0, 1, 2, 3, 4, 5), ready=cat_ready if j == 0 else None)
            mlp(U_MLP0, A, B, G_MLP0, R_MLP0, 0)
            project(U_IN1, A, G_IN1, R_IN1)
            for j in range(MIXT):
                unit(U_K + j, j, B, ready=normed(G_KV) if j == 0 else None)
            for j in range(MIXT + 1):
                if j < MIXT:
                    unit(U_V + j, j, B)
                if j >= 1:
                    h = j - 1
                    pe.wait_ge(unit_out, U_V + h + 1)
                    if h == 0:
                        pe.wait_ge(root_ready, R_IN1 + 1)
                    if h >= 2:
                        pe.wait_ge(v_ready, h - 1)
                    for t in range(QT):
                        pe.transpose(ps[:, 4 + 2 * (h % 2), lo_of(t)], T[:, h % TS, lo_of(t)], ident)
                    pe.transpose(ps[0:SAMPLE, 5 + 2 * (h % 2), 0:P], T[:, h % TS, PROMPT:TOK], ident)\
                        .then_inc(v_turned, 1)
            pe.wait_ge(unit_out, U_OUT1)
            pe.wait_ge(v_ready, MIXT)
            pe.wait_ge(q_roped, 1)
            pe.wait_ge(k_roped, 1)
            attention(L0_ITEMS, len(ITEMS))
            pe.wait_ge(drained, len(ITEMS))
            pe.wait_ge(squared, QT * HEADS + 1)
            pe.matmul(ps[:, 6, 0:NS], ones[:, :], SQ[:, 0, 0:NS], start=True, stop=True)
            pe.matmul(ps[:, 7, 0:NS], ones[:, :], SQ[:, 1, 0:NS], start=True, stop=True).then_inc(sub_mm, 1)
            for h in range(HEADS):
                pe.wait_ge(sub_scaled, h + 1)
                for i in range(QT):
                    mm = pe.transpose(ps[:, h, lo_of(i)], O[:, QT * h + i, :], ident)
                mm.then_inc(sub_turned, 1)
            pe.wait_ge(cat_lo, 2)
            pe.wait_ge(mix_lo, MIXT + 7)
            for j in range(KT):
                unit(U_OUT1 + j, j, A)
            mlp(U_MLP1, B, A, G_MLP1, R_MLP1, BLOCKS * KT)
            norm_sum(R_FINAL)

        @block.scalar
        def _(act):
            own = Order(act, act_order)

            def weight_high(u, s, turn_value, first=False):
                act.wait_ge(raw_loaded[s], turn_value)
                if not first:
                    act.wait_ge(unit_done, u - HL + 1)
                act.activation(split[:, s % HL, 0, :], raw[:, s, :], ACT.Copy).then_inc(weight_hi, 1)

            def high(u):
                if u < N_UNITS:
                    weight_high(u, u % RAW, 16 * (u // RAW + 1), u < HL)

            def norm_high(g, k, src, dst):
                act.activation(dst, src, ACT.Copy, scale=gain(g, k)).then_inc(norm_hi, 1)

            def square(r, k, src, cols):
                if k >= 2 or r:
                    act.wait_ge(sq_summed, (KT - 1) * r + (max(k - 2, 1) if k >= 2 else 0))
                act.activation(SQ[:, k % 2, 0:cols], src, ACT.Square).then_inc(sq_ready, 1)

            def root(r, cols=TOK):
                act.wait_ge(norm_mm, r + 1)
                if r == R_MEM:
                    act.activation(rms_mem[:, :], ps[:, 6, 0:MEM], ACT.Sqrt, bias=epsc, scale=1.0 / D)\
                        .then_inc(root_ready, 1)
                else:
                    act.activation(halves(rms[:, :]), ps[:, 6:8, 0:HALF], ACT.Sqrt, bias=epsc, scale=1.0 / D)\
                        .then_inc(root_ready, 1)

            def residual_tile(u, o, r, gs):
                act.wait_ge(unit_out, u + 1)
                for g, dst in gs:
                    norm_high(g, o, X[:, o, :], dst[:, 0, o, :])
                square(r, o, X[:, o, :], TOK)

            def mlp(u0, hidden, r, nr, gs):
                def turn(i, j):
                    return i * 64 + 16 * ((u0 + j + HL) // RAW + 1)

                for j in range(KT):
                    weight_high(u0 + j + HL, (u0 + j + HL) % RAW, turn(0, j))
                    if j == 0:
                        root(r)
                    act.wait_ge(unit_out, u0 + j + 1)
                    act.activation(hidden[:, 0, j, :], T[:, j % TS, :], ACT.Square).then_inc(hid_hi, 1)
                with act.Fori(0, BLOCKS - 1) as i:
                    u = i * (2 * KT) + u0
                    for j in range(KT, 2 * KT):
                        weight_high(u + (j + HL), (u0 + j + HL) % RAW, turn(i, j))
                    for j in range(KT):
                        act.wait_ge(unit_out, u + (2 * KT + j + 1))
                        act.activation(hidden[:, 0, j, :], T[:, j % TS, :], ACT.Square).then_inc(hid_hi, 1)
                        weight_high(u + (2 * KT + j + HL), (u0 + j + HL) % RAW, turn(i, 2 * KT + j))
                u = u0 + (BLOCKS - 1) * 2 * KT
                for j in range(KT):
                    residual_tile(u + KT + j, j, nr, gs)
                    high(u + KT + j + HL)

            def items_exp(n):
                kind, a, i = ITEMS[n]
                l = int(n >= L0_ITEMS)
                act.wait_ge(biased, n + 1)
                if n >= 2:
                    act.wait_ge(turned, n - 1)
                s0, pr, s = 2 * (n % 2), Pr[l][n % 2], n % 2
                n_keys = {"mem": MEM, "memdec": MEM, "diff": (i + 1) * P, "decode": PAST + SAMPLE}[kind]
                for j in range(1 if kind in ("memdec", "decode") else 2):
                    ins = act.activation(pr[:, j, 0:n_keys], ps[:, s0 + j, 0:n_keys], ACT.Exp,
                                         bias=nb[:, s, j:j + 1], scale=SCALE, accum_out=sums[:, s, j:j + 1])
                ins.then_inc(exped, 1)

            def items_copy(n):
                kind, a, i = ITEMS[n]
                act.wait_ge(turned, n + 1)
                if n >= 2:
                    act.wait_ge(mixed, n - 1)
                t0 = 4 + n % 2
                cols = {"mem": 512, "memdec": 256, "diff": (i + 1) * P, "decode": 96}[kind]
                if kind == "decode":
                    own.step(act.activation(PT[n % 2][0:SAMPLE, 96:144], ps[0:SAMPLE, t0, 96:144], ACT.Copy))
                act.activation(PT[n % 2][:, 0:cols], ps[:, t0, 0:cols], ACT.Copy).then_inc(copied, 1)

            def items_square(n):
                kind, a, i = ITEMS[n]
                if kind == "diff":
                    act.wait_ge(drained, n + 1)
                    k = QT * a + i
                    if k:
                        act.wait_ge(squared, k)
                    own.step(act.activation(SQ[:, 1, 0:P], SQ[:, 0, k % 2 * P:k % 2 * P + P], ACT.Square,
                                            accum_out=ss[:, k:k + 1]))
                    act.activation(SQ[:, 1, P:2 * P], O[:, k, :], ACT.Square, scale=BIG,
                                   accum_out=ss_big[:, k:k + 1]).then_inc(squared, 1)

            def attention(n0, n1):
                for n in range(n0, n1 + 2):
                    if n < n1:
                        items_exp(n)
                    if n0 <= n - 1 < n1:
                        items_copy(n - 1)
                    if n0 <= n - 2 < n1:
                        items_square(n - 2)

            act.wait_ge(const_ready, 1)
            act.wait_ge(memx_loaded, 16)
            act.wait_ge(par_loaded, 16)
            high(0)
            for k in range(KT):
                norm_high(G_MEM, k, memX[:, k, :], A[:, 0, k, 0:MEM])
                square(R_MEM, k, memX[:, k, :], MEM)
            high(1)
            act.wait_ge(x_loaded, 16)
            for k in range(KT):
                norm_high(G_IN0, k, X[:, k, :], B[:, 0, k, :])
                if k == 1:
                    root(R_MEM)
                square(R_IN0, k, X[:, k, :], TOK)
            for u in range(8):
                high(u + HL)
            act.wait_ge(lam_dot, 1)
            act.activation(lamw[:, 2:4], lamw[:, 0:2], ACT.Exp).then_inc(lam_exp, 1)
            for j in range(KT):
                high(U_IN0 + j + HL)
                if j == 0:
                    root(R_IN0)
                if j == 1:
                    act.wait_ge(memv_turned, 1)
                    for l in range(2):
                        act.activation(memVt[:, l, :, :], ps[:, 6 + l, :].rearrange("p (k f) -> p k f", k=2), ACT.Copy)\
                           .then_inc(memv_ready, 1)
            for n in range(0, L0_ITEMS + 2):
                if n < L0_ITEMS:
                    items_exp(n)
                if 0 <= n - 1 < L0_ITEMS:
                    items_copy(n - 1)
                if n < MIXT:
                    o = n
                    if o == 0:
                        act.wait_ge(hist_loaded, 16)
                    if o >= 2:
                        act.wait_ge(pooled, o - 1)
                    ln = line[:, o % 2, :]
                    reqs = ln[:, 16 + PROMPT:EXT].rearrange("p (b t) -> p b t", b=REQS)
                    act.activation(ln[:, 16:16 + PROMPT], Z[:, o, 0:PROMPT], ACT.Copy).then_inc(line_ready, 1)
                    act.activation(reqs[:, :, 0:HIST], histb[:, o, :, :], ACT.Copy).then_inc(line_ready, 1)
                    act.activation(reqs[:, :, HIST:HIST + STEPS],
                                   Z[:, o, PROMPT:TOK].rearrange("p (b t) -> p b t", b=REQS), ACT.Copy)\
                       .then_inc(line_ready, 1)
                if 3 <= n < MIXT + 3:
                    o = n - 3
                    act.wait_ge(pooled, o + 1)
                    act.activation(A[:, 0, o, :], T[:, 2 + o % 2, :], ACT.Copy).then_inc(mix_hi, 1)
            act.wait_ge(drained, L0_ITEMS)
            act.activation(B[:, 0, 6:8, :], Z[:, 6:8, :], ACT.Copy).then_inc(cat_hi, 1)
            for j in range(MIXT):
                act.wait_ge(unit_done, U_POOL + j + 1)
                act.activation(halves(B[:, 0, j, :]), unit_psum(j), ACT.Copy,
                               scale=par[:, C_PSCALE + j:C_PSCALE + j + 1]).then_inc(mix_hi, 1)
                high(U_POOL + j + HL)
            for j in range(KT):
                residual_tile(U_OUT0 + j, j, R_MLP0, [(G_MLP0, A)])
                high(U_OUT0 + j + HL)
            mlp(U_MLP0, B, R_MLP0, R_IN1, [(G_IN1, A)])
            act.wait_ge(unit_done, U_IN1)
            for k in range(KT):
                norm_high(G_KV, k, X[:, k, :], B[:, 0, k, :])
            for j in range(KT):
                high(U_IN1 + j + HL)
                if j == 0:
                    root(R_IN1)
            for j in range(MIXT):
                high(U_K + j + HL)
            for j in range(MIXT + 1):
                if j < MIXT:
                    high(U_V + j + HL)
                if j >= 1:
                    h = j - 1
                    act.wait_ge(v_turned, h + 1)
                    own.step(act.activation(Vt[:, :, h * P:(h + 1) * P],
                                            ps[:, 4 + 2 * (h % 2), :].rearrange("p (t e) -> p t e", t=QT), ACT.Copy))
                    act.activation(Vn[:, h * P:(h + 1) * P], ps[0:SAMPLE, 5 + 2 * (h % 2), 0:P], ACT.Copy)\
                       .then_inc(v_ready, 1)
            attention(L0_ITEMS, len(ITEMS))
            act.wait_ge(sub_mean, 1)
            act.wait_ge(squared, QT * HEADS)
            own.step(act.activation(SQ[:, 0, 0:NS], small[0], ACT.Square))
            act.activation(SQ[:, 1, 0:NS].rearrange("p (h t) -> p h t", h=MIXT), Z[:, 0:MIXT, PROMPT:TOK], ACT.Square,
                           scale=BIG).then_inc(squared, 1)
            act.wait_ge(v_stored, 32)
            act.activation(A[:, 0, 6:8, :], Z[:, 6:8, :], ACT.Copy).then_inc(cat_hi, 1)
            act.wait_ge(sub_mean, 2)
            act.activation(rr[:, :], ss[:, :], ACT.Sqrt, bias=eps_sub, scale=SUB).then_inc(sub_root, 1)
            act.wait_ge(sub_mean, 3)
            act.activation(small[0], small[1], ACT.Sqrt, bias=eps_sub, scale=SUB).then_inc(sub_root, 1)
            for h in range(HEADS):
                act.wait_ge(sub_turned, h + 1)
                act.activation(A[:, 0, h, 0:PROMPT], ps[:, h, :], ACT.Copy, scale=gsub).then_inc(mix_hi, 1)
            act.wait_ge(sub_sample, 1)
            act.activation(A[:, 0, 0:MIXT, PROMPT:TOK], Z[:, 0:MIXT, PROMPT:TOK], ACT.Copy, scale=gsub)\
               .then_inc(mix_hi, 1)
            for j in range(KT):
                residual_tile(U_OUT1 + j, j, R_MLP1, [(G_MLP1, B)])
                high(U_OUT1 + j + HL)
            mlp(U_MLP1, A, R_MLP1, R_FINAL, [])
            root(R_FINAL)

        @block.vector
        def _(dve):
            own = Order(dve, dve_order)

            def weight_rest(u, s, first=False):
                dve.wait_ge(weight_hi, u + 1)
                dve.tensor_tensor(split[:, s % HL, 1, :], raw[:, s, :], split[:, s % HL, 0, :].bitcast(F32),
                                  ALU.subtract).then_inc(weight_lo, 1)

            def rest(u):
                if u < N_UNITS:
                    weight_rest(u, u % RAW)

            def norm_rest(g, k, src, dst):
                dve.wait_ge(norm_hi, KT * g + k + 1)
                dve.scalar_tensor_tensor(out=dst[1], in0=src, scalar=gain(g, k), in1=dst[0].bitcast(F32),
                                         op0=ALU.mult, op1=ALU.subtract).then_inc(norm_lo, 1)

            def pair_of(op, k, cols=TOK):
                return op[:, 0, k, 0:cols], op[:, 1, k, 0:cols]

            def inverse(r):
                dve.wait_ge(root_ready, r + 1)
                t = rms_mem[:, :] if r == R_MEM else rms[:, :]
                dve.reciprocal(t, t).then_inc(rms_ready, 1)

            def add_residual(u, j, o):
                dve.wait_ge(unit_done, u + 1)
                dve.tensor_tensor(halves(X[:, o, :]), unit_psum(j), halves(X[:, o, :]), ALU.add).then_inc(unit_out, 1)

            def out_units(u0, g, dst):
                for j in range(KT):
                    add_residual(u0 + j, u0 + j, j)
                    norm_rest(g, j, X[:, j, :], pair_of(dst, j))
                    rest(u0 + j + HL)

            def mlp(u0, r, g, dst):
                def hidden(u, j, n):
                    dve.wait_ge(unit_done, u + 1)
                    dve.wait_ge(hid_lo, n)
                    dve.scalar_tensor_tensor(out=halves(T[:, j % TS, :]), in0=unit_psum(j), scalar=0.0,
                                             in1=halves(rms[:, :]), op0=ALU.max, op1=ALU.mult).then_inc(unit_out, 1)

                n0 = BLOCKS * KT * (u0 == U_MLP1)
                inverse(r)
                dve.wait_ge(rms_ready, r + 1)
                for j in range(KT):
                    if j < TS:
                        dve.wait_ge(unit_done, u0 + j + 1)
                        dve.scalar_tensor_tensor(out=halves(T[:, j % TS, :]), in0=unit_psum(j), scalar=0.0,
                                                 in1=halves(rms[:, :]), op0=ALU.max, op1=ALU.mult).then_inc(unit_out, 1)
                    else:
                        hidden(u0 + j, j, n0 + j - TS + 1)
                    weight_rest(u0 + j + HL, (u0 + j + HL) % RAW)
                with dve.Fori(0, BLOCKS - 1) as i:
                    u = i * (2 * KT) + u0
                    for j in range(KT):
                        dve.wait_ge(unit_done, u + (KT + j + 1))
                        dve.wait_ge(unit_out, u + (j + 1 - KT))
                        dve.tensor_tensor(halves(X[:, j, :]), unit_psum(j), halves(X[:, j, :]), ALU.add)\
                           .then_inc(unit_out, 1)
                        weight_rest(u + (KT + j + HL), (u0 + KT + j + HL) % RAW)
                    for j in range(KT):
                        hidden(u + (2 * KT + j), j, i * KT + (n0 + KT + j - TS + 1))
                        weight_rest(u + (2 * KT + j + HL), (u0 + j + HL) % RAW)
                u = u0 + (BLOCKS - 1) * 2 * KT
                for j in range(KT):
                    dve.wait_ge(unit_out, u + j + 1 - KT)
                    add_residual(u + KT + j, j, j)
                    if g is not None:
                        norm_rest(g, j, X[:, j, :], pair_of(dst, j))
                    rest(u + KT + j + HL)

            def items_bias(n):
                kind, a, i = ITEMS[n]
                s0, s = 2 * (n % 2), n % 2
                dve.wait_ge(scored, n + 1)
                if n >= 2:
                    dve.wait_ge(weighted, n - 1)
                if kind == "diff":
                    at = ps[:, s0:s0 + 2, i * P:(i + 1) * P]
                    own.chain(dve.tensor_tensor(at, at, causal.unsqueeze(1).to_broadcast([P, 2, P]), ALU.add))
                if kind == "decode":
                    at = ps[:, s0, PAST:PAST + SAMPLE]
                    m = K_DMASK + a * SAMPLE
                    own.chain(dve.tensor_tensor(at, at, con[:, m:m + SAMPLE], ALU.add))
                if kind in ("mem", "diff"):
                    n_keys = MEM if kind == "mem" else (i + 1) * P
                    own.chain(dve.tensor_reduce(mx[:, s, :], ps[:, s0:s0 + 2, 0:n_keys], AX.X, ALU.max))
                    dve.tensor_scalar(nb[:, s, :], mx[:, s, :], -SCALE, None, ALU.mult).then_inc(biased, 1)
                else:
                    n_keys = MEM if kind == "memdec" else PAST + SAMPLE
                    own.chain(dve.tensor_reduce(mx[:, s, 0:1], ps[:, s0, 0:n_keys], AX.X, ALU.max))
                    dve.tensor_scalar(nb[:, s, 0:1], mx[:, s, 0:1], -SCALE, None, ALU.mult).then_inc(biased, 1)

            def items_weight(n):
                kind, a, i = ITEMS[n]
                l = int(n >= L0_ITEMS)
                s, pr = n % 2, Pr[l][n % 2]
                dve.wait_ge(exped, n + 1)
                nj = 1 if kind in ("memdec", "decode") else 2
                own.chain(dve.reciprocal(coef[:, s, 0:nj], sums[:, s, 0:nj]))
                if kind == "mem":
                    for j in range(2):
                        ins = dve.tensor_scalar(pr[:, j, 0:MEM], pr[:, j, 0:MEM], coef[:, s, j:j + 1], None, ALU.mult)
                elif kind == "memdec":
                    ins = dve.tensor_scalar(pr[:, 0, 0:MEM], pr[:, 0, 0:MEM], coef[:, s, 0:1], None, ALU.mult)
                elif kind == "diff":
                    k = (i + 1) * P
                    own.step(dve.tensor_scalar(coef[:, s, 1:2], coef[:, s, 1:2], lam_n, None, ALU.mult))
                    own.chain(dve.tensor_scalar(pr[:, 0, 0:k], pr[:, 0, 0:k], coef[:, s, 0:1], None, ALU.mult))
                    ins = dve.scalar_tensor_tensor(out=pr[:, 0, 0:k], in0=pr[:, 1, 0:k], scalar=coef[:, s, 1:2],
                                                   in1=pr[:, 0, 0:k], op0=ALU.mult, op1=ALU.add)
                else:
                    own.chain(dve.tensor_scalar(coef[:, s, 1:2], coef[:, s, 0:1], sgn, None, ALU.mult))
                    ins = dve.tensor_scalar(C2[:, s, :], con[:, K_SEL:K_SEL + 48], coef[:, s, 1:2], None, ALU.mult)
                ins.then_inc(weighted, 1)

            def items_drain(n):
                kind, a, i = ITEMS[n]
                m0 = 6 + n % 2
                dve.wait_ge(mixed, n + 1)
                if kind == "mem":
                    ins = dve.tensor_copy(Z[:, 6 + a, i * P:(i + 1) * P], ps[:, m0, 0:P])
                elif kind == "memdec":
                    for hh in range(2):
                        lane = slice(64 * hh, 64 * hh + 64)
                        for pr in range(MEM_PAIRS):
                            src = ps[lane, m0, pr * 32:pr * 32 + 32].rearrange("p (b h t) -> p b h t", b=4, h=2)
                            dst = Z[lane, 6 + pr, PROMPT + 16 * a:PROMPT + 16 * a + 16].rearrange("p (b t) -> p b t", b=4)
                            ins = dve.tensor_copy(dst, src[:, :, hh, :])
                elif kind == "diff":
                    k = QT * a + i
                    own.step(dve.tensor_copy(O[:, k, :], ps[:, m0, 0:P]))
                    if k >= 2:
                        dve.wait_ge(squared, k - 1)
                    ins = dve.tensor_scalar(SQ[:, 0, k % 2 * P:k % 2 * P + P], ps[:, m0, 0:P], CLAMP, -CLAMP,
                                            ALU.min, ALU.max)
                else:
                    ins = dve.tensor_copy(Z[:, 0:HEADS, PROMPT + 8 * a:PROMPT + 8 * a + 8],
                                          ps[:, m0, 0:48].rearrange("p (h t) -> p h t", h=HEADS))
                ins.then_inc(drained, 1)

            def attention(n0, n1, between=None):
                items_bias(n0)
                for n in range(n0, n1 + 2):
                    if n < n1:
                        items_weight(n)
                    if n + 1 < n1:
                        items_bias(n + 1)
                    if n - 2 >= n0:
                        items_drain(n - 2)
                    if between:
                        between(n)

            def pooling(n):
                if n - 3 in range(MIXT):
                    o = n - 3
                    dve.wait_ge(mix_hi, o + 1)
                    dve.tensor_tensor(A[:, 1, o, :], T[:, 2 + o % 2, :], A[:, 0, o, :].bitcast(F32),
                                      ALU.subtract).then_inc(mix_lo, 1)
                if n - 1 in range(MIXT):
                    o = n - 1
                    dve.wait_ge(window_ready, o + 1)
                    if o >= 2:
                        dve.wait_ge(mix_lo, o - 1)
                    ln, wd, t = line[:, o % 2, :], window[:, o % 2, :], T[:, 2 + o % 2, :]
                    inv = con[:, K_INVW + o:K_INVW + o + 1]
                    own.step(dve.scalar_tensor_tensor(out=t[:, 16:PROMPT], in0=wd[:, 32:16 + PROMPT], scalar=inv,
                                                      in1=ln[:, 32:16 + PROMPT], op0=ALU.mult, op1=ALU.subtract))
                    sp_ = lambda v: v[:, 16 + PROMPT:EXT].rearrange("p (b t) -> p b t", b=REQS)[:, :, HIST:HIST + STEPS]
                    own.step(dve.scalar_tensor_tensor(out=t[:, PROMPT:TOK].rearrange("p (b t) -> p b t", b=REQS),
                                                      in0=sp_(wd), scalar=inv, in1=sp_(ln), op0=ALU.mult,
                                                      op1=ALU.subtract))
                    own.chain(dve.tensor_tensor(t[:, 0:16], wd[:, 16:32], con[:, K_TAB + 16 * o:K_TAB + 16 * o + 16],
                                                ALU.mult))
                    dve.tensor_tensor(t[:, 0:16], t[:, 0:16], ln[:, 16:32], ALU.subtract).then_inc(pooled, 1)

            rest(0)
            dve.wait_ge(memx_loaded, 16)
            dve.wait_ge(par_loaded, 16)
            for k in range(KT):
                norm_rest(G_MEM, k, memX[:, k, :], pair_of(A, k, MEM))
            rest(1)
            lam = par[:, C_LAM:C_LAM + 256].rearrange("p (v d) -> p v d", v=4)
            own.chain(dve.tensor_tensor(T[:, 0, 0:64], lam[:, 0, :], lam[:, 1, :], ALU.mult))
            own.chain(dve.tensor_tensor(T[:, 0, 64:128], lam[:, 2, :], lam[:, 3, :], ALU.mult))
            dve.tensor_reduce(lamw[:, 0:2], T[:, 0, 0:128].rearrange("p (v d) -> p v d", v=2), AX.X, ALU.add)\
               .then_inc(lam_dot, 1)
            dve.wait_ge(x_loaded, 16)
            for k in range(2):
                norm_rest(G_IN0, k, X[:, k, :], pair_of(B, k))
            inverse(R_MEM)
            for k in range(2, KT):
                norm_rest(G_IN0, k, X[:, k, :], pair_of(B, k))
            dve.wait_ge(rms_ready, 1)
            for u in range(8):
                dve.wait_ge(unit_done, u + 1)
                dst = memKT[:, u // 2, u % 2, :] if u < 4 else T[:, u - 4, 0:MEM]
                if u == 4:
                    dve.wait_ge(lam_dot, 1)
                dve.tensor_tensor(dst, ps[:, 2 * (u % PS), 0:MEM], rms_mem[:, :], ALU.mult).then_inc(unit_out, 1)
                rest(u + HL)
            inverse(R_IN0)
            dve.wait_ge(lam_exp, 1)
            dve.wait_ge(rms_ready, 2)
            own.chain(dve.tensor_tensor(lamw[:, 4:5], lamw[:, 2:3], lamw[:, 3:4], ALU.subtract))
            own.step(dve.tensor_scalar(gsub, par[:, C_SUBLN:C_SUBLN + 1], 1.0 - LAM_INIT, None, ALU.mult))
            own.chain(dve.tensor_scalar(lam_n, lamw[:, 4:5], LAM_INIT, -1.0, ALU.add, ALU.mult))
            dve.wait_ge(con_loaded, 16)
            own.chain(dve.tensor_scalar(sgn, con[:, K_ROWJ + 1:K_ROWJ + 2], lam_n, None, ALU.mult))
            own.chain(dve.tensor_tensor(sgn, sgn, con[:, K_ROWJ:K_ROWJ + 1], ALU.add))
            for j in range(KT):
                dve.wait_ge(unit_done, U_IN0 + j + 1)
                dve.tensor_tensor(halves(Z[:, IN_ORDER[j], :]), unit_psum(j), halves(rms[:, :]), ALU.mult)\
                   .then_inc(unit_out, 1)
                rest(U_IN0 + j + HL)
            attention(0, L0_ITEMS, pooling)
            dve.wait_ge(cat_hi, 1)
            dve.tensor_tensor(B[:, 1, 6:8, :], Z[:, 6:8, :], B[:, 0, 6:8, :].bitcast(F32), ALU.subtract)\
               .then_inc(cat_lo, 1)
            for j in range(MIXT):
                dve.wait_ge(mix_hi, MIXT + j + 1)
                dve.scalar_tensor_tensor(out=halves(B[:, 1, j, :]), in0=unit_psum(j),
                                         scalar=par[:, C_PSCALE + j:C_PSCALE + j + 1],
                                         in1=halves(B[:, 0, j, :].bitcast(F32)), op0=ALU.mult, op1=ALU.subtract)\
                   .then_inc(unit_out, 1)
                rest(U_POOL + j + HL)
            out_units(U_OUT0, G_MLP0, A)
            mlp(U_MLP0, R_MLP0, G_IN1, A)
            for k in range(KT):
                norm_rest(G_KV, k, X[:, k, :], pair_of(B, k))
            inverse(R_IN1)
            dve.wait_ge(rms_ready, R_IN1 + 1)
            dve.wait_ge(pool_stored, 16)
            for j in range(KT):
                dve.wait_ge(unit_done, U_IN1 + j + 1)
                dve.tensor_tensor(halves(Z[:, IN_ORDER[j], :]), unit_psum(j), halves(rms[:, :]), ALU.mult)\
                   .then_inc(unit_out, 1)
                rest(U_IN1 + j + HL)
            for j in range(MIXT):
                dve.wait_ge(unit_done, U_K + j + 1)
                dve.tensor_tensor(halves(Kt[:, j, :]), unit_psum(j), halves(rms[:, :]), ALU.mult).then_inc(unit_out, 1)
                rest(U_K + j + HL)
            for j in range(MIXT):
                dve.wait_ge(unit_done, U_V + j + 1)
                if j >= TS:
                    dve.wait_ge(v_turned, j - TS + 1)
                dve.tensor_tensor(halves(T[:, j % TS, :]), unit_psum(j), halves(rms[:, :]), ALU.mult)\
                   .then_inc(unit_out, 1)
                rest(U_V + j + HL)
                if j == 0:
                    dve.wait_ge(k_swapped, 64)
                own.step(dve.tensor_tensor(swap[:, j, :], swap[:, j, :], rope[:, 1, :], ALU.mult))
                own.chain(dve.tensor_tensor(Kt[:, j, :], Kt[:, j, :], rope[:, 0, :], ALU.mult))
                ins = dve.tensor_tensor(Kt[:, j, :], Kt[:, j, :], swap[:, j, :], ALU.add)
                if j == MIXT - 1:
                    ins.then_inc(k_roped, 1)
            attention(L0_ITEMS, len(ITEMS))
            zs = Z[:, 0:MIXT, PROMPT:TOK]
            grid = lambda v: v.rearrange("p (h t) -> p h t", h=MIXT)
            dve.wait_ge(drained, len(ITEMS))
            dve.tensor_scalar(grid(small[0]), zs, CLAMP, -CLAMP, ALU.min, ALU.max).then_inc(sub_mean, 1)

            def means(total, total_big, mean, scratch, keep):
                own.step(dve.tensor_scalar(keep, total_big, BIG_END, SUB ** 0.5, ALU.is_lt, ALU.mult))
                own.step(dve.tensor_scalar(mean, total, 1.0 / P, None, ALU.mult))
                own.chain(dve.tensor_scalar(scratch, total_big, BIG_END, 2.0 ** 100, ALU.min, ALU.mult))
                dve.scalar_tensor_tensor(out=mean, in0=scratch, scalar=2.0 ** 36 / P, in1=mean, op0=ALU.mult,
                                         op1=ALU.max).then_inc(sub_mean, 1)

            dve.wait_ge(squared, QT * HEADS)
            means(ss[:, :], ss_big[:, :], ss[:, :], rr2[:, :], keep[:, :])
            dve.wait_ge(sub_mm, 1)
            means(ps[:, 6, 0:NS], ps[:, 7, 0:NS], small[1], small[2], small[3])
            dve.wait_ge(sub_root, 1)
            own.chain(dve.reciprocal(rr2[:, :], rr[:, :]))
            dve.tensor_tensor(rr2[:, :], rr2[:, :], keep[:, :], ALU.mult).then_inc(sub_rms, 1)
            dve.wait_ge(sub_rms, 1)
            for h in range(HEADS):
                for i in range(QT):
                    n = QT * h + i
                    ins = dve.tensor_scalar(O[:, n, :], O[:, n, :], rr2[:, n:n + 1], None, ALU.mult)
                ins.then_inc(sub_scaled, 1)
            dve.wait_ge(sub_root, 2)
            own.chain(dve.reciprocal(small[0], small[0]))
            own.chain(dve.tensor_tensor(small[0], small[0], small[3], ALU.mult))
            dve.tensor_tensor(zs, zs, grid(small[0]), ALU.mult).then_inc(sub_sample, 1)
            dve.wait_ge(cat_hi, 2)
            dve.tensor_tensor(A[:, 1, 6:8, :], Z[:, 6:8, :], A[:, 0, 6:8, :].bitcast(F32), ALU.subtract)\
               .then_inc(cat_lo, 1)
            for h in range(HEADS):
                dve.wait_ge(mix_hi, 2 * MIXT + h + 1)
                dve.scalar_tensor_tensor(out=A[:, 1, h, 0:PROMPT], in0=ps[:, h, :], scalar=gsub,
                                         in1=A[:, 0, h, 0:PROMPT].bitcast(F32), op0=ALU.mult, op1=ALU.subtract)\
                   .then_inc(mix_lo, 1)
            dve.wait_ge(mix_hi, 3 * MIXT + 1)
            dve.scalar_tensor_tensor(out=A[:, 1, 0:MIXT, PROMPT:TOK], in0=zs, scalar=gsub,
                                     in1=A[:, 0, 0:MIXT, PROMPT:TOK].bitcast(F32), op0=ALU.mult, op1=ALU.subtract)\
               .then_inc(mix_lo, 1)
            out_units(U_OUT1, G_MLP1, B)
            mlp(U_MLP1, R_MLP1, None, None)
            inverse(R_FINAL)
            dve.wait_ge(rms_ready, R_FINAL + 1)
            for k in range(KT):
                dve.scalar_tensor_tensor(out=Z[:, k, :], in0=X[:, k, :], scalar=gain(G_FINAL, k), in1=rms[:, :],
                                         op0=ALU.mult, op1=ALU.mult).then_inc(y_ready, 1)

        @block.gpsimd
        def _(pool):
            own = Order(pool, pool_order)

            def sum_squares(r, cols=TOK):
                if r:
                    pool.wait_ge(norm_mm, r)
                for k in range(1, KT):
                    pool.wait_ge(sq_ready, KT * r + k + 1)
                    if k >= 2:
                        pool.wait_ge(sq_summed, (KT - 1) * r + k - 1)
                    a = SQ[:, 0, 0:cols] if k == 1 else sq_sum[:, 0:cols]
                    pool.tensor_tensor(sq_sum[:, 0:cols], a, SQ[:, k % 2, 0:cols], ALU.add).then_inc(sq_summed, 1)

            def hidden_rest(hidden, j, n):
                pool.wait_ge(hid_hi, n)
                t = T[:, j % TS, :]
                sq = SQ[:, j % 2, :]
                pool.tensor_tensor(sq, t, t, ALU.mult).then_inc(hid_sq, 1)
                pool.wait_ge(hid_sq, n)
                pool.tensor_tensor(hidden[:, 1, j, :], sq, hidden[:, 0, j, :].bitcast(F32), ALU.subtract)\
                    .then_inc(hid_lo, 1)

            def mlp(u0, hidden, r):
                n0 = BLOCKS * KT * (u0 == U_MLP1)
                with pool.Fori(0, BLOCKS) as i:
                    for j in range(KT):
                        hidden_rest(hidden, j, i * KT + (n0 + j + 1))
                sum_squares(r)

            def rotate(swapped, done, dst):
                for q in range(4):
                    pool.dma_start(swap[32 * q:32 * q + 32, :, :], dst[32 * (q ^ 1):32 * (q ^ 1) + 32, 0:MIXT, :])\
                        .then_inc(swapped, 16)

            def query_blocks(layer):
                for hh in range(2):
                    lane = slice(64 * hh, 64 * hh + 64)
                    for pr in range(MEM_PAIRS):
                        c = 8 * pr + 4 * hh
                        ins = pool.tensor_copy(QbdM[lane, :, pr, c:c + STEPS],
                                               Z[lane, 6 + pr, PROMPT:TOK].rearrange("p (b t) -> p b t", b=REQS))
                        if (hh, pr) != (1, 1):
                            own.chain(ins)
                ins.then_inc(qbdm_ready, 1)
                pool.wait_ge(qbdm_ready, layer + 1)

            own.step(pool.memset(epsc, EPS))
            own.step(pool.memset(eps_sub, EPS * SUB))
            own.step(pool.memset(line[:, :, 0:16], 0.0))
            own.step(pool.memset(QbdM[:, :, :, :], 0.0))
            pool.memset(ones[:, :], 1.0).then_inc(const_ready, 1)
            sum_squares(R_MEM, MEM)
            sum_squares(R_IN0)
            pool.wait_ge(unit_out, 4)
            pool.dma_start(o_memk, memKT[:, :, :, :]).then_inc(memk_stored, 16)
            pool.wait_ge(unit_out, U_IN0 + 2)
            own.settle()
            query_blocks(0)
            pool.wait_ge(memv_ready, 2)
            pool.dma_start(o_memv, memVt[:, :, :, :]).then_inc(memv_stored, 16)
            pool.wait_ge(unit_out, U_POOL)
            pool.dma_start(o_pool, Z[:, 0:MIXT, PROMPT - HIST:PROMPT]).then_inc(pool_stored, 16)
            for o in range(MIXT):
                pool.wait_ge(line_ready, 3 * (o + 1))
                if o >= 2:
                    pool.wait_ge(pooled, o - 1)
                ln, wd = line[:, o % 2, :], window[:, o % 2, :]
                lo_w, hi_w = WINDOWS[(2 * o) // 3], WINDOWS[(2 * o + 1) // 3]
                parts = [(0, P, lo_w)] if lo_w == hi_w else [(0, 64, lo_w), (64, P, hi_w)]
                for p0, p1, w in parts:
                    src, shift, n = ln, 1, 0
                    while shift < w:
                        last = 2 * shift == w
                        dst = wd if last else partial[:, n % 2, :]
                        t0 = 16 if last else 2 * shift - 1
                        if n:
                            own.settle()
                        own.step(pool.tensor_tensor(dst[p0:p1, t0:EXT], src[p0:p1, t0:EXT],
                                                    src[p0:p1, t0 - shift:EXT - shift], ALU.add))
                        src, shift, n = dst, 2 * shift, n + 1
                    own.settle()
                reqs = ln[:, 16 + PROMPT:EXT].rearrange("p (b t) -> p b t", b=REQS)
                pool.tensor_copy(histb[:, o, :, :], reqs[:, :, STEPS:STEPS + HIST]).then_inc(window_ready, 1)
            pool.wait_ge(window_ready, MIXT)
            pool.dma_start(o_pools, histb[:, :, :, :]).then_inc(pools_stored, 16)
            sum_squares(R_MLP0)
            mlp(U_MLP0, B, R_IN1)
            pool.wait_ge(unit_out, U_IN1 + 2)
            query_blocks(1)
            pool.wait_ge(unit_out, U_K)
            rotate(q_swapped, None, Z)
            pool.wait_ge(q_swapped, 64)
            pool.wait_ge(rope_loaded, 16)
            for h in range(HEADS):
                own.step(pool.tensor_tensor(swap[:, h, :], swap[:, h, :], rope[:, 1, :], ALU.mult))
                own.chain(pool.tensor_tensor(Z[:, h, :], Z[:, h, :], rope[:, 0, :], ALU.mult))
                ins = pool.tensor_tensor(Z[:, h, :], Z[:, h, :], swap[:, h, :], ALU.add)
                if h < HEADS - 1:
                    own.step(ins)
            ins.then_inc(q_roped, 1)
            pool.wait_ge(q_roped, 1)
            pool.wait_ge(unit_out, U_V)
            rotate(k_swapped, None, Kt)
            pool.wait_ge(unit_done, U_OUT1)
            own.chain(pool.memset(Qbd[:, :, :, :], 0.0))
            for h in range(HEADS):
                for j in range(2):
                    lane = slice(64 * j, 64 * j + 64)
                    c = 8 * h + 4 * j
                    ins = pool.tensor_copy(Qbd[lane, h, :, c:c + STEPS],
                                           Z[lane, h, PROMPT:TOK].rearrange("p (b t) -> p b t", b=REQS))
                    if (h, j) != (HEADS - 1, 1):
                        own.chain(ins)
            ins.then_inc(qbd_ready, 1)
            pool.wait_ge(qbd_ready, 1)
            pool.wait_ge(v_ready, MIXT)
            pool.dma_start(o_v, Vt[:, :, :]).then_inc(v_stored, 16)
            pool.dma_start(o_vs, Vn[:, :]).then_inc(v_stored, 16)
            pool.wait_ge(k_roped, 1)
            pool.dma_start(o_k, Kt[:, :, :]).then_inc(k_stored, 16)
            sum_squares(R_MLP1)
            mlp(U_MLP1, A, R_FINAL)
            for s, n in ((memk_stored, 16), (memv_stored, 16), (pool_stored, 16), (pools_stored, 16),
                         (v_stored, 32), (k_stored, 16)):
                pool.wait_ge(s, n)

    return nc


def _units(w):
    k, m = w.shape
    return w.reshape(k // P, P, m // P, P).transpose(2, 1, 0, 3).reshape(m // P, P, k)


def _lanes(v):
    return v.T.reshape(-1, P, v.shape[0]).transpose(1, 0, 2)


def _constants():
    c = np.zeros((P, K_CONST), np.float32)
    c[:, K_IDENT:K_IDENT + P] = np.eye(P)
    c[:, K_CAUSAL:K_CAUSAL + P] = np.where(np.arange(P)[None, :] > np.arange(P)[:, None], NEG, 0.0)
    for row in range(P):
        o, rest = divmod(row, 64)
        h, j, t = rest // 8, rest % 8 // 4, rest % 4
        if h >= HEADS:
            continue
        for a in range(4):
            for key in range(SAMPLE):
                if not (key // STEPS == 2 * a + o and key % STEPS <= t):
                    c[row, K_DMASK + a * SAMPLE + key] = NEG
        c[row, K_SEL + o * 24 + h * 4 + t] = 1.0
        c[row, K_ROWJ + j] = 1.0
    for tile in range(MIXT):
        w = np.array([WINDOWS[(tile * P + p) // 192] for p in range(P)])
        c[:, K_INVW + tile] = 1.0 / w
        c[:, K_TAB + 16 * tile:K_TAB + 16 * tile + 16] = 1.0 / np.minimum(w[:, None], np.arange(16)[None, :] + 1)
    return c


def _angles():
    inv = (1.0 / (np.float32(10000.0) ** (np.arange(0, HD, 2, dtype=np.float32) / np.float32(HD)))).astype(np.float32)
    pos = np.concatenate([np.arange(PROMPT), np.tile(PAST + np.arange(STEPS), REQS)]).astype(np.float32)
    ang = (pos[None, :] * inv[np.arange(P) % 32][:, None]).astype(np.float32).astype(np.float64)
    sign = np.where(np.arange(P) % HD < 32, -1.0, 1.0)[:, None]
    return np.stack([np.cos(ang), sign * np.sin(ang)], axis=1).astype(np.float32)


def kernel(x_prompt, x_sample, state_pool, cache_mem_k, cache_mem_v, cache_k, cache_v, page_table, mem_prompt,
           norm1, norm2, final_norm, kv_norm, mem_norm, w_in, w_out, w_mem_k, w_mem_v, w_pool, pool_scale,
           w_k, w_v, lambda_q1, lambda_k1, lambda_q2, lambda_k2, subln, w_mlp1, w_mlp2):
    import concourse.bacc as bacc
    from concourse.bass_utils import run_bass_kernel_spmd

    f = np.ascontiguousarray
    a = {k: np.asarray(v) for k, v in locals().items() if k not in ("bacc", "run_bass_kernel_spmd", "f")}
    (x_prompt, x_sample, w_in, w_out, w_mem_k, w_mem_v, w_k, w_v, w_mlp1, w_mlp2, w_pool) = (
        a[n] for n in ("x_prompt", "x_sample", "w_in", "w_out", "w_mem_k", "w_mem_v", "w_k", "w_v",
                       "w_mlp1", "w_mlp2", "w_pool"))

    def w_mlp(l):
        up, down = _units(w_mlp1[l]), w_mlp2[l].reshape(BLOCKS, D, D)
        return [m for b in range(BLOCKS) for m in (up[KT * b:KT * b + KT], _units(down[b]))]

    pool_units = np.zeros((MIXT, P, D), np.float32)
    for pair in range(2):
        block = np.zeros((384, 384), np.float32)
        block[:192, :192], block[192:, 192:] = w_pool[0, 2 * pair], w_pool[0, 2 * pair + 1]
        pool_units[3 * pair:3 * pair + 3, :, :384] = _units(block)
    weights = np.concatenate(
        [_units(w_mem_k[0]), _units(w_mem_k[1]), _units(w_mem_v[0]), _units(w_mem_v[1]),
         _units(w_in[0])[IN_ORDER], pool_units, _units(w_out[0]), *w_mlp(0),
         _units(w_in[1])[IN_ORDER], _units(w_k), _units(w_v), _units(w_out[1]), *w_mlp(1)])

    tile = lambda v: v.reshape(-1, P).T
    lam = np.concatenate([a[n][0] for n in ("lambda_q1", "lambda_k1", "lambda_q2", "lambda_k2")])
    params = np.concatenate(
        [tile(v) for v in (a["mem_norm"], a["norm1"][0], a["norm2"][0], a["norm1"][1], a["kv_norm"],
                           a["norm2"][1], a["final_norm"], a["pool_scale"][0], a["subln"][0])]
        + [np.broadcast_to(lam, (P, 256))], axis=1)
    tokens = np.concatenate([x_prompt[0], x_sample.reshape(SAMPLE, D)])
    mem_k = a["cache_mem_k"].reshape(2, 4, 2, MEM, 2, 2, HD).transpose(0, 1, 5, 6, 2, 4, 3).reshape(2, 4, P, D)
    mem_v = a["cache_mem_v"].reshape(2, 4, 2, 2, P, 256).transpose(0, 1, 4, 2, 3, 5).reshape(2, 4, P, D)
    n_pool = a["cache_k"].shape[0]
    ins = {
        "x": _lanes(tokens), "mem": _lanes(a["mem_prompt"][0]),
        "hist": a["state_pool"][0].transpose(2, 0, 1).reshape(MIXT, P, REQS, HIST).transpose(1, 0, 2, 3),
        "params": params, "consts": _constants(), "angles": _angles(), "weights": weights,
        "mem_k": mem_k, "mem_v": mem_v,
        "page_k": a["cache_k"].transpose(0, 3, 4, 2, 1).reshape(n_pool, P, 768),
        "page_v": a["cache_v"].reshape(n_pool, P, 768),
        "page_table": a["page_table"].reshape(1, 16),
    }
    outs = {"y": (P, KT, TOK), "pool_prompt": (P, MIXT, HIST), "mem_k_prompt": (P, 2, 2, MEM),
            "mem_v_prompt": (P, 2, 2, MEM), "k": (P, HEADS, TOK), "v_prompt": (P, QT, 768),
            "pool_sample": (P, MIXT, REQS, HIST), "v_sample": (SAMPLE, 768)}
    nc = bacc.Bacc("TRN2", target_bir_lowering=False, num_devices=1)
    arrays = {f"in_{k}": f(v) for k, v in ins.items()}
    args = [nc.dram_tensor(k, v.shape, mybir.dt.from_np(v.dtype), kind="ExternalInput").ap() for k, v in arrays.items()]
    args += [nc.dram_tensor(f"out_{k}", s, mybir.dt.float32, kind="ExternalOutput").ap() for k, s in outs.items()]
    build(nc, *args)
    r = run_bass_kernel_spmd(nc, [arrays], core_ids=[0]).results[0]
    got = {k: np.asarray(r[f"out_{k}"]) for k in outs}

    rows = lambda v: v.transpose(2, 1, 0).reshape(v.shape[2], -1)
    y, k = rows(got["y"]), rows(got["k"])
    mk = got["mem_k_prompt"].transpose(1, 3, 2, 0).reshape(2, 1, MEM, 4, HD)
    mv = got["mem_v_prompt"].transpose(1, 2, 0, 3).reshape(2, 1, MEM, 4, HD)
    ps = got["pool_sample"].transpose(2, 3, 1, 0).reshape(1, REQS, HIST, 768)
    return (f(y[:PROMPT]).reshape(1, PROMPT, D), f(y[PROMPT:]).reshape(REQS, STEPS, D),
            f(rows(got["pool_prompt"])).reshape(1, 1, HIST, 768), f(mk), f(mv),
            f(k[:PROMPT]).reshape(1, PROMPT, HEADS, 2, HD),
            f(got["v_prompt"].transpose(1, 0, 2)).reshape(1, PROMPT, HEADS, 2 * HD), f(ps),
            f(k[PROMPT:]).reshape(REQS, STEPS, HEADS, 2, HD),
            f(got["v_sample"]).reshape(REQS, STEPS, HEADS, 2 * HD))
```

```python
import concourse.bass as bass
from concourse import mybir
from contextlib import ExitStack
import math
import numpy as np

D = 1024
P = 128
KT = D // P
PROMPT, REQS, STEPS = 512, 8, 4
SAMPLE = REQS * STEPS
TOK = PROMPT + SAMPLE
HALF = TOK // 2
SLOTS = 3
SHIFT = 14.0
PAST, PAGE = 256, 128
PAGES = PAST // PAGE
MEM, MEM_PAIRS, HD = 256, 2, 64
MIXT = 6
HIST = 15
WINDOWS = (2, 4, 8, 16)
EXT = 16 + PROMPT + REQS * (HIST + STEPS)
HEADS = 6
QT = PROMPT // P
SCALE = 64 ** -0.5
EPS = 1e-6
NEG = -1e30
CLAMP, BIG, BIG_END = 1.6e18, 2.0 ** -68, 2.0 ** -8
SUB = 2.0 ** -8
LAM_INIT = 0.8 - 0.6 * math.exp(-0.3)

U_MEM, U_IN0, U_POOL, U_OUT0, U_MLP0 = 0, 8, 16, 22, 30
U_IN1, U_K, U_V, U_OUT1, U_MLP1 = 94, 102, 108, 114, 122
N_UNITS = 186
POOL_COLS = 3 * P
BLOCKS = 4
RAW, HL, PS, TS = 4, 2, 2, 4
IN_ORDER = [[6, 7, 4, 5, 3, 1, 2, 0],
            [6, 7, 0, 1, 2, 3, 4, 5]]
POOL_TILES = IN_ORDER[0][2:]
POOL_OUT = [3, 4, 5, 0, 1, 2]

R_MEM, R_IN0, R_MLP0, R_IN1, R_MLP1, R_FINAL = range(6)
G_MEM, G_IN0, G_MLP0, G_IN1, G_KV, G_MLP1, G_FINAL = range(7)

C_GAIN = 0
C_PSCALE = C_GAIN + 7 * KT
C_SUBLN = C_PSCALE + MIXT
C_LAM = C_SUBLN + 1
C_PARAM = C_LAM + 256
GROUP = 40
K_IDENT = 0
K_CAUSAL = K_IDENT + P
K_DMASK = K_CAUSAL + P
K_SEL = K_DMASK + 4 * SAMPLE
K_ROWJ = K_SEL + 2 * GROUP
K_INVW = K_ROWJ + 2
K_TAB = K_INVW + MIXT
K_CONST = K_TAB + MIXT * 16


def attention_items(layer):
    mem = [("mem", pr, i) for pr in range(MEM_PAIRS) for i in range(QT)]
    cached = [("memdec", 0, 0), ("memdec", 1, 0)]
    if layer == 0:
        items, places = mem, (1, 7)
    else:
        items = mem + [("diff", h, i) for h in range(HEADS) for i in range(QT)]
        cached += [("decode", c, 0) for c in range(REQS // 2)]
        places = (3, 9, 16, 23, 30, 36)
    for at, item in zip(places, cached):
        items.insert(at, item)
    return items


ITEMS = attention_items(0) + attention_items(1)
L0_ITEMS = len(attention_items(0))


def build(nc, xT, memT, hist, params, consts, ropes, weights, memK, memV, cacheK, cacheV, pages,
          o_y, o_pool, o_memk, o_memv, o_k, o_v, o_pools, o_vs):
    F32, F32R, I32 = mybir.dt.float32, mybir.dt.float32r, mybir.dt.int32
    ALU, ACT, AX = mybir.AluOpType, mybir.ActivationFunctionType, mybir.AxisListType

    ctx = ExitStack()
    with ctx:
        base = nc.sbuf_base
        slab_bytes = 212800
        ctx.enter_context(nc.sbuf_tensor("slab", [P, slab_bytes // 4], F32))
        top = [(base + 31) // 32 * 32]
        end = base + slab_bytes

        def take(n_bytes):
            at = top[0]
            top[0] += (n_bytes + 31) // 32 * 32
            assert top[0] <= end, (top[0], end)
            return at

        def place(name, shape, dt, at):
            return nc.alloc_sbuf_tensor_at(name, shape, dt, offset=at)

        def new(name, shape, dt=F32):
            return place(name, shape, dt, take(4 * math.prod(shape[1:])))

        X = new("residual", [P, KT, TOK])
        a_at, b_at = take(8 * KT * TOK), take(8 * KT * TOK)
        A = place("operand_a", [P, 2, KT, TOK], F32R, a_at)
        B = place("operand_b", [P, 2, KT, TOK], F32R, b_at)
        Z = new("projected", [P, KT, TOK])
        raw = new("weights_raw", [P, RAW, D])
        split = new("weights_split", [P, HL, 2, D], F32R)
        T = new("staging", [P, TS, TOK])
        sq_at = take(12 * TOK)
        SQ = place("squares", [P, 2, TOK], F32, sq_at)
        sq_sum = place("squares_sum", [P, TOK], F32, sq_at + 8 * TOK)
        rms = new("inv_rms", [P, TOK])
        rms_mem = new("inv_rms_mem", [P, MEM])
        kv_at = take(2 * 12288)
        k_at = take(4 * HEADS * TOK)
        memKT = new("mem_keys", [P, 2, MEM_PAIRS, MEM])
        memVt = new("mem_values", [P, 2, 2, MEM])
        QbdM = new("mem_query_blocks", [P, REQS, MEM_PAIRS, 32])
        par = new("params", [P, C_PARAM])
        con = new("constants", [P, K_CONST])
        tiny = new("tiny", [P, 164])
        C2 = new("combine", [P, 2, 2 * GROUP])
        pg = new("page_table", [1, 16], I32)
        ones = new("ones", [P, P])
        Kt = place("keys", [P, HEADS, TOK], F32, k_at)
        line = place("pool_line", [P, 2, EXT], F32, k_at)
        window = place("pool_window", [P, 2, EXT], F32, k_at + 8 * EXT)
        kv = place("cache_tiles", [P, 2, 2, 2 * 768], F32, kv_at)
        swap = place("rotated", [P, MIXT, TOK], F32, kv_at)
        rope = place("cos_sin", [P, 2, TOK], F32, kv_at + 4 * MIXT * TOK)
        partial = place("window_partial", [P, 2, EXT], F32, sq_at)
        memX = place("mem_residual", [P, KT, MEM], F32, kv_at)
        histb = new("pool_history", [P, MIXT, REQS, HIST])
        Vt = place("values", [P, QT, 768], F32, a_at)
        Vn = place("values_new", [SAMPLE, 768], F32, a_at + 4 * KT * TOK)
        O = place("attention_out", [P, 24, P], F32, b_at)
        Qbd = place("query_blocks", [P, HEADS, REQS, 64], F32, b_at + 16384)
        Pr = [[place(f"probs_l0_{s}", [P, 2, MEM], F32, a_at + (KT * s + 6) * 4 * TOK) for s in range(2)],
              [place(f"probs_l1_{s}", [P, 2, 512], F32, b_at + at) for s, at in enumerate((12288, 28672))]]
        Pr[1].append(T[:, 2:4, :].rearrange("p a b -> p (a b)")[:, 0:1024].rearrange("p (a b) -> p a b", a=2))
        PT = [T[:, s, 0:512] for s in range(2)]

        ps = ctx.enter_context(nc.psum_tensor("psum", [P, 8, 512], F32))

        ident = con[:, K_IDENT:K_IDENT + P]
        causal = con[:, K_CAUSAL:K_CAUSAL + P]

        def gain(g, k):
            return par[:, C_GAIN + g * KT + k:C_GAIN + g * KT + k + 1]

        epsc, lam_n, gsub, sgn = tiny[:, 0:1], tiny[:, 1:2], tiny[:, 2:3], tiny[:, 3:4]
        lamw = tiny[:, 4:12]
        ss = tiny[:, 16:40]
        rr = tiny[:, 40:64]
        rr2 = tiny[:, 64:88]
        ss_big, keep = tiny[:, 88:112], tiny[:, 112:136]
        mx, nb, sums, coef = (tiny[:, 136 + 6 * i:142 + 6 * i].rearrange("p (s j) -> p s j", s=SLOTS) for i in range(4))
        ratio = tiny[:, 160:160 + SLOTS]
        exp_shift = tiny[:, 14:16]
        eps_sub = tiny[:, 12:13]
        NS = MIXT * SAMPLE
        small = [T[:, 2 + i // 2, (i % 2) * NS:(i % 2) * NS + NS] for i in range(4)]

        def sem(name):
            return ctx.enter_context(nc.semaphore(name))

        raw_loaded = [sem(f"raw_loaded{i}") for i in range(RAW)]
        weight_hi, weight_lo = sem("weight_hi"), sem("weight_lo")
        unit_done, unit_out = sem("unit_done"), sem("unit_out")
        x_loaded, memx_loaded = sem("x_loaded"), sem("memx_loaded")
        par_loaded, con_loaded = sem("par_loaded"), sem("con_loaded")
        hist_loaded, rope_loaded, pg_loaded = sem("hist_loaded"), sem("rope_loaded"), sem("pg_loaded")
        sq_ready, sq_summed = sem("sq_ready"), sem("sq_summed")
        norm_hi, norm_lo = sem("norm_hi"), sem("norm_lo")
        norm_mm, root_ready, rms_ready = sem("norm_mm"), sem("root_ready"), sem("rms_ready")
        hid_hi, hid_lo = sem("hid_hi"), sem("hid_lo")
        mix_hi, mix_lo = sem("mix_hi"), sem("mix_lo")
        cat_hi, cat_lo = sem("cat_hi"), sem("cat_lo")
        memv_turned, memv_ready = sem("memv_turned"), sem("memv_ready")
        v_turned, v_ready = sem("v_turned"), sem("v_ready")
        line_ready, window_ready, pooled = sem("line_ready"), sem("window_ready"), sem("pooled")
        kv_loaded = [sem(f"kv_loaded{i}") for i in range(2)]
        qbdm_ready, qbd_ready = sem("qbdm_ready"), sem("qbd_ready")
        q_swapped, k_swapped = sem("q_swapped"), sem("k_swapped")
        q_roped, k_roped = sem("q_roped"), sem("k_roped")
        scored, biased, exped = sem("scored"), sem("biased"), sem("exped")
        weighted, turned, copied = sem("weighted"), sem("turned"), sem("copied")
        mixed, drained = sem("mixed"), sem("drained")
        squared, clamped = sem("squared"), sem("clamped")
        half_scored = sem("half_scored")
        sub_mean = sem("sub_mean")
        sub_root, sub_rms, sub_mm = sem("sub_root"), sem("sub_rms"), sem("sub_mm")
        sub_sample = sem("sub_sample")
        sub_scaled, sub_turned = sem("sub_scaled"), sem("sub_turned")
        const_ready = sem("const_ready")
        lam_dot, lam_exp = sem("lam_dot"), sem("lam_exp")
        y_ready = sem("y_ready")
        stored = sem("stored")
        hid_sq = sem("hid_sq")
        v_stored, k_stored = sem("v_stored"), sem("k_stored")
        memk_stored, memv_stored = sem("memk_stored"), sem("memv_stored")
        pool_stored, pools_stored = sem("pool_stored"), sem("pools_stored")
        act_order, dve_order, pool_order = sem("act_order"), sem("dve_order"), sem("pool_order")
        lo_of = lambda k: slice(k * P, (k + 1) * P)

        class Order:

            def __init__(self, eng, s):
                self.eng, self.sem, self.n = eng, s, 0

            def step(self, ins):
                self.n += 1
                ins.then_inc(self.sem, 1)

            def settle(self):
                self.eng.wait_ge(self.sem, self.n)

            def chain(self, ins):
                self.step(ins)
                self.settle()

        def halves(ap):
            return ap.rearrange("p (a b) -> p a b", a=2)

        def unit_cols(u):
            return POOL_COLS if isinstance(u, int) and U_POOL <= u < U_OUT0 else D

        def unit_psum(j):
            return ps[:, 2 * (j % PS):2 * (j % PS) + 2, 0:HALF]

        chunks = ([("mem", 0, c) for c in range(4)] + [("mem", 1, c) for c in range(4)]
                  + [("page", 0, b) for b in range(REQS)])

        def kv_ready(eng, n):
            done = 32 * (n // 2 + 1) if n < 8 else 32 * 4 + 64 * ((n - 8) // 2 + 1)
            eng.wait_ge(kv_loaded[n % 2], done)

        def chunk_of(n):
            kind, a, _ = ITEMS[n]
            l = int(n >= L0_ITEMS)
            return 4 * l + 2 * a if kind == "memdec" else 8 + 2 * a

        def slots(n):
            return SLOTS if n >= L0_ITEMS else 2

        def score_banks(n):
            if n < L0_ITEMS:
                return ps[:, 4 + n % 2, :].rearrange("p (j k) -> p j k", j=2)
            return ps[:, 2 * (n % SLOTS):2 * (n % SLOTS) + 2, :]

        DEC = [n for n, it in enumerate(ITEMS) if it[0] in ("memdec", "decode")]

        block = ctx.enter_context(nc.Block())

        @block.sync
        def _(sp):
            def load(u, first):
                s = u % RAW
                if not first:
                    sp.wait_ge(weight_lo, u - RAW + 1)
                n = unit_cols(u)
                sp.dma_start(raw[:, s, 0:n], weights[u][:, 0:n]).then_inc(raw_loaded[s], 16)

            def load_units(a, b):
                while a < b and (a % RAW or a < RAW):
                    load(a, a < RAW)
                    a += 1
                turns = (b - a) // RAW
                if turns > 1:
                    with sp.Fori(0, turns) as t:
                        for s in range(RAW):
                            u = t * RAW + (a + s)
                            sp.wait_ge(weight_lo, u - RAW + 1)
                            sp.dma_start(raw[:, s, :], weights[u]).then_inc(raw_loaded[s], 16)
                    a += turns * RAW
                while a < b:
                    load(a, False)
                    a += 1

            def load_chunks(n):
                at = DEC.index(n)
                if at >= 1:
                    sp.wait_ge(mixed, DEC[at - 1] + 1)
                if n == DEC[2]:
                    sp.wait_ge(k_roped, 1)
                    sp.wait_ge(q_roped, 1)
                c0 = chunk_of(n)
                for c in (c0, c0 + 1):
                    s = c % 2
                    kind, l, i = chunks[c]
                    if kind == "mem":
                        sp.dma_start(kv[:, s, 0, 0:1024], memK[l, i]).then_inc(kv_loaded[s], 16)
                        sp.dma_start(kv[:, s, 1, 0:1024], memV[l, i]).then_inc(kv_loaded[s], 16)
                    else:
                        for g in range(PAGES):
                            page = sp.value_load(pg[0:1, PAGES * i + g:PAGES * i + g + 1], min_val=0,
                                                 max_val=cacheK.shape[0] - 1)
                            sp.dma_start(kv[:, s, 0, g * 768:(g + 1) * 768], cacheK[page]).then_inc(kv_loaded[s], 16)
                            sp.dma_start(kv[:, s, 1, g * 768:(g + 1) * 768], cacheV[page]).then_inc(kv_loaded[s], 16)

            sp.dma_start(memX[:, :, :], memT).then_inc(memx_loaded, 16)
            sp.dma_start(par[:, :], params).then_inc(par_loaded, 16)
            load_units(0, 2)
            sp.dma_start(X[:, :, :], xT).then_inc(x_loaded, 16)
            load_units(2, 4)
            sp.dma_start(con[:, :], consts).then_inc(con_loaded, 16)
            sp.dma_start(pg[:, :], pages).then_inc(pg_loaded, 16)
            load_units(4, 12)
            sp.dma_start(histb[:, :, :, :], hist).then_inc(hist_loaded, 16)
            sp.wait_ge(norm_lo, KT)
            sp.wait_ge(sq_ready, KT)
            load_chunks(DEC[0])
            load_units(12, 16)
            load_chunks(DEC[1])
            load_units(16, U_OUT0)
            load_units(U_OUT0, U_IN1)
            sp.wait_ge(mixed, DEC[1] + 1)
            sp.dma_start(rope[:, :, :], ropes).then_inc(rope_loaded, 16)
            load_units(U_IN1, U_OUT1 + HL)
            sp.wait_ge(pg_loaded, 16)
            load_chunks(DEC[2])
            load_chunks(DEC[3])
            for n in DEC[4:]:
                load_chunks(n)
            load_units(U_OUT1 + HL, N_UNITS)
            for k in range(KT):
                sp.wait_ge(y_ready, k + 1)
                sp.dma_start(o_y[:, k, :], Z[:, k, :]).then_inc(stored, 16)
            sp.wait_ge(stored, 16 * KT)

        @block.tensor
        def _(pe):
            def unit(u, j, act, kts=tuple(range(KT)), cols=TOK, ready=None, base_kt=0, first=False, mid=None):
                pe.wait_ge(weight_lo, u + 1)
                if not first:
                    pe.wait_ge(unit_out, u - PS + 1)
                n = cols // 2 if cols == TOK else cols
                for q, k in enumerate(kts):
                    if ready:
                        ready(k)
                    if mid and q == len(kts) // 2:
                        mid()
                    w = lambda r: split[:, j % HL, r, lo_of(k - base_kt)]
                    for wr, ar in ((0, 0), (0, 1), (1, 0)):
                        for hf in range(cols // n):
                            mm = pe.matmul(ps[:, 2 * (j % PS) + hf, 0:n], w(wr), act[:, ar, k, hf * n:(hf + 1) * n],
                                           start=(q == 0 and wr == 0 and ar == 0),
                                           stop=(q == len(kts) - 1 and wr == 1))
                mm.then_inc(unit_done, 1)

            def norm_sum(r, cols=TOK):
                pe.wait_ge(sq_summed, (KT - 1) * (r + 1))
                n = cols // 2 if cols == TOK else cols
                for hf in range(cols // n):
                    mm = pe.matmul(ps[:, 6 + hf, 0:n], ones[:, :], sq_sum[:, hf * n:(hf + 1) * n],
                                   start=True, stop=True)
                mm.then_inc(norm_mm, 1)

            def normed(g):
                return lambda k: pe.wait_ge(norm_lo, KT * g + k + 1)

            def project(u0, act, g, r=None):
                for j in range(KT):
                    unit(u0 + j, u0 + j, act, ready=normed(g) if j == 0 else None)
                    if j == 0 and r is not None:
                        norm_sum(r)

            def mlp(u0, h2, hidden, g, r, done):
                def block_(i, u, first):
                    for j in range(KT):
                        unit(u + j, u0 + j, h2, ready=normed(g) if first and j == 0 else None)
                        if first and j == 0:
                            norm_sum(r)
                    for j in range(KT):
                        ready = (lambda k: pe.wait_ge(hid_lo, i * KT + (done + k + 1))) if j == 0 else None
                        unit(u + (KT + j), u0 + j, hidden, ready=ready)

                block_(0, u0, True)
                with pe.Fori(1, BLOCKS) as i:
                    block_(i, i * (2 * KT) + u0, False)

            def scores(n):
                kind, a, i = ITEMS[n]
                l = int(n >= L0_ITEMS)
                sc = score_banks(n)
                if n >= slots(n):
                    pe.wait_ge(exped, n - slots(n) + 1)
                if kind == "mem":
                    for hh in range(2):
                        lane = slice(64 * hh, 64 * hh + 64)
                        if hh and l == 0:
                            pe.wait_ge(half_scored, QT * a + i + 1)
                        mm = pe.matmul(sc[:, hh, 0:MEM], Z[lane, 6 + a, i * P:(i + 1) * P],
                                       memKT[lane, l, a, :], start=True, stop=True)
                        if hh == 0 and l == 0:
                            mm.then_inc(half_scored, 1)
                elif kind == "memdec":
                    pe.wait_ge(qbdm_ready, l + 1)
                    for b in range(4):
                        c = chunk_of(n) + b // 2
                        kv_ready(pe, c)
                        for pr in range(MEM_PAIRS):
                            at = (b % 2) * 512 + pr * MEM
                            mm = pe.matmul(sc[32 * b:32 * b + 32, 0, 0:MEM], QbdM[:, 4 * a + b, pr, :],
                                           kv[:, c % 2, 0, at:at + MEM], start=(pr == 0), stop=(pr == 1))
                elif kind == "diff":
                    for j in range(2):
                        lane = slice(64 * j, 64 * j + 64)
                        mm = pe.matmul(sc[:, j, 0:(i + 1) * P], Z[lane, a, i * P:(i + 1) * P],
                                       Kt[lane, a, 0:(i + 1) * P], start=True, stop=True)
                else:
                    pe.wait_ge(qbd_ready, 1)
                    for o in range(2):
                        c = chunk_of(n) + o
                        kv_ready(pe, c)
                        keys = kv[:, c % 2, 0, :].rearrange("p (g h k) -> p h g k", g=PAGES, h=HEADS)
                        for h in range(HEADS):
                            pe.matmul(sc[64 * o:64 * o + 64, 0, 0:PAST].rearrange("p (g k) -> p g k", g=PAGES),
                                      Qbd[:, h, 2 * a + o, :], keys[:, h, :, :], start=(h == 0), stop=(h == 5))
                    for h in range(HEADS):
                        mm = pe.matmul(sc[:, 0, PAST:PAST + SAMPLE], Qbd[:, h, 2 * a:2 * a + 2, :],
                                       Kt[:, h, PROMPT:TOK], start=(h == 0), stop=(h == 5))
                mm.then_inc(scored, 1)

            def turn(n):
                kind, a, i = ITEMS[n]
                l = int(n >= L0_ITEMS)
                t0 = 6
                pr = Pr[l][n % slots(n)]
                pe.wait_ge(weighted, n + 1)
                if n >= 1:
                    pe.wait_ge(copied, n)
                if kind == "mem":
                    for kt in range(2):
                        for hh in range(2):
                            at = (2 * kt + hh) * P
                            mm = pe.transpose(ps[:, t0, at:at + P], pr[:, hh, lo_of(kt)], ident)
                elif kind == "memdec":
                    for kt in range(2):
                        mm = pe.transpose(ps[:, t0, lo_of(kt)], pr[:, 0, lo_of(kt)], ident)
                elif kind == "diff":
                    for kt in range(i + 1):
                        mm = pe.transpose(ps[:, t0, lo_of(kt)], pr[:, 0, lo_of(kt)], ident)
                else:
                    for kt in range(2):
                        pe.matmul(ps[:, t0, 2 * GROUP * kt:2 * GROUP * (kt + 1)], pr[:, 0, lo_of(kt)], C2[:, n % 2, :],
                                  start=True, stop=True)
                    mm = pe.matmul(ps[0:SAMPLE, t0, 4 * GROUP:6 * GROUP], pr[:, 0, PAST:PAST + SAMPLE], C2[:, n % 2, :],
                                   start=True, stop=True)
                mm.then_inc(turned, 1)

            def mix(n):
                kind, a, i = ITEMS[n]
                l = int(n >= L0_ITEMS)
                m0 = 7
                pt = PT[n % 2]
                pe.wait_ge(copied, n + 1)
                if n >= 1:
                    pe.wait_ge(drained, n)
                if kind == "mem":
                    for hh in range(2):
                        for kt in range(2):
                            mm = pe.matmul(ps[64 * hh:64 * hh + 64, m0, 0:P],
                                           memVt[:, l, kt, a * P + 64 * hh:a * P + 64 * hh + 64],
                                           pt[:, (2 * kt + hh) * P:(2 * kt + hh + 1) * P],
                                           start=(kt == 0), stop=(kt == 1))
                elif kind == "memdec":
                    for b in range(4):
                        c = chunk_of(n) + b // 2
                        for pr in range(MEM_PAIRS):
                            out = (pr * 4 + b) * 32
                            for kt in range(2):
                                at = (b % 2) * 512 + kt * MEM + pr * P
                                mm = pe.matmul(ps[:, m0, out:out + 32], kv[:, c % 2, 1, at:at + P],
                                               pt[:, kt * P + 32 * b:kt * P + 32 * b + 32],
                                               start=(kt == 0), stop=(kt == 1))
                elif kind == "diff":
                    for kt in range(i + 1):
                        mm = pe.matmul(ps[:, m0, 0:P], pt[:, lo_of(kt)], Vt[:, kt, a * P:(a + 1) * P],
                                       start=(kt == 0), stop=(kt == i))
                else:
                    for h in range(HEADS):
                        pe.matmul(ps[:, m0, 2 * GROUP * h:2 * GROUP * (h + 1)], Vn[:, h * P:(h + 1) * P],
                                  pt[0:SAMPLE, 4 * GROUP:6 * GROUP],
                                  start=True, stop=False)
                        for o in range(2):
                            c = chunk_of(n) + o
                            out = GROUP * (2 * h + o)
                            for kt in range(2):
                                mm = pe.matmul(ps[:, m0, out:out + GROUP],
                                               kv[:, c % 2, 1, kt * 768 + h * P:kt * 768 + (h + 1) * P],
                                               pt[:, GROUP * (2 * kt + o):GROUP * (2 * kt + o + 1)],
                                               start=False, stop=(o == 1 and kt == 1))
                mm.then_inc(mixed, 1)

            def attention(n0, n1):
                scores(n0)
                scores(n0 + 1)
                for n in range(n0, n1):
                    if n + 2 < n1:
                        scores(n + 2)
                    turn(n)
                    if n > n0:
                        mix(n - 1)
                mix(n1 - 1)

            def cat_ready(k):
                if k >= 6:
                    pe.wait_ge(cat_lo, 1)
                else:
                    pe.wait_ge(unit_out, U_POOL + POOL_OUT.index(k) + 1)

            pe.wait_ge(const_ready, 1)
            for u in range(8):
                unit(u, u, A, cols=MEM, ready=normed(G_MEM) if u == 0 else None, first=u < PS)
                if u == 0:
                    norm_sum(R_MEM, MEM)
            pe.wait_ge(con_loaded, 16)
            def start():
                scores(0)
                scores(1)

            def step(n):
                turn(n)
                if n + 2 < L0_ITEMS:
                    scores(n + 2)
                if n:
                    mix(n - 1)

            for j in range(KT):
                mid = start if j == 2 else (lambda: step(2 * (j - 3))) if j >= 3 else None
                unit(U_IN0 + j, j, B, ready=normed(G_IN0) if j == 0 else None, mid=mid)
                if j == 0:
                    pe.wait_ge(root_ready, 1)
                    norm_sum(R_IN0)
                if j == 1:
                    pe.wait_ge(root_ready, 2)
                    for m in range(4):
                        for kt in range(2):
                            mm = pe.transpose(ps[:, 6 + m // 2, (kt * 2 + m % 2) * P:(kt * 2 + m % 2 + 1) * P],
                                              T[:, m, lo_of(kt)], ident)
                    mm.then_inc(memv_turned, 1)
                if j == 2:
                    pe.wait_ge(memv_ready, 2)
                if j >= 3:
                    step(2 * (j - 3) + 1)
            mix(L0_ITEMS - 1)
            for j, o in enumerate(POOL_OUT):
                pair = o // 3
                kts = [3 * pair + k for k in ((0, 1), (0, 1, 2), (1, 2))[o % 3]]
                pe.wait_ge(mix_lo, 3 * (j // 3) + 3)
                unit(U_POOL + j, j, A, kts=kts, base_kt=3 * pair)
            for j in range(KT):
                unit(U_OUT0 + j, j, B, kts=(6, 7, *POOL_OUT), ready=cat_ready if j == 0 else None)
            mlp(U_MLP0, A, B, G_MLP0, R_MLP0, 0)
            project(U_IN1, A, G_IN1, R_IN1)
            for j in range(MIXT):
                unit(U_K + j, j, B, ready=normed(G_KV) if j == 0 else None)
            for j in range(MIXT + 1):
                if j < MIXT:
                    unit(U_V + j, j, B)
                if j >= 1:
                    h = j - 1
                    pe.wait_ge(unit_out, U_V + h + 1)
                    if h == 0:
                        pe.wait_ge(root_ready, R_IN1 + 1)
                    if h >= 2:
                        pe.wait_ge(v_ready, h - 1)
                    for t in range(QT):
                        pe.transpose(ps[:, 4 + 2 * (h % 2), lo_of(t)], T[:, h % TS, lo_of(t)], ident)
                    pe.transpose(ps[0:SAMPLE, 5 + 2 * (h % 2), 0:P], T[:, h % TS, PROMPT:TOK], ident)\
                        .then_inc(v_turned, 1)
            pe.wait_ge(unit_out, U_OUT1)
            pe.wait_ge(v_ready, MIXT)
            pe.wait_ge(q_roped, 1)
            pe.wait_ge(k_roped, 1)
            attention(L0_ITEMS, len(ITEMS))
            pe.wait_ge(drained, len(ITEMS))
            pe.wait_ge(squared, QT * HEADS + 1)
            pe.matmul(ps[:, 6, 0:NS], ones[:, :], SQ[:, 0, 0:NS], start=True, stop=True)
            pe.matmul(ps[:, 7, 0:NS], ones[:, :], SQ[:, 1, 0:NS], start=True, stop=True).then_inc(sub_mm, 1)
            for h in range(HEADS):
                pe.wait_ge(sub_scaled, h + 1)
                for i in range(QT):
                    mm = pe.transpose(ps[:, h, lo_of(i)], O[:, QT * h + i, :], ident)
                mm.then_inc(sub_turned, 1)
            pe.wait_ge(cat_lo, 2)
            pe.wait_ge(mix_lo, MIXT + 7)
            for j in range(KT):
                unit(U_OUT1 + j, j, A)
            mlp(U_MLP1, B, A, G_MLP1, R_MLP1, BLOCKS * KT)
            norm_sum(R_FINAL)

        @block.scalar
        def _(act):
            own = Order(act, act_order)

            def weight_high(u, s, turn_value, first=False):
                act.wait_ge(raw_loaded[s], turn_value)
                if not first:
                    act.wait_ge(unit_done, u - HL + 1)
                n = unit_cols(u)
                act.activation(split[:, s % HL, 0, 0:n], raw[:, s, 0:n], ACT.Copy).then_inc(weight_hi, 1)

            def high(u):
                if u < N_UNITS:
                    weight_high(u, u % RAW, 16 * (u // RAW + 1), u < HL)

            def norm_high(g, k, src, dst):
                act.activation(dst, src, ACT.Copy, scale=gain(g, k)).then_inc(norm_hi, 1)

            def square(r, k, src, cols):
                if k >= 2 or r:
                    act.wait_ge(sq_summed, (KT - 1) * r + (max(k - 2, 1) if k >= 2 else 0))
                act.activation(SQ[:, k % 2, 0:cols], src, ACT.Square).then_inc(sq_ready, 1)

            def root(r, cols=TOK):
                act.wait_ge(norm_mm, r + 1)
                if r == R_MEM:
                    act.activation(rms_mem[:, :], ps[:, 6, 0:MEM], ACT.Sqrt, bias=epsc, scale=1.0 / D)\
                        .then_inc(root_ready, 1)
                else:
                    act.activation(halves(rms[:, :]), ps[:, 6:8, 0:HALF], ACT.Sqrt, bias=epsc, scale=1.0 / D)\
                        .then_inc(root_ready, 1)

            def residual_tile(u, o, r, gs):
                act.wait_ge(unit_out, u + 1)
                for g, dst in gs:
                    norm_high(g, o, X[:, o, :], dst[:, 0, o, :])
                square(r, o, X[:, o, :], TOK)

            def mlp(u0, hidden, r, nr, gs):
                def turn(i, j):
                    return i * 64 + 16 * ((u0 + j + HL) // RAW + 1)

                for j in range(KT):
                    weight_high(u0 + j + HL, (u0 + j + HL) % RAW, turn(0, j))
                    if j == 0:
                        root(r)
                    act.wait_ge(unit_out, u0 + j + 1)
                    act.activation(hidden[:, 0, j, :], T[:, j % TS, :], ACT.Square).then_inc(hid_hi, 1)
                with act.Fori(0, BLOCKS - 1) as i:
                    u = i * (2 * KT) + u0
                    for j in range(KT, 2 * KT):
                        weight_high(u + (j + HL), (u0 + j + HL) % RAW, turn(i, j))
                    for j in range(KT):
                        act.wait_ge(unit_out, u + (2 * KT + j + 1))
                        act.activation(hidden[:, 0, j, :], T[:, j % TS, :], ACT.Square).then_inc(hid_hi, 1)
                        weight_high(u + (2 * KT + j + HL), (u0 + j + HL) % RAW, turn(i, 2 * KT + j))
                u = u0 + (BLOCKS - 1) * 2 * KT
                for j in range(KT):
                    residual_tile(u + KT + j, j, nr, gs)
                    high(u + KT + j + HL)

            def items_exp(n):
                kind, a, i = ITEMS[n]
                l = int(n >= L0_ITEMS)
                act.wait_ge(biased, n + 1)
                if n >= slots(n):
                    act.wait_ge(turned, n - slots(n) + 1)
                s, pr, sc = n % SLOTS, Pr[l][n % slots(n)], score_banks(n)
                n_keys = {"mem": MEM, "memdec": MEM, "diff": (i + 1) * P, "decode": PAST + SAMPLE}[kind]
                for j in range(1 if kind in ("memdec", "decode") else 2):
                    ins = act.activation(pr[:, j, 0:n_keys], sc[:, j, 0:n_keys], ACT.Exp,
                                         bias=nb[:, s, j:j + 1], scale=SCALE, accum_out=sums[:, s, j:j + 1])
                ins.then_inc(exped, 1)

            def items_copy(n):
                kind, a, i = ITEMS[n]
                act.wait_ge(turned, n + 1)
                if n >= 2:
                    act.wait_ge(mixed, n - 1)
                t0 = 6
                cols = {"mem": 512, "memdec": 256, "diff": (i + 1) * P, "decode": 4 * GROUP}[kind]
                if kind == "decode":
                    own.step(act.activation(PT[n % 2][0:SAMPLE, 4 * GROUP:6 * GROUP], ps[0:SAMPLE, t0, 4 * GROUP:6 * GROUP], ACT.Copy))
                act.activation(PT[n % 2][:, 0:cols], ps[:, t0, 0:cols], ACT.Copy).then_inc(copied, 1)

            def items_square(n):
                kind, a, i = ITEMS[n]
                if kind == "diff":
                    k = QT * a + i
                    act.wait_ge(clamped, k + 1)
                    if k:
                        act.wait_ge(squared, k)
                    own.step(act.activation(SQ[:, 1, 0:P], SQ[:, 0, k % 2 * P:k % 2 * P + P], ACT.Square,
                                            accum_out=ss[:, k:k + 1]))
                    act.activation(SQ[:, 1, P:2 * P], O[:, k, :], ACT.Square, scale=BIG,
                                   accum_out=ss_big[:, k:k + 1]).then_inc(squared, 1)

            def attention(n0, n1):
                items_exp(n0)
                for n in range(n0, n1 + 3):
                    if n + 1 < n1:
                        items_exp(n + 1)
                    if n < n1:
                        items_copy(n)
                    if n0 <= n - 3:
                        items_square(n - 3)

            act.wait_ge(const_ready, 1)
            act.wait_ge(memx_loaded, 16)
            act.wait_ge(par_loaded, 16)
            high(0)
            for k in range(KT):
                norm_high(G_MEM, k, memX[:, k, :], A[:, 0, k, 0:MEM])
                square(R_MEM, k, memX[:, k, :], MEM)
            high(1)
            act.wait_ge(x_loaded, 16)
            for k in range(KT):
                norm_high(G_IN0, k, X[:, k, :], B[:, 0, k, :])
                if k == 1:
                    root(R_MEM)
                square(R_IN0, k, X[:, k, :], TOK)
            for u in range(8):
                high(u + HL)
            act.wait_ge(lam_dot, 1)
            act.activation(lamw[:, 2:4], lamw[:, 0:2], ACT.Exp).then_inc(lam_exp, 1)
            def step(n):
                if n + 1 < L0_ITEMS:
                    items_exp(n + 1)
                items_copy(n)

            def pool_line(q):
                if q == 0:
                    act.wait_ge(hist_loaded, 16)
                if q >= 2:
                    act.wait_ge(pooled, q - 1)
                o = POOL_TILES[q]
                ln = line[:, q % 2, :]
                reqs = ln[:, 16 + PROMPT:EXT].rearrange("p (b t) -> p b t", b=REQS)
                act.wait_ge(unit_out, U_IN0 + q + 3)
                act.activation(ln[:, 16:16 + PROMPT], Z[:, o, 0:PROMPT], ACT.Copy).then_inc(line_ready, 1)
                act.activation(reqs[:, :, 0:HIST], histb[:, o, :, :], ACT.Copy).then_inc(line_ready, 1)
                act.activation(reqs[:, :, HIST:HIST + STEPS],
                               Z[:, o, PROMPT:TOK].rearrange("p (b t) -> p b t", b=REQS), ACT.Copy)\
                   .then_inc(line_ready, 1)

            def pool_high(q):
                act.wait_ge(pooled, q + 1)
                act.activation(A[:, 0, POOL_TILES[q], :], T[:, 2 + q % 2, :], ACT.Copy).then_inc(mix_hi, 1)

            for j in range(KT):
                if j == 2:
                    items_exp(0)
                if j >= 3:
                    step(2 * (j - 3))
                high(U_IN0 + j + HL)
                if j == 0:
                    root(R_IN0)
                if j == 1:
                    act.wait_ge(memv_turned, 1)
                    for l in range(2):
                        act.activation(memVt[:, l, :, :], ps[:, 6 + l, :].rearrange("p (k f) -> p k f", k=2), ACT.Copy)\
                           .then_inc(memv_ready, 1)
                if j >= 3:
                    step(2 * (j - 3) + 1)
                if j >= 5:
                    pool_high(j - 5)
                if j >= 2:
                    pool_line(j - 2)
            pool_high(3)
            act.wait_ge(drained, L0_ITEMS)
            act.activation(B[:, 0, 6:8, :], Z[:, 6:8, :], ACT.Copy).then_inc(cat_hi, 1)
            pool_high(4)
            pool_high(5)
            for j, o in enumerate(POOL_OUT):
                act.wait_ge(unit_done, U_POOL + j + 1)
                act.activation(halves(B[:, 0, o, :]), unit_psum(j), ACT.Copy,
                               scale=par[:, C_PSCALE + o:C_PSCALE + o + 1]).then_inc(mix_hi, 1)
                high(U_POOL + j + HL)
            for j in range(KT):
                residual_tile(U_OUT0 + j, j, R_MLP0, [(G_MLP0, A)])
                high(U_OUT0 + j + HL)
            mlp(U_MLP0, B, R_MLP0, R_IN1, [(G_IN1, A)])
            act.wait_ge(unit_done, U_IN1)
            for k in range(KT):
                norm_high(G_KV, k, X[:, k, :], B[:, 0, k, :])
            for j in range(KT):
                high(U_IN1 + j + HL)
                if j == 0:
                    root(R_IN1)
            for j in range(MIXT):
                high(U_K + j + HL)
            for j in range(MIXT + 1):
                if j < MIXT:
                    high(U_V + j + HL)
                if j >= 1:
                    h = j - 1
                    act.wait_ge(v_turned, h + 1)
                    own.step(act.activation(Vt[:, :, h * P:(h + 1) * P],
                                            ps[:, 4 + 2 * (h % 2), :].rearrange("p (t e) -> p t e", t=QT), ACT.Copy))
                    act.activation(Vn[:, h * P:(h + 1) * P], ps[0:SAMPLE, 5 + 2 * (h % 2), 0:P], ACT.Copy)\
                       .then_inc(v_ready, 1)
            attention(L0_ITEMS, len(ITEMS))
            act.wait_ge(sub_mean, 1)
            act.wait_ge(squared, QT * HEADS)
            own.step(act.activation(SQ[:, 0, 0:NS], small[0], ACT.Square))
            act.activation(SQ[:, 1, 0:NS].rearrange("p (h t) -> p h t", h=MIXT), Z[:, 0:MIXT, PROMPT:TOK], ACT.Square,
                           scale=BIG).then_inc(squared, 1)
            act.wait_ge(v_stored, 32)
            act.activation(A[:, 0, 6:8, :], Z[:, 6:8, :], ACT.Copy).then_inc(cat_hi, 1)
            act.wait_ge(sub_mean, 2)
            act.activation(rr[:, :], ss[:, :], ACT.Sqrt, bias=eps_sub, scale=SUB).then_inc(sub_root, 1)
            act.wait_ge(sub_mean, 3)
            act.activation(small[0], small[1], ACT.Sqrt, bias=eps_sub, scale=SUB).then_inc(sub_root, 1)
            for h in range(HEADS):
                act.wait_ge(sub_turned, h + 1)
                act.activation(A[:, 0, h, 0:PROMPT], ps[:, h, :], ACT.Copy, scale=gsub).then_inc(mix_hi, 1)
            act.wait_ge(sub_sample, 1)
            act.activation(A[:, 0, 0:MIXT, PROMPT:TOK], Z[:, 0:MIXT, PROMPT:TOK], ACT.Copy, scale=gsub)\
               .then_inc(mix_hi, 1)
            for j in range(KT):
                residual_tile(U_OUT1 + j, j, R_MLP1, [(G_MLP1, B)])
                high(U_OUT1 + j + HL)
            mlp(U_MLP1, A, R_MLP1, R_FINAL, [])
            root(R_FINAL)

        @block.vector
        def _(dve):
            own = Order(dve, dve_order)

            def weight_rest(u, s, first=False):
                dve.wait_ge(weight_hi, u + 1)
                n = unit_cols(u)
                dve.tensor_tensor(split[:, s % HL, 1, 0:n], raw[:, s, 0:n], split[:, s % HL, 0, 0:n].bitcast(F32),
                                  ALU.subtract).then_inc(weight_lo, 1)

            def rest(u):
                if u < N_UNITS:
                    weight_rest(u, u % RAW)

            def norm_rest(g, k, src, dst):
                dve.wait_ge(norm_hi, KT * g + k + 1)
                dve.scalar_tensor_tensor(out=dst[1], in0=src, scalar=gain(g, k), in1=dst[0].bitcast(F32),
                                         op0=ALU.mult, op1=ALU.subtract).then_inc(norm_lo, 1)

            def pair_of(op, k, cols=TOK):
                return op[:, 0, k, 0:cols], op[:, 1, k, 0:cols]

            def inverse(r):
                dve.wait_ge(root_ready, r + 1)
                t = rms_mem[:, :] if r == R_MEM else rms[:, :]
                dve.reciprocal(t, t).then_inc(rms_ready, 1)

            def add_residual(u, j, o):
                dve.wait_ge(unit_done, u + 1)
                dve.tensor_tensor(halves(X[:, o, :]), unit_psum(j), halves(X[:, o, :]), ALU.add).then_inc(unit_out, 1)

            def out_units(u0, g, dst):
                for j in range(KT):
                    add_residual(u0 + j, u0 + j, j)
                    norm_rest(g, j, X[:, j, :], pair_of(dst, j))
                    rest(u0 + j + HL)

            def mlp(u0, r, g, dst):
                def hidden(u, j, n):
                    dve.wait_ge(unit_done, u + 1)
                    dve.wait_ge(hid_lo, n)
                    dve.scalar_tensor_tensor(out=halves(T[:, j % TS, :]), in0=unit_psum(j), scalar=0.0,
                                             in1=halves(rms[:, :]), op0=ALU.max, op1=ALU.mult).then_inc(unit_out, 1)

                n0 = BLOCKS * KT * (u0 == U_MLP1)
                inverse(r)
                dve.wait_ge(rms_ready, r + 1)
                for j in range(KT):
                    if j < TS:
                        dve.wait_ge(unit_done, u0 + j + 1)
                        dve.scalar_tensor_tensor(out=halves(T[:, j % TS, :]), in0=unit_psum(j), scalar=0.0,
                                                 in1=halves(rms[:, :]), op0=ALU.max, op1=ALU.mult).then_inc(unit_out, 1)
                    else:
                        hidden(u0 + j, j, n0 + j - TS + 1)
                    weight_rest(u0 + j + HL, (u0 + j + HL) % RAW)
                with dve.Fori(0, BLOCKS - 1) as i:
                    u = i * (2 * KT) + u0
                    for j in range(KT):
                        dve.wait_ge(unit_done, u + (KT + j + 1))
                        dve.wait_ge(unit_out, u + (j + 1 - KT))
                        dve.tensor_tensor(halves(X[:, j, :]), unit_psum(j), halves(X[:, j, :]), ALU.add)\
                           .then_inc(unit_out, 1)
                        weight_rest(u + (KT + j + HL), (u0 + KT + j + HL) % RAW)
                    for j in range(KT):
                        hidden(u + (2 * KT + j), j, i * KT + (n0 + KT + j - TS + 1))
                        weight_rest(u + (2 * KT + j + HL), (u0 + j + HL) % RAW)
                u = u0 + (BLOCKS - 1) * 2 * KT
                for j in range(KT):
                    dve.wait_ge(unit_out, u + j + 1 - KT)
                    add_residual(u + KT + j, j, j)
                    if g is not None:
                        norm_rest(g, j, X[:, j, :], pair_of(dst, j))
                    rest(u + KT + j + HL)

            def items_weight(n, between=None):
                kind, a, i = ITEMS[n]
                s, pr = n % SLOTS, Pr[int(n >= L0_ITEMS)][n % slots(n)]
                nj = 1 if kind in ("memdec", "decode") else 2
                dve.wait_ge(exped, n + 1)
                own.step(dve.reciprocal(coef[:, s, 0:nj], sums[:, s, 0:nj]))
                if between:
                    between()
                own.settle()
                if kind == "mem":
                    for j in range(2):
                        ins = dve.tensor_scalar(pr[:, j, 0:MEM], pr[:, j, 0:MEM], coef[:, s, j:j + 1], None, ALU.mult)
                elif kind == "memdec":
                    ins = dve.tensor_scalar(pr[:, 0, 0:MEM], pr[:, 0, 0:MEM], coef[:, s, 0:1], None, ALU.mult)
                elif kind == "diff":
                    k = (i + 1) * P
                    own.chain(dve.tensor_scalar(ratio[:, s:s + 1], sums[:, s, 0:1], coef[:, s, 1:2], lam_n,
                                                ALU.mult, ALU.mult))
                    ins = dve.scalar_tensor_tensor(out=pr[:, 0, 0:k], in0=pr[:, 1, 0:k], scalar=ratio[:, s:s + 1],
                                                   in1=pr[:, 0, 0:k], op0=ALU.mult, op1=ALU.add)
                else:
                    own.chain(dve.tensor_scalar(coef[:, s, 1:2], coef[:, s, 0:1], sgn, None, ALU.mult))
                    ins = dve.tensor_scalar(C2[:, n % 2, :], con[:, K_SEL:K_SEL + 2 * GROUP], coef[:, s, 1:2], None, ALU.mult)
                ins.then_inc(weighted, 1)

            def items_bias(n):
                kind, a, i = ITEMS[n]
                s, sc = n % SLOTS, score_banks(n)
                dve.wait_ge(scored, n + 1)
                if kind == "diff":
                    at = sc[:, :, i * P:(i + 1) * P]
                    own.chain(dve.tensor_tensor(at, at, causal.unsqueeze(1).to_broadcast([P, 2, P]), ALU.add))
                if kind == "decode":
                    at = sc[:, 0, PAST:PAST + SAMPLE]
                    m = K_DMASK + a * SAMPLE
                    own.chain(dve.tensor_tensor(at, at, con[:, m:m + SAMPLE], ALU.add))
                n_keys = {"mem": MEM, "memdec": MEM, "diff": (i + 1) * P, "decode": PAST + SAMPLE}[kind]
                if kind in ("mem", "diff"):
                    own.chain(dve.tensor_reduce(mx[:, s, :], sc[:, :, 0:n_keys], AX.X, ALU.max))
                else:
                    own.chain(dve.tensor_reduce(mx[:, s, 0:1], sc[:, 0, 0:n_keys], AX.X, ALU.max))
                if kind == "diff":
                    ins = dve.scalar_tensor_tensor(out=nb[:, s, :], in0=mx[:, s, :], scalar=-SCALE, in1=exp_shift,
                                                   op0=ALU.mult, op1=ALU.add)
                else:
                    nj = 2 if kind == "mem" else 1
                    ins = dve.tensor_scalar(nb[:, s, 0:nj], mx[:, s, 0:nj], -SCALE, None, ALU.mult)
                ins.then_inc(biased, 1)

            def items_drain(n):
                kind, a, i = ITEMS[n]
                dve.wait_ge(mixed, n + 1)
                if kind == "mem":
                    ins = dve.tensor_copy(Z[:, 6 + a, i * P:(i + 1) * P], ps[:, 7, 0:P])
                elif kind == "memdec":
                    for hh in range(2):
                        lane = slice(64 * hh, 64 * hh + 64)
                        for pr in range(MEM_PAIRS):
                            grid = ps[lane, 7, P * pr:P * pr + P].rearrange("p (b c) -> p b c", b=4)
                            src = grid[:, :, 8 * pr + 4 * hh:8 * pr + 4 * hh + 4]
                            dst = Z[lane, 6 + pr, PROMPT + 16 * a:PROMPT + 16 * a + 16].rearrange("p (b t) -> p b t", b=4)
                            ins = dve.tensor_copy(dst, src)
                elif kind == "diff":
                    s = n % SLOTS
                    ins = dve.tensor_scalar(O[:, QT * a + i, :], ps[:, 7, 0:P], coef[:, s, 0:1], None, ALU.mult)
                else:
                    for h in range(HEADS):
                        src = ps[:, 7, 2 * GROUP * h:2 * GROUP * (h + 1)].rearrange("p (o c) -> p o c", o=2)[:, :, 4 * h:4 * h + 4]
                        dst = Z[:, h, PROMPT + 8 * a:PROMPT + 8 * a + 8].rearrange("p (o t) -> p o t", o=2)
                        ins = dve.tensor_copy(dst, src)
                ins.then_inc(drained, 1)

            def attention(n0, n1):
                items_bias(n0)
                items_bias(n0 + 1)
                for n in range(n0, n1 + 2):
                    drain = (lambda: items_drain(n - 2)) if n - 2 >= n0 else None
                    if n < n1:
                        items_weight(n, drain)
                    else:
                        drain()
                    if n + 2 < n1:
                        items_bias(n + 2)

            def pool_rest(q):
                dve.wait_ge(mix_hi, q + 1)
                o = POOL_TILES[q]
                dve.tensor_tensor(A[:, 1, o, :], T[:, 2 + q % 2, :], A[:, 0, o, :].bitcast(F32),
                                  ALU.subtract).then_inc(mix_lo, 1)

            def pool_mean(q):
                dve.wait_ge(window_ready, q + 1)
                if q >= 2:
                    dve.wait_ge(mix_lo, q - 1)
                o = POOL_TILES[q]
                ln, wd, t = line[:, q % 2, :], window[:, q % 2, :], T[:, 2 + q % 2, :]
                inv = con[:, K_INVW + o:K_INVW + o + 1]
                own.step(dve.scalar_tensor_tensor(out=t[:, 16:PROMPT], in0=wd[:, 32:16 + PROMPT], scalar=inv,
                                                  in1=ln[:, 32:16 + PROMPT], op0=ALU.mult, op1=ALU.subtract))
                sample = lambda v: v[:, 16 + PROMPT:EXT].rearrange("p (b t) -> p b t", b=REQS)[:, :, HIST:HIST + STEPS]
                own.step(dve.scalar_tensor_tensor(out=t[:, PROMPT:TOK].rearrange("p (b t) -> p b t", b=REQS),
                                                  in0=sample(wd), scalar=inv, in1=sample(ln), op0=ALU.mult,
                                                  op1=ALU.subtract))
                own.chain(dve.tensor_tensor(t[:, 0:16], wd[:, 16:32], con[:, K_TAB + 16 * o:K_TAB + 16 * o + 16],
                                            ALU.mult))
                dve.tensor_tensor(t[:, 0:16], t[:, 0:16], ln[:, 16:32], ALU.subtract).then_inc(pooled, 1)

            rest(0)
            dve.wait_ge(memx_loaded, 16)
            dve.wait_ge(par_loaded, 16)
            for k in range(KT):
                norm_rest(G_MEM, k, memX[:, k, :], pair_of(A, k, MEM))
            rest(1)
            lam = par[:, C_LAM:C_LAM + 256].rearrange("p (v d) -> p v d", v=4)
            own.chain(dve.tensor_tensor(T[:, 0, 0:64], lam[:, 0, :], lam[:, 1, :], ALU.mult))
            own.chain(dve.tensor_tensor(T[:, 0, 64:128], lam[:, 2, :], lam[:, 3, :], ALU.mult))
            dve.tensor_reduce(lamw[:, 0:2], T[:, 0, 0:128].rearrange("p (v d) -> p v d", v=2), AX.X, ALU.add)\
               .then_inc(lam_dot, 1)
            dve.wait_ge(x_loaded, 16)
            for k in range(2):
                norm_rest(G_IN0, k, X[:, k, :], pair_of(B, k))
            inverse(R_MEM)
            for k in range(2, KT):
                norm_rest(G_IN0, k, X[:, k, :], pair_of(B, k))
            dve.wait_ge(rms_ready, 1)
            for u in range(8):
                dve.wait_ge(unit_done, u + 1)
                dst = memKT[:, u // 2, u % 2, :] if u < 4 else T[:, u - 4, 0:MEM]
                if u == 4:
                    dve.wait_ge(lam_dot, 1)
                dve.tensor_tensor(dst, ps[:, 2 * (u % PS), 0:MEM], rms_mem[:, :], ALU.mult).then_inc(unit_out, 1)
                rest(u + HL)
            inverse(R_IN0)
            dve.wait_ge(lam_exp, 1)
            dve.wait_ge(rms_ready, 2)
            own.chain(dve.tensor_tensor(lamw[:, 4:5], lamw[:, 2:3], lamw[:, 3:4], ALU.subtract))
            own.step(dve.tensor_scalar(gsub, par[:, C_SUBLN:C_SUBLN + 1], 1.0 - LAM_INIT, None, ALU.mult))
            own.chain(dve.tensor_scalar(lam_n, lamw[:, 4:5], LAM_INIT, -1.0, ALU.add, ALU.mult))
            dve.wait_ge(con_loaded, 16)
            own.chain(dve.tensor_scalar(sgn, con[:, K_ROWJ + 1:K_ROWJ + 2], lam_n, None, ALU.mult))
            own.chain(dve.tensor_tensor(sgn, sgn, con[:, K_ROWJ:K_ROWJ + 1], ALU.add))
            def step(n):
                if n + 1 < L0_ITEMS:
                    items_weight(n + 1)
                if n + 2 < L0_ITEMS:
                    items_bias(n + 2)
                if n:
                    items_drain(n - 1)

            for j in range(KT):
                if j == 2:
                    items_bias(0)
                    items_bias(1)
                    items_weight(0)
                if j >= 3:
                    step(2 * (j - 3))
                dve.wait_ge(unit_done, U_IN0 + j + 1)
                dve.tensor_tensor(halves(Z[:, IN_ORDER[0][j], :]), unit_psum(j), halves(rms[:, :]), ALU.mult)\
                   .then_inc(unit_out, 1)
                rest(U_IN0 + j + HL)
                if j >= 3:
                    step(2 * (j - 3) + 1)
                if j >= 6:
                    pool_rest(j - 6)
                if j >= 4:
                    pool_mean(j - 4)
            items_drain(L0_ITEMS - 1)
            pool_rest(2)
            dve.wait_ge(cat_hi, 1)
            dve.tensor_tensor(B[:, 1, 6:8, :], Z[:, 6:8, :], B[:, 0, 6:8, :].bitcast(F32), ALU.subtract)\
               .then_inc(cat_lo, 1)
            pool_rest(3)
            pool_mean(4)
            pool_mean(5)
            pool_rest(4)
            pool_rest(5)
            for j, o in enumerate(POOL_OUT):
                dve.wait_ge(mix_hi, MIXT + j + 1)
                dve.scalar_tensor_tensor(out=halves(B[:, 1, o, :]), in0=unit_psum(j),
                                         scalar=par[:, C_PSCALE + o:C_PSCALE + o + 1],
                                         in1=halves(B[:, 0, o, :].bitcast(F32)), op0=ALU.mult, op1=ALU.subtract)\
                   .then_inc(unit_out, 1)
                rest(U_POOL + j + HL)
            out_units(U_OUT0, G_MLP0, A)
            mlp(U_MLP0, R_MLP0, G_IN1, A)
            for k in range(KT):
                norm_rest(G_KV, k, X[:, k, :], pair_of(B, k))
            inverse(R_IN1)
            dve.wait_ge(rms_ready, R_IN1 + 1)
            dve.wait_ge(pool_stored, 16)
            for j in range(KT):
                dve.wait_ge(unit_done, U_IN1 + j + 1)
                dve.tensor_tensor(halves(Z[:, IN_ORDER[1][j], :]), unit_psum(j), halves(rms[:, :]), ALU.mult)\
                   .then_inc(unit_out, 1)
                rest(U_IN1 + j + HL)
            for j in range(MIXT):
                dve.wait_ge(unit_done, U_K + j + 1)
                dve.tensor_tensor(halves(Kt[:, j, :]), unit_psum(j), halves(rms[:, :]), ALU.mult).then_inc(unit_out, 1)
                rest(U_K + j + HL)
            for j in range(MIXT):
                dve.wait_ge(unit_done, U_V + j + 1)
                if j >= TS:
                    dve.wait_ge(v_turned, j - TS + 1)
                dve.tensor_tensor(halves(T[:, j % TS, :]), unit_psum(j), halves(rms[:, :]), ALU.mult)\
                   .then_inc(unit_out, 1)
                rest(U_V + j + HL)
                if j == 0:
                    dve.wait_ge(k_swapped, 64)
                own.step(dve.tensor_tensor(swap[:, j, :], swap[:, j, :], rope[:, 1, :], ALU.mult))
                own.chain(dve.tensor_tensor(Kt[:, j, :], Kt[:, j, :], rope[:, 0, :], ALU.mult))
                ins = dve.tensor_tensor(Kt[:, j, :], Kt[:, j, :], swap[:, j, :], ALU.add)
                if j == MIXT - 1:
                    ins.then_inc(k_roped, 1)
            attention(L0_ITEMS, len(ITEMS))
            zs = Z[:, 0:MIXT, PROMPT:TOK]
            grid = lambda v: v.rearrange("p (h t) -> p h t", h=MIXT)
            dve.wait_ge(drained, len(ITEMS))
            dve.tensor_scalar(grid(small[0]), zs, CLAMP, -CLAMP, ALU.min, ALU.max).then_inc(sub_mean, 1)

            def means(total, total_big, mean, scratch, keep):
                own.step(dve.tensor_scalar(keep, total_big, BIG_END, SUB ** 0.5, ALU.is_lt, ALU.mult))
                own.step(dve.tensor_scalar(mean, total, 1.0 / P, None, ALU.mult))
                own.chain(dve.tensor_scalar(scratch, total_big, BIG_END, 2.0 ** 100, ALU.min, ALU.mult))
                dve.scalar_tensor_tensor(out=mean, in0=scratch, scalar=2.0 ** 36 / P, in1=mean, op0=ALU.mult,
                                         op1=ALU.max).then_inc(sub_mean, 1)

            dve.wait_ge(squared, QT * HEADS)
            means(ss[:, :], ss_big[:, :], ss[:, :], rr2[:, :], keep[:, :])
            dve.wait_ge(sub_mm, 1)
            means(ps[:, 6, 0:NS], ps[:, 7, 0:NS], small[1], small[2], small[3])
            dve.wait_ge(sub_root, 1)
            own.chain(dve.reciprocal(rr2[:, :], rr[:, :]))
            dve.tensor_tensor(rr2[:, :], rr2[:, :], keep[:, :], ALU.mult).then_inc(sub_rms, 1)
            dve.wait_ge(sub_rms, 1)
            for h in range(HEADS):
                for i in range(QT):
                    n = QT * h + i
                    ins = dve.tensor_scalar(O[:, n, :], O[:, n, :], rr2[:, n:n + 1], None, ALU.mult)
                ins.then_inc(sub_scaled, 1)
            dve.wait_ge(sub_root, 2)
            own.chain(dve.reciprocal(small[0], small[0]))
            own.chain(dve.tensor_tensor(small[0], small[0], small[3], ALU.mult))
            dve.tensor_tensor(zs, zs, grid(small[0]), ALU.mult).then_inc(sub_sample, 1)
            dve.wait_ge(cat_hi, 2)
            dve.tensor_tensor(A[:, 1, 6:8, :], Z[:, 6:8, :], A[:, 0, 6:8, :].bitcast(F32), ALU.subtract)\
               .then_inc(cat_lo, 1)
            for h in range(HEADS):
                dve.wait_ge(mix_hi, 2 * MIXT + h + 1)
                dve.scalar_tensor_tensor(out=A[:, 1, h, 0:PROMPT], in0=ps[:, h, :], scalar=gsub,
                                         in1=A[:, 0, h, 0:PROMPT].bitcast(F32), op0=ALU.mult, op1=ALU.subtract)\
                   .then_inc(mix_lo, 1)
            dve.wait_ge(mix_hi, 3 * MIXT + 1)
            dve.scalar_tensor_tensor(out=A[:, 1, 0:MIXT, PROMPT:TOK], in0=zs, scalar=gsub,
                                     in1=A[:, 0, 0:MIXT, PROMPT:TOK].bitcast(F32), op0=ALU.mult, op1=ALU.subtract)\
               .then_inc(mix_lo, 1)
            out_units(U_OUT1, G_MLP1, B)
            mlp(U_MLP1, R_MLP1, None, None)
            inverse(R_FINAL)
            dve.wait_ge(rms_ready, R_FINAL + 1)
            for k in range(KT):
                dve.scalar_tensor_tensor(out=Z[:, k, :], in0=X[:, k, :], scalar=gain(G_FINAL, k), in1=rms[:, :],
                                         op0=ALU.mult, op1=ALU.mult).then_inc(y_ready, 1)

        @block.gpsimd
        def _(pool):
            own = Order(pool, pool_order)

            def sum_squares(r, cols=TOK):
                if r:
                    pool.wait_ge(norm_mm, r)
                for k in range(1, KT):
                    pool.wait_ge(sq_ready, KT * r + k + 1)
                    if k >= 2:
                        pool.wait_ge(sq_summed, (KT - 1) * r + k - 1)
                    a = SQ[:, 0, 0:cols] if k == 1 else sq_sum[:, 0:cols]
                    pool.tensor_tensor(sq_sum[:, 0:cols], a, SQ[:, k % 2, 0:cols], ALU.add).then_inc(sq_summed, 1)

            def hidden_rest(hidden, j, n):
                pool.wait_ge(hid_hi, n)
                t = T[:, j % TS, :]
                sq = SQ[:, j % 2, :]
                pool.tensor_tensor(sq, t, t, ALU.mult).then_inc(hid_sq, 1)
                pool.wait_ge(hid_sq, n)
                pool.tensor_tensor(hidden[:, 1, j, :], sq, hidden[:, 0, j, :].bitcast(F32), ALU.subtract)\
                    .then_inc(hid_lo, 1)

            def mlp(u0, hidden, r):
                n0 = BLOCKS * KT * (u0 == U_MLP1)
                with pool.Fori(0, BLOCKS) as i:
                    for j in range(KT):
                        hidden_rest(hidden, j, i * KT + (n0 + j + 1))
                sum_squares(r)

            def rotate(swapped, done, dst):
                for q in range(4):
                    pool.dma_start(swap[32 * q:32 * q + 32, :, :], dst[32 * (q ^ 1):32 * (q ^ 1) + 32, 0:MIXT, :])\
                        .then_inc(swapped, 16)

            def query_blocks(layer):
                for hh in range(2):
                    lane = slice(64 * hh, 64 * hh + 64)
                    for pr in range(MEM_PAIRS):
                        c = 8 * pr + 4 * hh
                        ins = pool.tensor_copy(QbdM[lane, :, pr, c:c + STEPS],
                                               Z[lane, 6 + pr, PROMPT:TOK].rearrange("p (b t) -> p b t", b=REQS))
                        if (hh, pr) != (1, 1):
                            own.chain(ins)
                ins.then_inc(qbdm_ready, 1)
                pool.wait_ge(qbdm_ready, layer + 1)

            own.step(pool.memset(epsc, EPS))
            own.step(pool.memset(eps_sub, EPS * SUB))
            own.step(pool.memset(exp_shift[:, 0:1], -SHIFT))
            own.step(pool.memset(exp_shift[:, 1:2], 0.0))
            own.step(pool.memset(line[:, :, 0:16], 0.0))
            own.step(pool.memset(QbdM[:, :, :, :], 0.0))
            pool.memset(ones[:, :], 1.0).then_inc(const_ready, 1)
            sum_squares(R_MEM, MEM)
            sum_squares(R_IN0)
            pool.wait_ge(unit_out, 4)
            pool.dma_start(o_memk, memKT[:, :, :, :]).then_inc(memk_stored, 16)
            pool.wait_ge(unit_out, U_IN0 + 2)
            own.settle()
            query_blocks(0)
            pool.wait_ge(memv_ready, 2)
            pool.dma_start(o_memv, memVt[:, :, :, :]).then_inc(memv_stored, 16)
            for q, o in enumerate(POOL_TILES):
                pool.wait_ge(line_ready, 3 * (q + 1))
                if q >= 2:
                    pool.wait_ge(pooled, q - 1)
                ln, wd = line[:, q % 2, :], window[:, q % 2, :]
                lo_w, hi_w = WINDOWS[(2 * o) // 3], WINDOWS[(2 * o + 1) // 3]
                parts = [(0, P, lo_w)] if lo_w == hi_w else [(0, 64, lo_w), (64, P, hi_w)]
                for p0, p1, w in parts:
                    src, shift, n = ln, 1, 0
                    while shift < w:
                        last = 2 * shift == w
                        dst = wd if last else partial[:, n % 2, :]
                        t0 = 16 if last else 2 * shift - 1
                        if n:
                            own.settle()
                        own.step(pool.tensor_tensor(dst[p0:p1, t0:EXT], src[p0:p1, t0:EXT],
                                                    src[p0:p1, t0 - shift:EXT - shift], ALU.add))
                        src, shift, n = dst, 2 * shift, n + 1
                    own.settle()
                reqs = ln[:, 16 + PROMPT:EXT].rearrange("p (b t) -> p b t", b=REQS)
                pool.tensor_copy(histb[:, o, :, :], reqs[:, :, STEPS:STEPS + HIST]).then_inc(window_ready, 1)
            pool.wait_ge(unit_out, U_POOL)
            pool.dma_start(o_pool, Z[:, 0:MIXT, PROMPT - HIST:PROMPT]).then_inc(pool_stored, 16)
            pool.wait_ge(window_ready, MIXT)
            pool.dma_start(o_pools, histb[:, :, :, :]).then_inc(pools_stored, 16)
            sum_squares(R_MLP0)
            mlp(U_MLP0, B, R_IN1)
            pool.wait_ge(unit_out, U_IN1 + 2)
            query_blocks(1)
            pool.wait_ge(unit_out, U_K)
            rotate(q_swapped, None, Z)
            pool.wait_ge(q_swapped, 64)
            pool.wait_ge(rope_loaded, 16)
            for h in range(HEADS):
                own.step(pool.tensor_tensor(swap[:, h, :], swap[:, h, :], rope[:, 1, :], ALU.mult))
                own.chain(pool.tensor_tensor(Z[:, h, :], Z[:, h, :], rope[:, 0, :], ALU.mult))
                ins = pool.tensor_tensor(Z[:, h, :], Z[:, h, :], swap[:, h, :], ALU.add)
                if h < HEADS - 1:
                    own.step(ins)
            ins.then_inc(q_roped, 1)
            pool.wait_ge(q_roped, 1)
            pool.wait_ge(unit_out, U_V)
            rotate(k_swapped, None, Kt)
            pool.wait_ge(unit_done, U_OUT1)
            own.chain(pool.memset(Qbd[:, :, :, :], 0.0))
            for h in range(HEADS):
                for j in range(2):
                    lane = slice(64 * j, 64 * j + 64)
                    c = 8 * h + 4 * j
                    ins = pool.tensor_copy(Qbd[lane, h, :, c:c + STEPS],
                                           Z[lane, h, PROMPT:TOK].rearrange("p (b t) -> p b t", b=REQS))
                    if (h, j) != (HEADS - 1, 1):
                        own.chain(ins)
            ins.then_inc(qbd_ready, 1)
            pool.wait_ge(qbd_ready, 1)
            pool.wait_ge(v_ready, MIXT)
            pool.dma_start(o_v, Vt[:, :, :]).then_inc(v_stored, 16)
            pool.dma_start(o_vs, Vn[:, :]).then_inc(v_stored, 16)
            pool.wait_ge(k_roped, 1)
            pool.dma_start(o_k, Kt[:, :, :]).then_inc(k_stored, 16)
            for n, (kind, a, i) in enumerate(ITEMS):
                if kind == "diff":
                    k = QT * a + i
                    pool.wait_ge(drained, n + 1)
                    if k >= 2:
                        pool.wait_ge(squared, k - 1)
                    pool.tensor_scalar(SQ[:, 0, k % 2 * P:k % 2 * P + P], O[:, k, :], CLAMP, -CLAMP, ALU.min, ALU.max)\
                        .then_inc(clamped, 1)
            sum_squares(R_MLP1)
            mlp(U_MLP1, A, R_FINAL)
            for s, n in ((memk_stored, 16), (memv_stored, 16), (pool_stored, 16), (pools_stored, 16),
                         (v_stored, 32), (k_stored, 16)):
                pool.wait_ge(s, n)

    return nc


def _units(w):
    k, m = w.shape
    return w.reshape(k // P, P, m // P, P).transpose(2, 1, 0, 3).reshape(m // P, P, k)


def _lanes(v):
    return v.T.reshape(-1, P, v.shape[0]).transpose(1, 0, 2)


def _constants():
    c = np.zeros((P, K_CONST), np.float32)
    c[:, K_IDENT:K_IDENT + P] = np.eye(P)
    c[:, K_CAUSAL:K_CAUSAL + P] = np.where(np.arange(P)[None, :] > np.arange(P)[:, None], NEG, 0.0)
    for row in range(P):
        o, rest = divmod(row, 64)
        h, j, t = rest // 8, rest % 8 // 4, rest % 4
        if h >= HEADS:
            continue
        for a in range(4):
            for key in range(SAMPLE):
                if not (key // STEPS == 2 * a + o and key % STEPS <= t):
                    c[row, K_DMASK + a * SAMPLE + key] = NEG
        c[row, K_SEL + o * GROUP + h * 4 + t] = 1.0
        c[row, K_ROWJ + j] = 1.0
    for tile in range(MIXT):
        w = np.array([WINDOWS[(tile * P + p) // 192] for p in range(P)])
        c[:, K_INVW + tile] = 1.0 / w
        c[:, K_TAB + 16 * tile:K_TAB + 16 * tile + 16] = 1.0 / np.minimum(w[:, None], np.arange(16)[None, :] + 1)
    return c


def _angles():
    inv = (1.0 / (np.float32(10000.0) ** (np.arange(0, HD, 2, dtype=np.float32) / np.float32(HD)))).astype(np.float32)
    pos = np.concatenate([np.arange(PROMPT), np.tile(PAST + np.arange(STEPS), REQS)]).astype(np.float32)
    ang = (pos[None, :] * inv[np.arange(P) % 32][:, None]).astype(np.float32).astype(np.float64)
    sign = np.where(np.arange(P) % HD < 32, -1.0, 1.0)[:, None]
    return np.stack([np.cos(ang), sign * np.sin(ang)], axis=1).astype(np.float32)


def kernel(x_prompt, x_sample, state_pool, cache_mem_k, cache_mem_v, cache_k, cache_v, page_table, mem_prompt,
           norm1, norm2, final_norm, kv_norm, mem_norm, w_in, w_out, w_mem_k, w_mem_v, w_pool, pool_scale,
           w_k, w_v, lambda_q1, lambda_k1, lambda_q2, lambda_k2, subln, w_mlp1, w_mlp2):
    import concourse.bacc as bacc
    from concourse.bass_utils import run_bass_kernel_spmd

    f = np.ascontiguousarray
    a = {k: np.asarray(v) for k, v in locals().items() if k not in ("bacc", "run_bass_kernel_spmd", "f")}
    (x_prompt, x_sample, w_in, w_out, w_mem_k, w_mem_v, w_k, w_v, w_mlp1, w_mlp2, w_pool) = (
        a[n] for n in ("x_prompt", "x_sample", "w_in", "w_out", "w_mem_k", "w_mem_v", "w_k", "w_v",
                       "w_mlp1", "w_mlp2", "w_pool"))

    def w_mlp(l):
        up, down = _units(w_mlp1[l]), w_mlp2[l].reshape(BLOCKS, D, D)
        return [m for b in range(BLOCKS) for m in (up[KT * b:KT * b + KT], _units(down[b]))]

    pool_units = np.zeros((MIXT, P, D), np.float32)
    for pair in range(2):
        block = np.zeros((384, 384), np.float32)
        block[:192, :192], block[192:, 192:] = w_pool[0, 2 * pair], w_pool[0, 2 * pair + 1]
        pool_units[3 * pair:3 * pair + 3, :, :POOL_COLS] = _units(block)
    weights = np.concatenate(
        [_units(w_mem_k[0]), _units(w_mem_k[1]), _units(w_mem_v[0]), _units(w_mem_v[1]),
         _units(w_in[0])[IN_ORDER[0]], pool_units[POOL_OUT], _units(w_out[0]), *w_mlp(0),
         _units(w_in[1])[IN_ORDER[1]], _units(w_k), _units(w_v), _units(w_out[1]), *w_mlp(1)])

    tile = lambda v: v.reshape(-1, P).T
    lam = np.concatenate([a[n][0] for n in ("lambda_q1", "lambda_k1", "lambda_q2", "lambda_k2")])
    params = np.concatenate(
        [tile(v) for v in (a["mem_norm"], a["norm1"][0], a["norm2"][0], a["norm1"][1], a["kv_norm"],
                           a["norm2"][1], a["final_norm"], a["pool_scale"][0], a["subln"][0])]
        + [np.broadcast_to(lam, (P, 256))], axis=1)
    tokens = np.concatenate([x_prompt[0], x_sample.reshape(SAMPLE, D)])
    mem_k = a["cache_mem_k"].reshape(2, 4, 2, MEM, 2, 2, HD).transpose(0, 1, 5, 6, 2, 4, 3).reshape(2, 4, P, D)
    mem_v = a["cache_mem_v"].reshape(2, 4, 2, 2, P, 256).transpose(0, 1, 4, 2, 3, 5).reshape(2, 4, P, D)
    n_pool = a["cache_k"].shape[0]
    ins = {
        "x": _lanes(tokens), "mem": _lanes(a["mem_prompt"][0]),
        "hist": a["state_pool"][0].transpose(2, 0, 1).reshape(MIXT, P, REQS, HIST).transpose(1, 0, 2, 3),
        "params": params, "consts": _constants(), "angles": _angles(), "weights": weights,
        "mem_k": mem_k, "mem_v": mem_v,
        "page_k": a["cache_k"].transpose(0, 3, 4, 2, 1).reshape(n_pool, P, 768),
        "page_v": a["cache_v"].reshape(n_pool, P, 768),
        "page_table": a["page_table"].reshape(1, 16),
    }
    outs = {"y": (P, KT, TOK), "pool_prompt": (P, MIXT, HIST), "mem_k_prompt": (P, 2, 2, MEM),
            "mem_v_prompt": (P, 2, 2, MEM), "k": (P, HEADS, TOK), "v_prompt": (P, QT, 768),
            "pool_sample": (P, MIXT, REQS, HIST), "v_sample": (SAMPLE, 768)}
    nc = bacc.Bacc("TRN2", target_bir_lowering=False, num_devices=1)
    arrays = {f"in_{k}": f(v) for k, v in ins.items()}
    args = [nc.dram_tensor(k, v.shape, mybir.dt.from_np(v.dtype), kind="ExternalInput").ap() for k, v in arrays.items()]
    args += [nc.dram_tensor(f"out_{k}", s, mybir.dt.float32, kind="ExternalOutput").ap() for k, s in outs.items()]
    build(nc, *args)
    r = run_bass_kernel_spmd(nc, [arrays], core_ids=[0]).results[0]
    got = {k: np.asarray(r[f"out_{k}"]) for k in outs}

    rows = lambda v: v.transpose(2, 1, 0).reshape(v.shape[2], -1)
    y, k = rows(got["y"]), rows(got["k"])
    mk = got["mem_k_prompt"].transpose(1, 3, 2, 0).reshape(2, 1, MEM, 4, HD)
    mv = got["mem_v_prompt"].transpose(1, 2, 0, 3).reshape(2, 1, MEM, 4, HD)
    ps = got["pool_sample"].transpose(2, 3, 1, 0).reshape(1, REQS, HIST, 768)
    return (f(y[:PROMPT]).reshape(1, PROMPT, D), f(y[PROMPT:]).reshape(REQS, STEPS, D),
            f(rows(got["pool_prompt"])).reshape(1, 1, HIST, 768), f(mk), f(mv),
            f(k[:PROMPT]).reshape(1, PROMPT, HEADS, 2, HD),
            f(got["v_prompt"].transpose(1, 0, 2)).reshape(1, PROMPT, HEADS, 2 * HD), f(ps),
            f(k[PROMPT:]).reshape(REQS, STEPS, HEADS, 2, HD),
            f(got["v_sample"]).reshape(REQS, STEPS, HEADS, 2 * HD))
```

```python
import concourse.bass as bass
from concourse import mybir
from contextlib import ExitStack
import math
import numpy as np

D = 1024
P = 128
KT = D // P
PROMPT, REQS, STEPS = 512, 8, 4
SAMPLE = REQS * STEPS
TOK = PROMPT + SAMPLE
HALF = TOK // 2
SLOTS = 3
SHIFT = 14.0
PAST, PAGE = 256, 128
PAGES = PAST // PAGE
MEM, MEM_PAIRS, HD = 256, 2, 64
MIXT = 6
HIST = 15
WINDOWS = (2, 4, 8, 16)
EXT = 16 + PROMPT + REQS * (HIST + STEPS)
HEADS = 6
QT = PROMPT // P
SCALE = 64 ** -0.5
EPS = 1e-6
NEG = -1e30
CLAMP, BIG, BIG_END = 1.6e18, 2.0 ** -68, 2.0 ** -8
SUB = 2.0 ** -8
LAM_INIT = 0.8 - 0.6 * math.exp(-0.3)

U_MEM, U_IN0, U_POOL, U_OUT0, U_MLP0 = 0, 8, 16, 22, 30
U_IN1, U_K, U_V, U_OUT1, U_MLP1 = 94, 102, 108, 114, 122
N_UNITS = 186
POOL_COLS = 3 * P
BLOCKS = 4
RAW, HL, PS, TS = 4, 2, 2, 4
IN_ORDER = [[6, 7, 4, 5, 3, 1, 2, 0],
            [6, 7, 0, 1, 2, 3, 4, 5]]
POOL_TILES = IN_ORDER[0][2:]
POOL_OUT = [3, 4, 5, 0, 1, 2]

R_MEM, R_IN0, R_MLP0, R_IN1, R_MLP1, R_FINAL = range(6)
G_MEM, G_IN0, G_MLP0, G_IN1, G_KV, G_MLP1, G_FINAL = range(7)

C_GAIN = 0
C_PSCALE = C_GAIN + 7 * KT
C_SUBLN = C_PSCALE + MIXT
C_LAM = C_SUBLN + 1
C_PARAM = C_LAM + 256
GROUP = 40
K_IDENT = 0
K_CAUSAL = K_IDENT + P
K_DMASK = K_CAUSAL + P
K_SEL = K_DMASK + 4 * SAMPLE
K_ROWJ = K_SEL + 2 * GROUP
K_INVW = K_ROWJ + 2
K_TAB = K_INVW + MIXT
K_CONST = K_TAB + MIXT * 16


DECODE_AT = (8, 12, 17, 23)


def attention_items(layer):
    items = [("mem", pr, i) for pr in range(MEM_PAIRS) for i in range(QT)]
    items.insert(1, ("memdec", 0, 0))
    items.insert(6, ("memdec", 1, 0))
    if layer == 1:
        heads = [("diff", h, i) for h in range(HEADS) for i in range(QT)]
        for c in range(REQS // 2):
            heads.insert(DECODE_AT[c], ("decode", c, 0))
        items += heads
    return items


ITEMS = attention_items(0) + attention_items(1)
L0_ITEMS = len(attention_items(0))
EARLY_HEADS = 4
EARLY = QT * EARLY_HEADS
Y_POOL = 3
FIRST_HEAD = 2 * L0_ITEMS


def build(nc, xT, memT, hist, params, consts, ropes, weights, memK, memV, cacheK, cacheV, pages,
          o_y, o_pool, o_memk, o_memv, o_k, o_v, o_pools, o_vs):
    F32, F32R, I32 = mybir.dt.float32, mybir.dt.float32r, mybir.dt.int32
    ALU, ACT, AX = mybir.AluOpType, mybir.ActivationFunctionType, mybir.AxisListType

    ctx = ExitStack()
    with ctx:
        base = nc.sbuf_base
        slab_bytes = 212800
        ctx.enter_context(nc.sbuf_tensor("slab", [P, slab_bytes // 4], F32))
        top = [(base + 31) // 32 * 32]
        end = base + slab_bytes

        def take(n_bytes):
            at = top[0]
            top[0] += (n_bytes + 31) // 32 * 32
            assert top[0] <= end, (top[0], end)
            return at

        def place(name, shape, dt, at):
            return nc.alloc_sbuf_tensor_at(name, shape, dt, offset=at)

        def new(name, shape, dt=F32):
            return place(name, shape, dt, take(4 * math.prod(shape[1:])))

        X = new("residual", [P, KT, TOK])
        a_at, b_at = take(8 * KT * TOK), take(8 * KT * TOK)
        A = place("operand_a", [P, 2, KT, TOK], F32R, a_at)
        B = place("operand_b", [P, 2, KT, TOK], F32R, b_at)
        Z = new("projected", [P, KT, TOK])
        raw = new("weights_raw", [P, RAW, D])
        split = new("weights_split", [P, HL, 2, D], F32R)
        T = new("staging", [P, TS, TOK])
        sq_at = take(12 * TOK)
        SQ = place("squares", [P, 2, TOK], F32, sq_at)
        sq_sum = place("squares_sum", [P, TOK], F32, sq_at + 8 * TOK)
        rms = new("inv_rms", [P, TOK])
        rms_mem_at = take(4 * MEM)
        rms_mem = place("inv_rms_mem", [P, MEM], F32, rms_mem_at)
        kv_at = take(2 * 12288)
        k_at = take(4 * HEADS * TOK)
        memKT = new("mem_keys", [P, 2, MEM_PAIRS, MEM])
        memVt = new("mem_values", [P, 2, 2, MEM])
        QbdM = new("mem_query_blocks", [P, REQS, MEM_PAIRS, 32])
        par = new("params", [P, C_PARAM])
        con = new("constants", [P, K_CONST])
        tiny = new("tiny", [P, 164])
        C2 = new("combine", [P, 2, 2 * GROUP])
        pg = new("page_table", [1, 16], I32)
        ones = new("ones", [P, P])
        Kt = place("keys", [P, HEADS, TOK], F32, k_at)
        line = place("pool_line", [P, 2, EXT], F32, k_at)
        window = place("pool_window", [P, 2, EXT], F32, k_at + 8 * EXT)
        kv = place("cache_tiles", [P, 2, 2, 2 * 768], F32, kv_at)
        swap = place("rotated", [P, MIXT, TOK], F32, kv_at)
        rope = place("cos_sin", [P, 2, TOK], F32, kv_at + 4 * MIXT * TOK)
        partial = place("window_partial", [P, 2, EXT], F32, sq_at)
        memX = place("mem_residual", [P, KT, MEM], F32, kv_at)
        p_new = place("probs_new", [P, REQS, HEADS * STEPS], F32, rms_mem_at)
        histb = new("pool_history", [P, MIXT, REQS, HIST])
        Vt = place("values", [P, QT, 768], F32, a_at)
        Vn = place("values_new", [SAMPLE, 768], F32, a_at + 4 * KT * TOK)
        O = place("attention_out", [P, 24, P], F32, b_at)
        Qbd = place("query_blocks", [P, HEADS, REQS, 64], F32, b_at + 16384)
        Pr = [[place(f"probs_l0_{s}", [P, 2, MEM], F32, a_at + (KT * s + 6) * 4 * TOK) for s in range(2)],
              [place(f"probs_l1_{s}", [P, 2, MEM], F32, k_at + 8 * MEM * s) for s in range(2)],
              [place(f"probs_heads_{s}", [P, 2, 512], F32, b_at + at) for s, at in enumerate((12288, 28672))]]
        Pr[2].append(T[:, 2:4, :].rearrange("p a b -> p (a b)")[:, 0:1024].rearrange("p (a b) -> p a b", a=2))
        PT = [T[:, s, 0:512] for s in range(2)]

        ps = ctx.enter_context(nc.psum_tensor("psum", [P, 8, 512], F32))

        ident = con[:, K_IDENT:K_IDENT + P]
        causal = con[:, K_CAUSAL:K_CAUSAL + P]

        def gain(g, k):
            return par[:, C_GAIN + g * KT + k:C_GAIN + g * KT + k + 1]

        epsc, lam_n, gsub, sgn = tiny[:, 0:1], tiny[:, 1:2], tiny[:, 2:3], tiny[:, 3:4]
        lamw = tiny[:, 4:12]
        ss = tiny[:, 16:40]
        rr = tiny[:, 40:64]
        rr2 = tiny[:, 64:88]
        ss_big, keep = tiny[:, 88:112], tiny[:, 112:136]
        mx, nb, sums, coef = (tiny[:, 136 + 6 * i:142 + 6 * i].rearrange("p (s j) -> p s j", s=SLOTS) for i in range(4))
        ratio = tiny[:, 160:160 + SLOTS]
        exp_shift = tiny[:, 14:16]
        eps_sub = tiny[:, 12:13]
        NS = MIXT * SAMPLE
        small = [T[:, 2 + i // 2, (i % 2) * NS:(i % 2) * NS + NS] for i in range(4)]

        def sem(name):
            return ctx.enter_context(nc.semaphore(name))

        raw_loaded = [sem(f"raw_loaded{i}") for i in range(RAW)]
        weight_hi, weight_lo = sem("weight_hi"), sem("weight_lo")
        unit_done, unit_out = sem("unit_done"), sem("unit_out")
        x_loaded = sem("x_loaded")
        memx_loaded, memx_loaded_late = sem("memx_loaded"), sem("memx_loaded_late")
        par_loaded, con_loaded = sem("par_loaded"), sem("con_loaded")
        hist_loaded, rope_loaded, pg_loaded = sem("hist_loaded"), sem("rope_loaded"), sem("pg_loaded")
        sq_ready, sq_summed = sem("sq_ready"), sem("sq_summed")
        norm_hi, norm_lo = sem("norm_hi"), sem("norm_lo")
        norm_mm, root_ready, rms_ready = sem("norm_mm"), sem("root_ready"), sem("rms_ready")
        hid_hi, hid_lo = sem("hid_hi"), sem("hid_lo")
        mix_hi, mix_lo = sem("mix_hi"), sem("mix_lo")
        out_hi = sem("out_hi")
        cat_hi, cat_lo = sem("cat_hi"), sem("cat_lo")
        memv_turned, memv_ready = sem("memv_turned"), sem("memv_ready")
        v_turned, v_ready = sem("v_turned"), sem("v_ready")
        line_ready, window_ready, pooled = sem("line_ready"), sem("window_ready"), sem("pooled")
        k_loaded = [sem(f"k_loaded{i}") for i in range(2)]
        v_loaded = [sem(f"v_loaded{i}") for i in range(2)]
        qbdm_ready, qbd_ready = sem("qbdm_ready"), sem("qbd_ready")
        q_swapped, k_swapped = sem("q_swapped"), sem("k_swapped")
        q_roped, k_roped = sem("q_roped"), sem("k_roped")
        scored, biased, exped = sem("scored"), sem("biased"), sem("exped")
        weighted, turned, copied = sem("weighted"), sem("turned"), sem("copied")
        mixed, drained = sem("mixed"), sem("drained")
        squared, clamped = sem("squared"), sem("clamped")
        half_scored = sem("half_scored")
        new_mixed, new_added = sem("new_mixed"), sem("new_added")
        sub_mean = sem("sub_mean")
        sub_root, sub_rms, sub_mm = sem("sub_root"), sem("sub_rms"), sem("sub_mm")
        sub_sample = sem("sub_sample")
        sub_scaled, sub_turned = sem("sub_scaled"), sem("sub_turned")
        const_ready = sem("const_ready")
        lam_dot, lam_exp = sem("lam_dot"), sem("lam_exp")
        y_ready, y_pool_ready, y_scaled = sem("y_ready"), sem("y_pool_ready"), sem("y_scaled")
        stored = sem("stored")
        hid_sq = sem("hid_sq")
        v_stored, k_stored = sem("v_stored"), sem("k_stored")
        memk_stored, memv_stored = sem("memk_stored"), sem("memv_stored")
        pool_stored, pools_stored = sem("pool_stored"), sem("pools_stored")
        act_order, dve_order, pool_order = sem("act_order"), sem("dve_order"), sem("pool_order")
        lo_of = lambda k: slice(k * P, (k + 1) * P)

        class Order:

            def __init__(self, eng, s):
                self.eng, self.sem, self.n = eng, s, 0

            def step(self, ins):
                self.n += 1
                ins.then_inc(self.sem, 1)

            def settle(self):
                self.eng.wait_ge(self.sem, self.n)

            def chain(self, ins):
                self.step(ins)
                self.settle()

        def halves(ap):
            return ap.rearrange("p (a b) -> p a b", a=2)

        def unit_cols(u):
            return POOL_COLS if isinstance(u, int) and U_POOL <= u < U_OUT0 else D

        def unit_psum(j):
            return ps[:, 2 * (j % PS):2 * (j % PS) + 2, 0:HALF]

        chunks = ([("mem", 0, c) for c in range(4)] + [("mem", 1, c) for c in range(4)]
                  + [("page", 0, b) for b in range(REQS)])

        def chunk_ready(eng, loaded, n):
            done = 16 * (n // 2 + 1) if n < 8 else 16 * 4 + 32 * ((n - 8) // 2 + 1)
            eng.wait_ge(loaded[n % 2], done)

        def chunk_of(n):
            kind, a, _ = ITEMS[n]
            l = int(n >= L0_ITEMS)
            return 4 * l + 2 * a if kind == "memdec" else 8 + 2 * a

        def slots(n):
            return SLOTS if n >= FIRST_HEAD else 2

        def probs(n):
            return Pr[2 if n >= FIRST_HEAD else int(n >= L0_ITEMS)][n % slots(n)]

        def score_banks(n):
            if n < FIRST_HEAD:
                return ps[:, 4 + n % 2, :].rearrange("p (j k) -> p j k", j=2)
            return ps[:, 2 * (n % SLOTS):2 * (n % SLOTS) + 2, :]

        EARLY_DONE = FIRST_HEAD + ITEMS[FIRST_HEAD:].index(("diff", EARLY_HEADS - 1, QT - 1)) + 3

        DEC = [n for n, it in enumerate(ITEMS) if it[0] in ("memdec", "decode")]

        block = ctx.enter_context(nc.Block())

        @block.sync
        def _(sp):
            def load(u, first):
                s = u % RAW
                if not first:
                    sp.wait_ge(weight_lo, u - RAW + 1)
                n = unit_cols(u)
                sp.dma_start(raw[:, s, 0:n], weights[u][:, 0:n]).then_inc(raw_loaded[s], 16)

            def load_units(a, b):
                while a < b and (a % RAW or a < RAW):
                    load(a, a < RAW)
                    a += 1
                turns = (b - a) // RAW
                if turns > 1:
                    with sp.Fori(0, turns) as t:
                        for s in range(RAW):
                            u = t * RAW + (a + s)
                            sp.wait_ge(weight_lo, u - RAW + 1)
                            sp.dma_start(raw[:, s, :], weights[u]).then_inc(raw_loaded[s], 16)
                    a += turns * RAW
                while a < b:
                    load(a, False)
                    a += 1

            def load_chunks(n):
                at = DEC.index(n)
                if n == DEC[4]:
                    sp.wait_ge(k_roped, 1)
                    sp.wait_ge(q_roped, 1)
                c0 = chunk_of(n)
                for part, mem_part, pages_part, loaded, used in ((0, memK, cacheK, k_loaded, scored),
                                                                 (1, memV, cacheV, v_loaded, mixed)):
                    if at >= 1:
                        sp.wait_ge(used, DEC[at - 1] + 1)
                    for c in (c0, c0 + 1):
                        s = c % 2
                        kind, l, i = chunks[c]
                        if kind == "mem":
                            sp.dma_start(kv[:, s, part, 0:1024], mem_part[l, i]).then_inc(loaded[s], 16)
                        else:
                            for g in range(PAGES):
                                page = sp.value_load(pg[0:1, PAGES * i + g:PAGES * i + g + 1], min_val=0,
                                                     max_val=cacheK.shape[0] - 1)
                                sp.dma_start(kv[:, s, part, g * 768:(g + 1) * 768], pages_part[page])\
                                    .then_inc(loaded[s], 16)

            sp.dma_start(par[:, :], params).then_inc(par_loaded, 16)
            sp.dma_start(memX[:, 0:KT // 2, :], memT[:, 0:KT // 2, :]).then_inc(memx_loaded, 16)
            load_units(0, 1)
            sp.dma_start(memX[:, KT // 2:KT, :], memT[:, KT // 2:KT, :]).then_inc(memx_loaded_late, 16)
            load_units(1, 2)
            sp.dma_start(X[:, :, :], xT).then_inc(x_loaded, 16)
            load_units(2, 4)
            sp.dma_start(con[:, :], consts).then_inc(con_loaded, 16)
            sp.dma_start(pg[:, :], pages).then_inc(pg_loaded, 16)
            load_units(4, 12)
            sp.dma_start(histb[:, :, :, :], hist).then_inc(hist_loaded, 16)
            sp.wait_ge(norm_lo, KT)
            sp.wait_ge(sq_ready, KT)
            load_chunks(DEC[0])
            load_units(12, 16)
            load_chunks(DEC[1])
            load_units(16, U_OUT0)
            load_chunks(DEC[2])
            load_units(U_OUT0, U_K)
            load_chunks(DEC[3])
            load_units(U_K, U_K + 3)
            sp.wait_ge(mixed, DEC[3] + 1)
            sp.dma_start(rope[:, :, :], ropes).then_inc(rope_loaded, 16)
            load_units(U_K + 3, U_OUT1 + HL)
            sp.wait_ge(pg_loaded, 16)
            for n in DEC[4:]:
                load_chunks(n)
            load_units(U_OUT1 + HL, N_UNITS)
            for k in range(KT):
                if k < KT - Y_POOL:
                    sp.wait_ge(y_ready, k + 1)
                else:
                    sp.wait_ge(y_pool_ready, k - (KT - Y_POOL) + 1)
                sp.dma_start(o_y[:, k, :], Z[:, k, :]).then_inc(stored, 16)
            sp.wait_ge(stored, 16 * KT)

        @block.tensor
        def _(pe):
            def unit(u, j, act, kts=tuple(range(KT)), cols=TOK, ready=None, base_kt=0, first=False, mid=None):
                pe.wait_ge(weight_lo, u + 1)
                if not first:
                    pe.wait_ge(unit_out, u - PS + 1)
                n = cols // 2 if cols == TOK else cols
                for q, k in enumerate(kts):
                    if ready:
                        ready(k)
                    if mid and q == len(kts) // 2:
                        mid()
                    w = lambda r: split[:, j % HL, r, lo_of(k - base_kt)]
                    for wr, ar in ((0, 0), (0, 1), (1, 0)):
                        for hf in range(cols // n):
                            mm = pe.matmul(ps[:, 2 * (j % PS) + hf, 0:n], w(wr), act[:, ar, k, hf * n:(hf + 1) * n],
                                           start=(q == 0 and wr == 0 and ar == 0),
                                           stop=(q == len(kts) - 1 and wr == 1))
                mm.then_inc(unit_done, 1)

            def norm_sum(r, cols=TOK):
                last = r == R_FINAL
                pe.wait_ge(sq_summed, (KT - 1) * (r + 1) - last)
                n = cols // 2 if cols == TOK else cols
                for hf in range(cols // n):
                    mm = pe.matmul(ps[:, 6 + hf, 0:n], ones[:, :], sq_sum[:, hf * n:(hf + 1) * n],
                                   start=True, stop=not last)
                if last:
                    pe.wait_ge(sq_ready, KT * (r + 1))
                    for hf in range(2):
                        mm = pe.matmul(ps[:, 6 + hf, 0:n], ones[:, :], SQ[:, (KT - 1) % 2, hf * n:(hf + 1) * n],
                                       start=False, stop=True)
                mm.then_inc(norm_mm, 1)

            def normed(g):
                return lambda k: pe.wait_ge(norm_lo, KT * g + k + 1)

            def mlp(u0, h2, hidden, g, r, done):
                def block_(i, u, first):
                    for j in range(KT):
                        unit(u + j, u0 + j, h2, ready=normed(g) if first and j == 0 else None)
                        if first and j == 0:
                            norm_sum(r)
                    for j in range(KT):
                        ready = (lambda k: pe.wait_ge(hid_lo, i * KT + (done + k + 1))) if j == 0 else None
                        unit(u + (KT + j), u0 + j, hidden, ready=ready)

                block_(0, u0, True)
                with pe.Fori(1, BLOCKS) as i:
                    block_(i, i * (2 * KT) + u0, False)

            def scores(n):
                kind, a, i = ITEMS[n]
                l = int(n >= L0_ITEMS)
                sc = score_banks(n)
                if n >= slots(n):
                    pe.wait_ge(exped, n - slots(n) + 1)
                if kind == "mem":
                    for hh in range(2):
                        lane = slice(64 * hh, 64 * hh + 64)
                        if hh:
                            pe.wait_ge(half_scored, QT * (MEM_PAIRS * l + a) + i + 1)
                        mm = pe.matmul(sc[:, hh, 0:MEM], Z[lane, 6 + a, i * P:(i + 1) * P],
                                       memKT[lane, l, a, :], start=True, stop=True)
                        if hh == 0:
                            mm.then_inc(half_scored, 1)
                elif kind == "memdec":
                    pe.wait_ge(qbdm_ready, l + 1)
                    for b in range(4):
                        c = chunk_of(n) + b // 2
                        chunk_ready(pe, k_loaded, c)
                        for pr in range(MEM_PAIRS):
                            at = (b % 2) * 512 + pr * MEM
                            mm = pe.matmul(sc[32 * b:32 * b + 32, 0, 0:MEM], QbdM[:, 4 * a + b, pr, :],
                                           kv[:, c % 2, 0, at:at + MEM], start=(pr == 0), stop=(pr == 1))
                elif kind == "diff":
                    for j in range(2):
                        lane = slice(64 * j, 64 * j + 64)
                        mm = pe.matmul(sc[:, j, 0:(i + 1) * P], Z[lane, a, i * P:(i + 1) * P],
                                       Kt[lane, a, 0:(i + 1) * P], start=True, stop=True)
                else:
                    pe.wait_ge(qbd_ready, 1)
                    for o in range(2):
                        c = chunk_of(n) + o
                        chunk_ready(pe, k_loaded, c)
                        keys = kv[:, c % 2, 0, :].rearrange("p (g h k) -> p h g k", g=PAGES, h=HEADS)
                        for h in range(HEADS):
                            pe.matmul(sc[64 * o:64 * o + 64, 0, 0:PAST].rearrange("p (g k) -> p g k", g=PAGES),
                                      Qbd[:, h, 2 * a + o, :], keys[:, h, :, :], start=(h == 0), stop=(h == 5))
                    for h in range(HEADS):
                        mm = pe.matmul(sc[:, 0, PAST:PAST + SAMPLE], Qbd[:, h, 2 * a:2 * a + 2, :],
                                       Kt[:, h, PROMPT:TOK], start=(h == 0), stop=(h == 5))
                mm.then_inc(scored, 1)

            def turn(n):
                kind, a, i = ITEMS[n]
                l = int(n >= L0_ITEMS)
                t0 = 6
                pr = probs(n)
                pe.wait_ge(weighted, n + 1)
                if n >= 1:
                    pe.wait_ge(copied, n)
                if kind == "mem":
                    for kt in range(2):
                        for hh in range(2):
                            at = (2 * kt + hh) * P
                            mm = pe.transpose(ps[:, t0, at:at + P], pr[:, hh, lo_of(kt)], ident)
                elif kind == "memdec":
                    for kt in range(2):
                        mm = pe.transpose(ps[:, t0, lo_of(kt)], pr[:, 0, lo_of(kt)], ident)
                elif kind == "diff":
                    for kt in range(i + 1):
                        mm = pe.transpose(ps[:, t0, lo_of(kt)], pr[:, 0, lo_of(kt)], ident)
                else:
                    for kt in range(2):
                        pe.matmul(ps[:, t0, 2 * GROUP * kt:2 * GROUP * (kt + 1)], pr[:, 0, lo_of(kt)], C2[:, n % 2, :],
                                  start=True, stop=True)
                    mm = pe.matmul(ps[0:SAMPLE, t0, 4 * GROUP:6 * GROUP], pr[:, 0, PAST:PAST + SAMPLE], C2[:, n % 2, :],
                                   start=True, stop=True)
                mm.then_inc(turned, 1)

            def mix(n):
                kind, a, i = ITEMS[n]
                l = int(n >= L0_ITEMS)
                m0 = 7
                pt = PT[n % 2]
                pe.wait_ge(copied, n + 1)
                if n >= 1:
                    pe.wait_ge(drained, n)
                if kind == "mem":
                    for hh in range(2):
                        for kt in range(2):
                            mm = pe.matmul(ps[64 * hh:64 * hh + 64, m0, 0:P],
                                           memVt[:, l, kt, a * P + 64 * hh:a * P + 64 * hh + 64],
                                           pt[:, (2 * kt + hh) * P:(2 * kt + hh + 1) * P],
                                           start=(kt == 0), stop=(kt == 1))
                elif kind == "memdec":
                    for b in range(4):
                        c = chunk_of(n) + b // 2
                        chunk_ready(pe, v_loaded, c)
                        for pr in range(MEM_PAIRS):
                            out = (pr * 4 + b) * 32
                            for kt in range(2):
                                at = (b % 2) * 512 + kt * MEM + pr * P
                                mm = pe.matmul(ps[:, m0, out:out + 32], kv[:, c % 2, 1, at:at + P],
                                               pt[:, kt * P + 32 * b:kt * P + 32 * b + 32],
                                               start=(kt == 0), stop=(kt == 1))
                elif kind == "diff":
                    for kt in range(i + 1):
                        mm = pe.matmul(ps[:, m0, 0:P], pt[:, lo_of(kt)], Vt[:, kt, a * P:(a + 1) * P],
                                       start=(kt == 0), stop=(kt == i))
                else:
                    for h in range(HEADS):
                        for o in range(2):
                            c = chunk_of(n) + o
                            if h == 0:
                                chunk_ready(pe, v_loaded, c)
                            out = GROUP * (2 * h + o)
                            for kt in range(2):
                                mm = pe.matmul(ps[:, m0, out:out + GROUP],
                                               kv[:, c % 2, 1, kt * 768 + h * P:kt * 768 + (h + 1) * P],
                                               pt[:, GROUP * (2 * kt + o):GROUP * (2 * kt + o + 1)],
                                               start=(kt == 0), stop=(kt == 1))
                mm.then_inc(mixed, 1)

            def mix_new(n):
                pe.wait_ge(copied, DEC[-1] + 1)
                pe.wait_ge(exped, n)
                for h in range(HEADS):
                    mm = pe.matmul(ps[:, 2 * ((n - 1) % SLOTS), SAMPLE * h:SAMPLE * (h + 1)]
                                   .rearrange("p (b t) -> p b t", b=REQS), Vn[:, h * P:(h + 1) * P],
                                   p_new[0:SAMPLE, :, STEPS * h:STEPS * (h + 1)], start=True, stop=True)
                mm.then_inc(new_mixed, 1)

            def attention(n0, n1):
                for n in range(n0, n1):
                    if n + 2 < n1:
                        scores(n + 2)
                    turn(n)
                    if n > n0:
                        mix(n - 1)
                    if n == n1 - 1:
                        mix_new(n)
                mix(n1 - 1)

            def cat_ready(k):
                if k >= 6:
                    pe.wait_ge(cat_lo, 1)
                else:
                    pe.wait_ge(unit_out, U_POOL + POOL_OUT.index(k) + 1)

            pe.wait_ge(const_ready, 1)
            for u in range(8):
                unit(u, u, A, cols=MEM, ready=normed(G_MEM) if u == 0 else None, first=u < PS)
                if u == 0:
                    norm_sum(R_MEM, MEM)
            pe.wait_ge(con_loaded, 16)
            def memory_step(n0, at):
                if at == "start":
                    scores(n0)
                    scores(n0 + 1)
                    return
                turn(n0 + at)
                if at + 2 < L0_ITEMS:
                    scores(n0 + at + 2)
                if at:
                    mix(n0 + at - 1)

            for j in range(KT):
                mid = (lambda: memory_step(0, "start" if j == 2 else 2 * (j - 3))) if j >= 2 else None
                unit(U_IN0 + j, j, B, ready=normed(G_IN0) if j == 0 else None, mid=mid)
                if j == 0:
                    pe.wait_ge(root_ready, 1)
                    norm_sum(R_IN0)
                if j == 1:
                    pe.wait_ge(root_ready, 2)
                    for m in range(4):
                        for kt in range(2):
                            mm = pe.transpose(ps[:, 6 + m // 2, (kt * 2 + m % 2) * P:(kt * 2 + m % 2 + 1) * P],
                                              T[:, m, lo_of(kt)], ident)
                    mm.then_inc(memv_turned, 1)
                if j == 2:
                    pe.wait_ge(memv_ready, 2)
                if j >= 3:
                    memory_step(0, 2 * (j - 3) + 1)
            mix(L0_ITEMS - 1)
            for j, o in enumerate(POOL_OUT):
                pair = o // 3
                kts = [3 * pair + k for k in ((0, 1), (0, 1, 2), (1, 2))[o % 3]]
                pe.wait_ge(mix_lo, 3 * (j // 3) + 3)
                unit(U_POOL + j, j, A, kts=kts, base_kt=3 * pair)
            for j in range(KT):
                unit(U_OUT0 + j, j, B, kts=(6, 7, *POOL_OUT), ready=cat_ready if j == 0 else None)
            mlp(U_MLP0, A, B, G_MLP0, R_MLP0, 0)
            for j in range(KT):
                mid = (lambda: memory_step(L0_ITEMS, "start" if j == 2 else 2 * (j - 3))) if j >= 2 else None
                unit(U_IN1 + j, j, A, ready=normed(G_IN1) if j == 0 else None, mid=mid)
                if j == 0:
                    norm_sum(R_IN1)
                if j == 2:
                    pe.wait_ge(root_ready, R_IN1 + 1)
                if j >= 3:
                    memory_step(L0_ITEMS, 2 * (j - 3) + 1)
            mix(FIRST_HEAD - 1)
            for j in range(MIXT):
                unit(U_K + j, j, B, ready=normed(G_KV) if j == 0 else None)
            for j in range(MIXT + 1):
                if j < MIXT:
                    unit(U_V + j, j, B)
                if j >= 1:
                    h = j - 1
                    if h == MIXT - 1:
                        pe.wait_ge(q_roped, 1)
                        pe.wait_ge(k_roped, 1)
                        pe.wait_ge(v_ready, h)
                        pe.wait_ge(unit_out, U_V + h)
                        scores(FIRST_HEAD)
                        scores(FIRST_HEAD + 1)
                    pe.wait_ge(unit_out, U_V + h + 1)
                    if h == 0:
                        pe.wait_ge(drained, FIRST_HEAD)
                    if h >= 2:
                        pe.wait_ge(v_ready, h - 1)
                    for t in range(QT):
                        pe.transpose(ps[:, 4 + 2 * (h % 2), lo_of(t)], T[:, h % TS, lo_of(t)], ident)
                    pe.transpose(ps[0:SAMPLE, 5 + 2 * (h % 2), 0:P], T[:, h % TS, PROMPT:TOK], ident)\
                        .then_inc(v_turned, 1)
            pe.wait_ge(unit_out, U_OUT1)
            pe.wait_ge(v_ready, MIXT)
            attention(FIRST_HEAD, len(ITEMS))
            pe.wait_ge(drained, len(ITEMS))
            def turn_head(h):
                pe.wait_ge(sub_scaled, h + 1)
                for i in range(QT):
                    mm = pe.transpose(ps[:, h, lo_of(i)], O[:, QT * h + i, :], ident)
                mm.then_inc(sub_turned, 1)

            for h in range(2):
                turn_head(h)
            pe.wait_ge(squared, QT * HEADS + 1)
            pe.matmul(ps[:, 6, 0:NS], ones[:, :], SQ[:, 0, 0:NS], start=True, stop=True)
            pe.matmul(ps[:, 7, 0:NS], ones[:, :], SQ[:, 1, 0:NS], start=True, stop=True).then_inc(sub_mm, 1)
            for h in range(2, HEADS):
                turn_head(h)
            pe.wait_ge(cat_lo, 2)
            pe.wait_ge(mix_lo, MIXT + 4)

            def head_ready(k):
                if k in (3, 4, 5):
                    pe.wait_ge(mix_lo, MIXT + k + 2)

            for j in range(KT):
                unit(U_OUT1 + j, j, A, kts=(6, 7, 0, 1, 2, 3, 4, 5), ready=head_ready if j == 0 else None)
            mlp(U_MLP1, B, A, G_MLP1, R_MLP1, BLOCKS * KT)
            norm_sum(R_FINAL)

        @block.scalar
        def _(act):
            own = Order(act, act_order)

            def weight_high(u, s, turn_value, first=False):
                act.wait_ge(raw_loaded[s], turn_value)
                if not first:
                    act.wait_ge(unit_done, u - HL + 1)
                n = unit_cols(u)
                act.activation(split[:, s % HL, 0, 0:n], raw[:, s, 0:n], ACT.Copy).then_inc(weight_hi, 1)

            def high(u):
                if u < N_UNITS:
                    weight_high(u, u % RAW, 16 * (u // RAW + 1), u < HL)

            def norm_high(g, k, src, dst):
                act.activation(dst, src, ACT.Copy, scale=gain(g, k)).then_inc(norm_hi, 1)

            def square(r, k, src, cols):
                if k >= 2 or r:
                    act.wait_ge(sq_summed, (KT - 1) * r + (max(k - 2, 1) if k >= 2 else 0))
                act.activation(SQ[:, k % 2, 0:cols], src, ACT.Square).then_inc(sq_ready, 1)

            def root(r, cols=TOK):
                act.wait_ge(norm_mm, r + 1)
                if r == R_MEM:
                    act.activation(rms_mem[:, :], ps[:, 6, 0:MEM], ACT.Sqrt, bias=epsc, scale=1.0 / D)\
                        .then_inc(root_ready, 1)
                else:
                    act.activation(halves(rms[:, :]), ps[:, 6:8, 0:HALF], ACT.Sqrt, bias=epsc, scale=1.0 / D)\
                        .then_inc(root_ready, 1)

            def residual_tile(u, o, r, gs):
                act.wait_ge(unit_out, u + 1)
                for g, dst in gs:
                    norm_high(g, o, X[:, o, :], dst[:, 0, o, :])
                square(r, o, X[:, o, :], TOK)

            def mlp(u0, hidden, r, nr, gs):
                def turn(i, j):
                    return i * 64 + 16 * ((u0 + j + HL) // RAW + 1)

                for j in range(KT):
                    weight_high(u0 + j + HL, (u0 + j + HL) % RAW, turn(0, j))
                    if j == 0:
                        root(r)
                    act.wait_ge(unit_out, u0 + j + 1)
                    act.activation(hidden[:, 0, j, :], T[:, j % TS, :], ACT.Square).then_inc(hid_hi, 1)
                with act.Fori(0, BLOCKS - 1) as i:
                    u = i * (2 * KT) + u0
                    for j in range(KT, 2 * KT):
                        weight_high(u + (j + HL), (u0 + j + HL) % RAW, turn(i, j))
                    for j in range(KT):
                        act.wait_ge(unit_out, u + (2 * KT + j + 1))
                        act.activation(hidden[:, 0, j, :], T[:, j % TS, :], ACT.Square).then_inc(hid_hi, 1)
                        weight_high(u + (2 * KT + j + HL), (u0 + j + HL) % RAW, turn(i, 2 * KT + j))
                u = u0 + (BLOCKS - 1) * 2 * KT
                for j in range(KT):
                    residual_tile(u + KT + j, j, nr, gs)
                    high(u + KT + j + HL)

            def items_exp(n):
                kind, a, i = ITEMS[n]
                l = int(n >= L0_ITEMS)
                act.wait_ge(biased, n + 1)
                if n >= slots(n):
                    act.wait_ge(turned, n - slots(n) + 1)
                s, pr, sc = n % SLOTS, probs(n), score_banks(n)
                n_keys = {"mem": MEM, "memdec": MEM, "diff": (i + 1) * P, "decode": PAST + SAMPLE}[kind]
                for j in range(1 if kind in ("memdec", "decode") else 2):
                    ins = act.activation(pr[:, j, 0:n_keys], sc[:, j, 0:n_keys], ACT.Exp,
                                         bias=nb[:, s, j:j + 1], scale=SCALE, accum_out=sums[:, s, j:j + 1])
                ins.then_inc(exped, 1)

            def items_copy(n):
                kind, a, i = ITEMS[n]
                act.wait_ge(turned, n + 1)
                if n >= 2:
                    act.wait_ge(mixed, n - 1)
                t0 = 6
                cols = {"mem": 512, "memdec": 256, "diff": (i + 1) * P, "decode": 4 * GROUP}[kind]
                if kind == "decode":
                    src = ps[0:SAMPLE, t0, 4 * GROUP:6 * GROUP].rearrange("p (o c) -> p o c", o=2)
                    own.step(act.activation(p_new[0:SAMPLE, 2 * a:2 * a + 2, :], src[:, :, 0:HEADS * STEPS], ACT.Copy))
                act.activation(PT[n % 2][:, 0:cols], ps[:, t0, 0:cols], ACT.Copy).then_inc(copied, 1)

            def items_square(n):
                kind, a, i = ITEMS[n]
                if kind == "diff":
                    k = QT * a + i
                    act.wait_ge(clamped, k + 1)
                    if k:
                        act.wait_ge(squared, k)
                    own.step(act.activation(SQ[:, 1, 0:P], SQ[:, 0, k % 2 * P:k % 2 * P + P], ACT.Square,
                                            accum_out=ss[:, k:k + 1]))
                    act.activation(SQ[:, 1, P:2 * P], O[:, k, :], ACT.Square, scale=BIG,
                                   accum_out=ss_big[:, k:k + 1]).then_inc(squared, 1)

            def attention(n0, n1):
                items_exp(n0)
                for n in range(n0, n1 + 3):
                    if n + 1 < n1:
                        items_exp(n + 1)
                    if n < n1:
                        items_copy(n)
                    if n0 <= n - 3:
                        items_square(n - 3)
                    if n == EARLY_DONE + 2:
                        act.wait_ge(sub_mean, 1)
                        act.activation(rr[:, 0:EARLY], ss[:, 0:EARLY], ACT.Sqrt, bias=eps_sub, scale=SUB)\
                           .then_inc(sub_root, 1)

            act.wait_ge(const_ready, 1)
            own.step(act.activation(tiny[:, 13:14], epsc, ACT.Square))
            act.wait_ge(memx_loaded, 16)
            act.wait_ge(par_loaded, 16)
            for k in range(KT):
                if k == KT // 2:
                    high(0)
                    act.wait_ge(memx_loaded_late, 16)
                norm_high(G_MEM, k, memX[:, k, :], A[:, 0, k, 0:MEM])
                square(R_MEM, k, memX[:, k, :], MEM)
            high(1)
            root(R_MEM)
            act.wait_ge(x_loaded, 16)
            for u in range(8):
                high(u + HL)
                norm_high(G_IN0, u, X[:, u, :], B[:, 0, u, :])
                square(R_IN0, u, X[:, u, :], TOK)
            act.wait_ge(lam_dot, 1)
            act.activation(lamw[:, 2:4], lamw[:, 0:2], ACT.Exp).then_inc(lam_exp, 1)
            def memory_step(n0, at):
                if at + 1 < L0_ITEMS:
                    items_exp(n0 + at + 1)
                items_copy(n0 + at)

            def pool_line(q):
                if q == 0:
                    act.wait_ge(hist_loaded, 16)
                if q >= 2:
                    act.wait_ge(pooled, q - 1)
                o = POOL_TILES[q]
                ln = line[:, q % 2, :]
                reqs = ln[:, 16 + PROMPT:EXT].rearrange("p (b t) -> p b t", b=REQS)
                act.wait_ge(unit_out, U_IN0 + q + 3)
                act.activation(ln[:, 16:16 + PROMPT], Z[:, o, 0:PROMPT], ACT.Copy).then_inc(line_ready, 1)
                act.activation(reqs[:, :, 0:HIST], histb[:, o, :, :], ACT.Copy).then_inc(line_ready, 1)
                act.activation(reqs[:, :, HIST:HIST + STEPS],
                               Z[:, o, PROMPT:TOK].rearrange("p (b t) -> p b t", b=REQS), ACT.Copy)\
                   .then_inc(line_ready, 1)

            def pool_high(q):
                act.wait_ge(pooled, q + 1)
                act.activation(A[:, 0, POOL_TILES[q], :], T[:, 2 + q % 2, :], ACT.Copy).then_inc(mix_hi, 1)

            for j in range(KT):
                if j == 2:
                    items_exp(0)
                if j >= 3:
                    memory_step(0, 2 * (j - 3))
                high(U_IN0 + j + HL)
                if j == 0:
                    root(R_IN0)
                if j == 1:
                    act.wait_ge(memv_turned, 1)
                    for l in range(2):
                        act.activation(memVt[:, l, :, :], ps[:, 6 + l, :].rearrange("p (k f) -> p k f", k=2), ACT.Copy)\
                           .then_inc(memv_ready, 1)
                if j >= 3:
                    memory_step(0, 2 * (j - 3) + 1)
                if j >= 5:
                    pool_high(j - 5)
                if j >= 2:
                    pool_line(j - 2)
            pool_high(3)
            act.wait_ge(drained, L0_ITEMS)
            act.activation(B[:, 0, 6:8, :], Z[:, 6:8, :], ACT.Copy).then_inc(cat_hi, 1)
            pool_high(4)
            pool_high(5)
            for j, o in enumerate(POOL_OUT):
                act.wait_ge(unit_done, U_POOL + j + 1)
                act.activation(halves(B[:, 0, o, :]), unit_psum(j), ACT.Copy,
                               scale=par[:, C_PSCALE + o:C_PSCALE + o + 1]).then_inc(out_hi, 1)
                high(U_POOL + j + HL)
            for j in range(KT):
                residual_tile(U_OUT0 + j, j, R_MLP0, [(G_MLP0, A)])
                high(U_OUT0 + j + HL)
            mlp(U_MLP0, B, R_MLP0, R_IN1, [(G_IN1, A)])
            for j in range(KT):
                if j == 2:
                    items_exp(L0_ITEMS)
                if j >= 3:
                    memory_step(L0_ITEMS, 2 * (j - 3))
                high(U_IN1 + j + HL)
                if j == 0:
                    root(R_IN1)
                norm_high(G_KV, j, X[:, j, :], B[:, 0, j, :])
                if j >= 3:
                    memory_step(L0_ITEMS, 2 * (j - 3) + 1)
            for j in range(MIXT):
                high(U_K + j + HL)
            for j in range(MIXT + 1):
                if j < MIXT:
                    high(U_V + j + HL)
                if j == 0:
                    act.wait_ge(drained, FIRST_HEAD)
                    act.activation(A[:, 0, 6:8, :], Z[:, 6:8, :], ACT.Copy).then_inc(cat_hi, 1)
                if j >= 1:
                    h = j - 1
                    act.wait_ge(v_turned, h + 1)
                    own.step(act.activation(Vt[:, :, h * P:(h + 1) * P],
                                            ps[:, 4 + 2 * (h % 2), :].rearrange("p (t e) -> p t e", t=QT), ACT.Copy))
                    act.activation(Vn[:, h * P:(h + 1) * P], ps[0:SAMPLE, 5 + 2 * (h % 2), 0:P], ACT.Copy)\
                       .then_inc(v_ready, 1)
            attention(FIRST_HEAD, len(ITEMS))

            def head_high(h):
                act.wait_ge(sub_turned, h + 1)
                act.activation(A[:, 0, h, 0:PROMPT], ps[:, h, :], ACT.Copy, scale=gsub).then_inc(mix_hi, 1)

            act.wait_ge(sub_mean, 2)
            act.wait_ge(squared, QT * HEADS)
            own.step(act.activation(SQ[:, 0, 0:NS], small[0], ACT.Square))
            act.activation(SQ[:, 1, 0:NS].rearrange("p (h t) -> p h t", h=MIXT), Z[:, 0:MIXT, PROMPT:TOK], ACT.Square,
                           scale=BIG).then_inc(squared, 1)
            act.wait_ge(sub_mean, 3)
            act.activation(rr[:, EARLY:], ss[:, EARLY:], ACT.Sqrt, bias=eps_sub, scale=SUB).then_inc(sub_root, 1)
            act.wait_ge(v_stored, 32)
            head_high(0)
            act.wait_ge(sub_mean, 4)
            act.activation(small[0], small[1], ACT.Sqrt, bias=eps_sub, scale=SUB).then_inc(sub_root, 1)
            for h in range(1, HEADS):
                head_high(h)
            act.wait_ge(sub_sample, 1)
            act.activation(A[:, 0, 0:MIXT, PROMPT:TOK], Z[:, 0:MIXT, PROMPT:TOK], ACT.Copy, scale=gsub)\
               .then_inc(mix_hi, 1)
            for j in range(KT):
                residual_tile(U_OUT1 + j, j, R_MLP1, [(G_MLP1, B)])
                high(U_OUT1 + j + HL)
            mlp(U_MLP1, A, R_MLP1, R_FINAL, [])
            root(R_FINAL)

        @block.vector
        def _(dve):
            own = Order(dve, dve_order)

            def weight_rest(u, s, first=False):
                dve.wait_ge(weight_hi, u + 1)
                n = unit_cols(u)
                dve.tensor_tensor(split[:, s % HL, 1, 0:n], raw[:, s, 0:n], split[:, s % HL, 0, 0:n].bitcast(F32),
                                  ALU.subtract).then_inc(weight_lo, 1)

            def rest(u):
                if u < N_UNITS:
                    weight_rest(u, u % RAW)

            def norm_rest(g, k, src, dst):
                dve.wait_ge(norm_hi, KT * g + k + 1)
                dve.scalar_tensor_tensor(out=dst[1], in0=src, scalar=gain(g, k), in1=dst[0].bitcast(F32),
                                         op0=ALU.mult, op1=ALU.subtract).then_inc(norm_lo, 1)

            def pair_of(op, k, cols=TOK):
                return op[:, 0, k, 0:cols], op[:, 1, k, 0:cols]

            def inverse(r):
                dve.wait_ge(root_ready, r + 1)
                t = rms_mem[:, :] if r == R_MEM else rms[:, :]
                dve.reciprocal(t, t).then_inc(rms_ready, 1)

            def add_residual(u, j, o):
                dve.wait_ge(unit_done, u + 1)
                dve.tensor_tensor(halves(X[:, o, :]), unit_psum(j), halves(X[:, o, :]), ALU.add).then_inc(unit_out, 1)

            def out_units(u0, g, dst):
                for j in range(KT):
                    add_residual(u0 + j, u0 + j, j)
                    norm_rest(g, j, X[:, j, :], pair_of(dst, j))
                    rest(u0 + j + HL)

            def mlp(u0, r, g, dst):
                def hidden(u, j, n):
                    dve.wait_ge(unit_done, u + 1)
                    dve.wait_ge(hid_lo, n)
                    dve.scalar_tensor_tensor(out=halves(T[:, j % TS, :]), in0=unit_psum(j), scalar=0.0,
                                             in1=halves(rms[:, :]), op0=ALU.max, op1=ALU.mult).then_inc(unit_out, 1)

                n0 = BLOCKS * KT * (u0 == U_MLP1)
                inverse(r)
                dve.wait_ge(rms_ready, r + 1)
                for j in range(KT):
                    if j < TS:
                        dve.wait_ge(unit_done, u0 + j + 1)
                        dve.scalar_tensor_tensor(out=halves(T[:, j % TS, :]), in0=unit_psum(j), scalar=0.0,
                                                 in1=halves(rms[:, :]), op0=ALU.max, op1=ALU.mult).then_inc(unit_out, 1)
                    else:
                        hidden(u0 + j, j, n0 + j - TS + 1)
                    weight_rest(u0 + j + HL, (u0 + j + HL) % RAW)
                with dve.Fori(0, BLOCKS - 1) as i:
                    u = i * (2 * KT) + u0
                    for j in range(KT):
                        dve.wait_ge(unit_done, u + (KT + j + 1))
                        dve.wait_ge(unit_out, u + (j + 1 - KT))
                        dve.tensor_tensor(halves(X[:, j, :]), unit_psum(j), halves(X[:, j, :]), ALU.add)\
                           .then_inc(unit_out, 1)
                        weight_rest(u + (KT + j + HL), (u0 + KT + j + HL) % RAW)
                    for j in range(KT):
                        hidden(u + (2 * KT + j), j, i * KT + (n0 + KT + j - TS + 1))
                        weight_rest(u + (2 * KT + j + HL), (u0 + j + HL) % RAW)
                u = u0 + (BLOCKS - 1) * 2 * KT
                for j in range(KT):
                    dve.wait_ge(unit_out, u + j + 1 - KT)
                    add_residual(u + KT + j, j, j)
                    if g is not None:
                        norm_rest(g, j, X[:, j, :], pair_of(dst, j))
                    rest(u + KT + j + HL)

            def items_weight(n):
                kind, a, i = ITEMS[n]
                s, pr = n % SLOTS, probs(n)
                nj = 1 if kind in ("memdec", "decode") else 2
                dve.wait_ge(exped, n + 1)
                if n >= FIRST_HEAD + SLOTS:
                    dve.wait_ge(drained, n - SLOTS + 1)
                own.chain(dve.reciprocal(coef[:, s, 0:nj], sums[:, s, 0:nj]))
                if kind == "mem":
                    for j in range(2):
                        ins = dve.tensor_scalar(pr[:, j, 0:MEM], pr[:, j, 0:MEM], coef[:, s, j:j + 1], None, ALU.mult)
                elif kind == "memdec":
                    ins = dve.tensor_scalar(pr[:, 0, 0:MEM], pr[:, 0, 0:MEM], coef[:, s, 0:1], None, ALU.mult)
                elif kind == "diff":
                    k = (i + 1) * P
                    own.chain(dve.tensor_scalar(ratio[:, s:s + 1], sums[:, s, 0:1], coef[:, s, 1:2], lam_n,
                                                ALU.mult, ALU.mult))
                    ins = dve.scalar_tensor_tensor(out=pr[:, 0, 0:k], in0=pr[:, 1, 0:k], scalar=ratio[:, s:s + 1],
                                                   in1=pr[:, 0, 0:k], op0=ALU.mult, op1=ALU.add)
                else:
                    own.chain(dve.tensor_scalar(coef[:, s, 1:2], coef[:, s, 0:1], sgn, None, ALU.mult))
                    ins = dve.tensor_scalar(C2[:, n % 2, :], con[:, K_SEL:K_SEL + 2 * GROUP], coef[:, s, 1:2], None, ALU.mult)
                ins.then_inc(weighted, 1)

            def items_bias(n):
                kind, a, i = ITEMS[n]
                s, sc = n % SLOTS, score_banks(n)
                dve.wait_ge(scored, n + 1)
                if kind == "diff":
                    at = sc[:, :, i * P:(i + 1) * P]
                    own.chain(dve.tensor_tensor(at, at, causal.unsqueeze(1).to_broadcast([P, 2, P]), ALU.add))
                if kind == "decode":
                    at = sc[:, 0, PAST:PAST + SAMPLE]
                    m = K_DMASK + a * SAMPLE
                    own.chain(dve.tensor_tensor(at, at, con[:, m:m + SAMPLE], ALU.add))
                n_keys = {"mem": MEM, "memdec": MEM, "diff": (i + 1) * P, "decode": PAST + SAMPLE}[kind]
                if kind in ("mem", "diff"):
                    own.chain(dve.tensor_reduce(mx[:, s, :], sc[:, :, 0:n_keys], AX.X, ALU.max))
                else:
                    own.chain(dve.tensor_reduce(mx[:, s, 0:1], sc[:, 0, 0:n_keys], AX.X, ALU.max))
                if kind == "diff":
                    ins = dve.scalar_tensor_tensor(out=nb[:, s, :], in0=mx[:, s, :], scalar=-SCALE, in1=exp_shift,
                                                   op0=ALU.mult, op1=ALU.add)
                else:
                    nj = 2 if kind == "mem" else 1
                    ins = dve.tensor_scalar(nb[:, s, 0:nj], mx[:, s, 0:nj], -SCALE, None, ALU.mult)
                ins.then_inc(biased, 1)

            def items_drain(n):
                kind, a, i = ITEMS[n]
                dve.wait_ge(mixed, n + 1)
                if kind == "mem":
                    ins = dve.tensor_copy(Z[:, 6 + a, i * P:(i + 1) * P], ps[:, 7, 0:P])
                elif kind == "memdec":
                    for hh in range(2):
                        lane = slice(64 * hh, 64 * hh + 64)
                        for pr in range(MEM_PAIRS):
                            grid = ps[lane, 7, P * pr:P * pr + P].rearrange("p (b c) -> p b c", b=4)
                            src = grid[:, :, 8 * pr + 4 * hh:8 * pr + 4 * hh + 4]
                            dst = Z[lane, 6 + pr, PROMPT + 16 * a:PROMPT + 16 * a + 16].rearrange("p (b t) -> p b t", b=4)
                            ins = dve.tensor_copy(dst, src)
                elif kind == "diff":
                    s = n % SLOTS
                    ins = dve.tensor_scalar(O[:, QT * a + i, :], ps[:, 7, 0:P], coef[:, s, 0:1], None, ALU.mult)
                else:
                    for h in range(HEADS):
                        src = ps[:, 7, 2 * GROUP * h:2 * GROUP * (h + 1)].rearrange("p (o c) -> p o c", o=2)[:, :, 4 * h:4 * h + 4]
                        dst = Z[:, h, PROMPT + 8 * a:PROMPT + 8 * a + 8].rearrange("p (o t) -> p o t", o=2)
                        ins = dve.tensor_copy(dst, src)
                ins.then_inc(drained, 1)

            def means(total, total_big, mean, scratch, keep):
                own.step(dve.tensor_scalar(keep, total_big, BIG_END, SUB ** 0.5, ALU.is_lt, ALU.mult))
                own.step(dve.tensor_scalar(mean, total, 1.0 / P, None, ALU.mult))
                own.chain(dve.tensor_scalar(scratch, total_big, BIG_END, 2.0 ** 100, ALU.min, ALU.mult))
                dve.scalar_tensor_tensor(out=mean, in0=scratch, scalar=2.0 ** 36 / P, in1=mean, op0=ALU.mult,
                                         op1=ALU.max).then_inc(sub_mean, 1)

            def head_factors(k0, k1, roots):
                dve.wait_ge(sub_root, roots)
                own.chain(dve.reciprocal(rr2[:, k0:k1], rr[:, k0:k1]))
                dve.tensor_tensor(rr2[:, k0:k1], rr2[:, k0:k1], keep[:, k0:k1], ALU.mult).then_inc(sub_rms, 1)
                dve.wait_ge(sub_rms, roots)

            def scale_head(h):
                rows = slice(QT * h, QT * h + QT)
                dve.tensor_tensor(O[:, rows, :], O[:, rows, :], rr2[:, rows].unsqueeze(2).to_broadcast([P, QT, P]),
                                  ALU.mult).then_inc(sub_scaled, 1)

            def attention(n0, n1):
                items_bias(n0)
                items_bias(n0 + 1)
                for n in range(n0, n1 + 2):
                    if n < n1:
                        items_weight(n)
                    if n - 2 >= n0:
                        items_drain(n - 2)
                    if n + 2 < n1:
                        items_bias(n + 2)
                    if n == EARLY_DONE + 1:
                        dve.wait_ge(squared, EARLY)
                        means(ss[:, 0:EARLY], ss_big[:, 0:EARLY], ss[:, 0:EARLY], rr2[:, 0:EARLY], keep[:, 0:EARLY])
                    if n == EARLY_DONE + 3:
                        head_factors(0, EARLY, 1)
                        for h in range(EARLY_HEADS):
                            scale_head(h)
                dve.wait_ge(new_mixed, 1)
                dve.wait_ge(drained, DEC[-1] + 1)
                zs = Z[:, 0:MIXT, PROMPT:TOK]
                new = ps[:, 2 * ((n1 - 2) % SLOTS), 0:NS].rearrange("p (h t) -> p h t", h=MIXT)
                dve.tensor_tensor(zs, zs, new, ALU.add).then_inc(new_added, 1)

            def memory_step(n0, at):
                if at == "start":
                    items_bias(n0)
                    items_bias(n0 + 1)
                    items_weight(n0)
                    return
                if at + 1 < L0_ITEMS:
                    items_weight(n0 + at + 1)
                if at + 2 < L0_ITEMS:
                    items_bias(n0 + at + 2)
                if at:
                    items_drain(n0 + at - 1)

            def pool_rest(q):
                dve.wait_ge(mix_hi, q + 1)
                o = POOL_TILES[q]
                dve.tensor_tensor(A[:, 1, o, :], T[:, 2 + q % 2, :], A[:, 0, o, :].bitcast(F32),
                                  ALU.subtract).then_inc(mix_lo, 1)

            def pool_mean(q):
                dve.wait_ge(window_ready, q + 1)
                if q >= 2:
                    dve.wait_ge(mix_lo, q - 1)
                o = POOL_TILES[q]
                ln, wd, t = line[:, q % 2, :], window[:, q % 2, :], T[:, 2 + q % 2, :]
                inv = con[:, K_INVW + o:K_INVW + o + 1]
                own.step(dve.scalar_tensor_tensor(out=t[:, 16:PROMPT], in0=wd[:, 32:16 + PROMPT], scalar=inv,
                                                  in1=ln[:, 32:16 + PROMPT], op0=ALU.mult, op1=ALU.subtract))
                sample = lambda v: v[:, 16 + PROMPT:EXT].rearrange("p (b t) -> p b t", b=REQS)[:, :, HIST:HIST + STEPS]
                own.step(dve.scalar_tensor_tensor(out=t[:, PROMPT:TOK].rearrange("p (b t) -> p b t", b=REQS),
                                                  in0=sample(wd), scalar=inv, in1=sample(ln), op0=ALU.mult,
                                                  op1=ALU.subtract))
                own.chain(dve.tensor_tensor(t[:, 0:16], wd[:, 16:32], con[:, K_TAB + 16 * o:K_TAB + 16 * o + 16],
                                            ALU.mult))
                dve.tensor_tensor(t[:, 0:16], t[:, 0:16], ln[:, 16:32], ALU.subtract).then_inc(pooled, 1)

            dve.wait_ge(memx_loaded, 16)
            dve.wait_ge(par_loaded, 16)
            for k in range(KT):
                if k == KT // 2:
                    rest(0)
                    dve.wait_ge(memx_loaded_late, 16)
                norm_rest(G_MEM, k, memX[:, k, :], pair_of(A, k, MEM))
            rest(1)
            lam = par[:, C_LAM:C_LAM + 256].rearrange("p (v d) -> p v d", v=4)
            own.chain(dve.tensor_tensor(T[:, 0, 0:64], lam[:, 0, :], lam[:, 1, :], ALU.mult))
            own.chain(dve.tensor_tensor(T[:, 0, 64:128], lam[:, 2, :], lam[:, 3, :], ALU.mult))
            dve.tensor_reduce(lamw[:, 0:2], T[:, 0, 0:128].rearrange("p (v d) -> p v d", v=2), AX.X, ALU.add)\
               .then_inc(lam_dot, 1)
            inverse(R_MEM)
            dve.wait_ge(x_loaded, 16)
            dve.wait_ge(rms_ready, 1)
            for u in range(8):
                dve.wait_ge(unit_done, u + 1)
                dst = memKT[:, u // 2, u % 2, :] if u < 4 else T[:, u - 4, 0:MEM]
                if u == 4:
                    dve.wait_ge(lam_dot, 1)
                dve.tensor_tensor(dst, ps[:, 2 * (u % PS), 0:MEM], rms_mem[:, :], ALU.mult).then_inc(unit_out, 1)
                rest(u + HL)
                norm_rest(G_IN0, u, X[:, u, :], pair_of(B, u))
            inverse(R_IN0)
            dve.wait_ge(lam_exp, 1)
            dve.wait_ge(rms_ready, 2)
            own.chain(dve.tensor_tensor(lamw[:, 4:5], lamw[:, 2:3], lamw[:, 3:4], ALU.subtract))
            own.step(dve.tensor_scalar(gsub, par[:, C_SUBLN:C_SUBLN + 1], 1.0 - LAM_INIT, None, ALU.mult))
            own.chain(dve.tensor_scalar(lam_n, lamw[:, 4:5], LAM_INIT, -1.0, ALU.add, ALU.mult))
            dve.wait_ge(con_loaded, 16)
            own.chain(dve.tensor_scalar(sgn, con[:, K_ROWJ + 1:K_ROWJ + 2], lam_n, None, ALU.mult))
            own.chain(dve.tensor_tensor(sgn, sgn, con[:, K_ROWJ:K_ROWJ + 1], ALU.add))
            for j in range(KT):
                if j >= 2:
                    memory_step(0, "start" if j == 2 else 2 * (j - 3))
                dve.wait_ge(unit_done, U_IN0 + j + 1)
                dve.tensor_tensor(halves(Z[:, IN_ORDER[0][j], :]), unit_psum(j), halves(rms[:, :]), ALU.mult)\
                   .then_inc(unit_out, 1)
                rest(U_IN0 + j + HL)
                if j >= 3:
                    memory_step(0, 2 * (j - 3) + 1)
                if j >= 6:
                    pool_rest(j - 6)
                if j >= 4:
                    pool_mean(j - 4)
            items_drain(L0_ITEMS - 1)
            pool_rest(2)
            dve.wait_ge(cat_hi, 1)
            dve.tensor_tensor(B[:, 1, 6:8, :], Z[:, 6:8, :], B[:, 0, 6:8, :].bitcast(F32), ALU.subtract)\
               .then_inc(cat_lo, 1)
            pool_rest(3)
            pool_mean(4)
            pool_mean(5)
            pool_rest(4)
            pool_rest(5)
            for j, o in enumerate(POOL_OUT):
                dve.wait_ge(out_hi, j + 1)
                dve.scalar_tensor_tensor(out=halves(B[:, 1, o, :]), in0=unit_psum(j),
                                         scalar=par[:, C_PSCALE + o:C_PSCALE + o + 1],
                                         in1=halves(B[:, 0, o, :].bitcast(F32)), op0=ALU.mult, op1=ALU.subtract)\
                   .then_inc(unit_out, 1)
                rest(U_POOL + j + HL)
            out_units(U_OUT0, G_MLP0, A)
            mlp(U_MLP0, R_MLP0, G_IN1, A)
            inverse(R_IN1)
            dve.wait_ge(rms_ready, R_IN1 + 1)
            dve.wait_ge(pool_stored, 16)
            for j in range(KT):
                if j >= 2:
                    memory_step(L0_ITEMS, "start" if j == 2 else 2 * (j - 3))
                dve.wait_ge(unit_done, U_IN1 + j + 1)
                dve.tensor_tensor(halves(Z[:, IN_ORDER[1][j], :]), unit_psum(j), halves(rms[:, :]), ALU.mult)\
                   .then_inc(unit_out, 1)
                rest(U_IN1 + j + HL)
                norm_rest(G_KV, j, X[:, j, :], pair_of(B, j))
                if j >= 3:
                    memory_step(L0_ITEMS, 2 * (j - 3) + 1)
            items_drain(FIRST_HEAD - 1)
            for j in range(MIXT):
                dve.wait_ge(unit_done, U_K + j + 1)
                dve.tensor_tensor(halves(Kt[:, j, :]), unit_psum(j), halves(rms[:, :]), ALU.mult).then_inc(unit_out, 1)
                rest(U_K + j + HL)
            for j in range(MIXT):
                dve.wait_ge(unit_done, U_V + j + 1)
                if j >= TS:
                    dve.wait_ge(v_turned, j - TS + 1)
                dve.tensor_tensor(halves(T[:, j % TS, :]), unit_psum(j), halves(rms[:, :]), ALU.mult)\
                   .then_inc(unit_out, 1)
                rest(U_V + j + HL)
                if j == 0:
                    dve.wait_ge(k_swapped, 64)
                for h in ([j] if j < 4 else [4, 5] if j == 4 else []):
                    own.step(dve.tensor_tensor(swap[:, h, :], swap[:, h, :], rope[:, 1, :], ALU.mult))
                    own.chain(dve.tensor_tensor(Kt[:, h, :], Kt[:, h, :], rope[:, 0, :], ALU.mult))
                    ins = dve.tensor_tensor(Kt[:, h, :], Kt[:, h, :], swap[:, h, :], ALU.add)
                if j == 4:
                    ins.then_inc(k_roped, 1)
                if j == 1:
                    dve.wait_ge(cat_hi, 2)
                    dve.tensor_tensor(A[:, 1, 6:8, :], Z[:, 6:8, :], A[:, 0, 6:8, :].bitcast(F32), ALU.subtract)\
                       .then_inc(cat_lo, 1)
            attention(FIRST_HEAD, len(ITEMS))
            zs = Z[:, 0:MIXT, PROMPT:TOK]
            grid = lambda v: v.rearrange("p (h t) -> p h t", h=MIXT)
            dve.wait_ge(drained, len(ITEMS))
            dve.wait_ge(new_added, 1)
            dve.tensor_scalar(grid(small[0]), zs, CLAMP, -CLAMP, ALU.min, ALU.max).then_inc(sub_mean, 1)

            dve.wait_ge(squared, QT * HEADS)
            means(ss[:, EARLY:], ss_big[:, EARLY:], ss[:, EARLY:], rr2[:, EARLY:], keep[:, EARLY:])
            dve.wait_ge(sub_mm, 1)
            means(ps[:, 6, 0:NS], ps[:, 7, 0:NS], small[1], small[2], small[3])
            head_factors(EARLY, QT * HEADS, 2)
            for h in range(EARLY_HEADS, HEADS):
                scale_head(h)
            dve.wait_ge(sub_root, 3)
            own.chain(dve.reciprocal(small[0], small[0]))
            own.chain(dve.tensor_tensor(small[0], small[0], small[3], ALU.mult))
            dve.tensor_tensor(zs, zs, grid(small[0]), ALU.mult).then_inc(sub_sample, 1)
            for h in range(HEADS):
                if h == 3:
                    dve.wait_ge(mix_hi, 2 * MIXT + 1)
                    dve.scalar_tensor_tensor(out=A[:, 1, 0:MIXT, PROMPT:TOK], in0=zs, scalar=gsub,
                                             in1=A[:, 0, 0:MIXT, PROMPT:TOK].bitcast(F32), op0=ALU.mult,
                                             op1=ALU.subtract).then_inc(mix_lo, 1)
                dve.wait_ge(mix_hi, MIXT + h + 1)
                dve.scalar_tensor_tensor(out=A[:, 1, h, 0:PROMPT], in0=ps[:, h, :], scalar=gsub,
                                         in1=A[:, 0, h, 0:PROMPT].bitcast(F32), op0=ALU.mult, op1=ALU.subtract)\
                   .then_inc(mix_lo, 1)
            out_units(U_OUT1, G_MLP1, B)
            mlp(U_MLP1, R_MLP1, None, None)
            inverse(R_FINAL)
            dve.wait_ge(rms_ready, R_FINAL + 1)
            for k in range(KT - Y_POOL):
                dve.scalar_tensor_tensor(out=Z[:, k, :], in0=X[:, k, :], scalar=gain(G_FINAL, k), in1=rms[:, :],
                                         op0=ALU.mult, op1=ALU.mult).then_inc(y_ready, 1)

        @block.gpsimd
        def _(pool):
            own = Order(pool, pool_order)

            def sum_squares(r, cols=TOK):
                if r:
                    pool.wait_ge(norm_mm, r)
                for k in range(1, KT - (r == R_FINAL)):
                    pool.wait_ge(sq_ready, KT * r + k + 1)
                    if k >= 2:
                        pool.wait_ge(sq_summed, (KT - 1) * r + k - 1)
                    a = SQ[:, 0, 0:cols] if k == 1 else sq_sum[:, 0:cols]
                    pool.tensor_tensor(sq_sum[:, 0:cols], a, SQ[:, k % 2, 0:cols], ALU.add).then_inc(sq_summed, 1)

            def hidden_rest(hidden, j, n):
                pool.wait_ge(hid_hi, n)
                t = T[:, j % TS, :]
                sq = SQ[:, j % 2, :]
                pool.tensor_tensor(sq, t, t, ALU.mult).then_inc(hid_sq, 1)
                pool.wait_ge(hid_sq, n)
                pool.tensor_tensor(hidden[:, 1, j, :], sq, hidden[:, 0, j, :].bitcast(F32), ALU.subtract)\
                    .then_inc(hid_lo, 1)

            def mlp(u0, hidden, r):
                n0 = BLOCKS * KT * (u0 == U_MLP1)
                with pool.Fori(0, BLOCKS) as i:
                    for j in range(KT):
                        hidden_rest(hidden, j, i * KT + (n0 + j + 1))
                sum_squares(r)

            def rotate(swapped, dst):
                for q in range(4):
                    pool.dma_start(swap[32 * q:32 * q + 32, :, :], dst[32 * (q ^ 1):32 * (q ^ 1) + 32, 0:MIXT, :])\
                        .then_inc(swapped, 16)

            def query_blocks(layer):
                for hh in range(2):
                    lane = slice(64 * hh, 64 * hh + 64)
                    for pr in range(MEM_PAIRS):
                        c = 8 * pr + 4 * hh
                        ins = pool.tensor_copy(QbdM[lane, :, pr, c:c + STEPS],
                                               Z[lane, 6 + pr, PROMPT:TOK].rearrange("p (b t) -> p b t", b=REQS))
                        if (hh, pr) != (1, 1):
                            own.chain(ins)
                ins.then_inc(qbdm_ready, 1)
                pool.wait_ge(qbdm_ready, layer + 1)

            own.step(pool.memset(epsc, EPS))
            own.step(pool.memset(eps_sub, EPS * SUB))
            own.step(pool.memset(exp_shift[:, 0:1], -SHIFT))
            own.step(pool.memset(exp_shift[:, 1:2], 0.0))
            own.step(pool.memset(line[:, :, 0:16], 0.0))
            own.step(pool.memset(QbdM[:, :, :, :], 0.0))
            pool.memset(ones[:, :], 1.0).then_inc(const_ready, 1)
            sum_squares(R_MEM, MEM)
            sum_squares(R_IN0)
            pool.wait_ge(unit_out, 4)
            pool.dma_start(o_memk, memKT[:, :, :, :]).then_inc(memk_stored, 16)
            pool.wait_ge(unit_out, U_IN0 + 2)
            own.settle()
            query_blocks(0)
            pool.wait_ge(memv_ready, 2)
            pool.dma_start(o_memv, memVt[:, :, :, :]).then_inc(memv_stored, 16)
            for q, o in enumerate(POOL_TILES):
                pool.wait_ge(line_ready, 3 * (q + 1))
                if q >= 2:
                    pool.wait_ge(pooled, q - 1)
                ln, wd = line[:, q % 2, :], window[:, q % 2, :]
                lo_w, hi_w = WINDOWS[(2 * o) // 3], WINDOWS[(2 * o + 1) // 3]
                parts = [(0, P, lo_w)] if lo_w == hi_w else [(0, 64, lo_w), (64, P, hi_w)]
                for p0, p1, w in parts:
                    src, shift, n = ln, 1, 0
                    while shift < w:
                        last = 2 * shift == w
                        dst = wd if last else partial[:, n % 2, :]
                        t0 = 16 if last else 2 * shift - 1
                        if n:
                            own.settle()
                        own.step(pool.tensor_tensor(dst[p0:p1, t0:EXT], src[p0:p1, t0:EXT],
                                                    src[p0:p1, t0 - shift:EXT - shift], ALU.add))
                        src, shift, n = dst, 2 * shift, n + 1
                    own.settle()
                reqs = ln[:, 16 + PROMPT:EXT].rearrange("p (b t) -> p b t", b=REQS)
                pool.tensor_copy(histb[:, o, :, :], reqs[:, :, STEPS:STEPS + HIST]).then_inc(window_ready, 1)
            pool.wait_ge(unit_out, U_POOL)
            pool.dma_start(o_pool, Z[:, 0:MIXT, PROMPT - HIST:PROMPT]).then_inc(pool_stored, 16)
            pool.wait_ge(window_ready, MIXT)
            pool.dma_start(o_pools, histb[:, :, :, :]).then_inc(pools_stored, 16)
            sum_squares(R_MLP0)
            mlp(U_MLP0, B, R_IN1)
            pool.wait_ge(unit_out, U_IN1 + 2)
            query_blocks(1)
            pool.wait_ge(unit_out, U_K)
            pool.wait_ge(mixed, DEC[3] + 1)
            rotate(q_swapped, Z)
            pool.wait_ge(q_swapped, 64)
            pool.wait_ge(rope_loaded, 16)
            for h in range(HEADS):
                own.step(pool.tensor_tensor(swap[:, h, :], swap[:, h, :], rope[:, 1, :], ALU.mult))
                own.chain(pool.tensor_tensor(Z[:, h, :], Z[:, h, :], rope[:, 0, :], ALU.mult))
                ins = pool.tensor_tensor(Z[:, h, :], Z[:, h, :], swap[:, h, :], ALU.add)
                if h < HEADS - 1:
                    own.step(ins)
            ins.then_inc(q_roped, 1)
            pool.wait_ge(q_roped, 1)
            pool.wait_ge(unit_out, U_V)
            rotate(k_swapped, Kt)
            pool.wait_ge(unit_done, U_OUT1)
            own.chain(pool.memset(Qbd[:, :, :, :], 0.0))
            for h in range(HEADS):
                for j in range(2):
                    lane = slice(64 * j, 64 * j + 64)
                    c = 8 * h + 4 * j
                    ins = pool.tensor_copy(Qbd[lane, h, :, c:c + STEPS],
                                           Z[lane, h, PROMPT:TOK].rearrange("p (b t) -> p b t", b=REQS))
                    if (h, j) != (HEADS - 1, 1):
                        own.chain(ins)
            ins.then_inc(qbd_ready, 1)
            pool.wait_ge(qbd_ready, 1)
            pool.wait_ge(v_ready, MIXT)
            pool.dma_start(o_v, Vt[:, :, :]).then_inc(v_stored, 16)
            pool.dma_start(o_vs, Vn[:, :]).then_inc(v_stored, 16)
            pool.wait_ge(k_roped, 1)
            pool.dma_start(o_k, Kt[:, :, :]).then_inc(k_stored, 16)
            for n, (kind, a, i) in enumerate(ITEMS):
                if kind == "diff":
                    k = QT * a + i
                    pool.wait_ge(drained, n + 1)
                    if k >= 2:
                        pool.wait_ge(squared, k - 1)
                    pool.tensor_scalar(SQ[:, 0, k % 2 * P:k % 2 * P + P], O[:, k, :], CLAMP, -CLAMP, ALU.min, ALU.max)\
                        .then_inc(clamped, 1)
            sum_squares(R_MLP1)
            mlp(U_MLP1, A, R_FINAL)
            for k in range(KT - Y_POOL, KT):
                pool.wait_ge(unit_out, N_UNITS - KT + k + 1)
                pool.tensor_scalar(Z[:, k, :], X[:, k, :], gain(G_FINAL, k), None, ALU.mult).then_inc(y_scaled, 1)
            pool.wait_ge(rms_ready, R_FINAL + 1)
            for i, k in enumerate(range(KT - Y_POOL, KT)):
                pool.wait_ge(y_scaled, i + 1)
                pool.tensor_tensor(Z[:, k, :], Z[:, k, :], rms[:, :], ALU.mult).then_inc(y_pool_ready, 1)
            for s, n in ((memk_stored, 16), (memv_stored, 16), (pool_stored, 16), (pools_stored, 16),
                         (v_stored, 32), (k_stored, 16)):
                pool.wait_ge(s, n)

    return nc


def _units(w):
    k, m = w.shape
    return w.reshape(k // P, P, m // P, P).transpose(2, 1, 0, 3).reshape(m // P, P, k)


def _lanes(v):
    return v.T.reshape(-1, P, v.shape[0]).transpose(1, 0, 2)


def _constants():
    c = np.zeros((P, K_CONST), np.float32)
    c[:, K_IDENT:K_IDENT + P] = np.eye(P)
    c[:, K_CAUSAL:K_CAUSAL + P] = np.where(np.arange(P)[None, :] > np.arange(P)[:, None], NEG, 0.0)
    for row in range(P):
        o, rest = divmod(row, 64)
        h, j, t = rest // 8, rest % 8 // 4, rest % 4
        if h >= HEADS:
            continue
        for a in range(4):
            for key in range(SAMPLE):
                if not (key // STEPS == 2 * a + o and key % STEPS <= t):
                    c[row, K_DMASK + a * SAMPLE + key] = NEG
        c[row, K_SEL + o * GROUP + h * 4 + t] = 1.0
        c[row, K_ROWJ + j] = 1.0
    for tile in range(MIXT):
        w = np.array([WINDOWS[(tile * P + p) // 192] for p in range(P)])
        c[:, K_INVW + tile] = 1.0 / w
        c[:, K_TAB + 16 * tile:K_TAB + 16 * tile + 16] = 1.0 / np.minimum(w[:, None], np.arange(16)[None, :] + 1)
    return c


def _angles():
    inv = (1.0 / (np.float32(10000.0) ** (np.arange(0, HD, 2, dtype=np.float32) / np.float32(HD)))).astype(np.float32)
    pos = np.concatenate([np.arange(PROMPT), np.tile(PAST + np.arange(STEPS), REQS)]).astype(np.float32)
    ang = (pos[None, :] * inv[np.arange(P) % 32][:, None]).astype(np.float32).astype(np.float64)
    sign = np.where(np.arange(P) % HD < 32, -1.0, 1.0)[:, None]
    return np.stack([np.cos(ang), sign * np.sin(ang)], axis=1).astype(np.float32)


def kernel(x_prompt, x_sample, state_pool, cache_mem_k, cache_mem_v, cache_k, cache_v, page_table, mem_prompt,
           norm1, norm2, final_norm, kv_norm, mem_norm, w_in, w_out, w_mem_k, w_mem_v, w_pool, pool_scale,
           w_k, w_v, lambda_q1, lambda_k1, lambda_q2, lambda_k2, subln, w_mlp1, w_mlp2):
    import concourse.bacc as bacc
    from concourse.bass_utils import run_bass_kernel_spmd

    f = np.ascontiguousarray
    a = {k: np.asarray(v) for k, v in locals().items() if k not in ("bacc", "run_bass_kernel_spmd", "f")}
    (x_prompt, x_sample, w_in, w_out, w_mem_k, w_mem_v, w_k, w_v, w_mlp1, w_mlp2, w_pool) = (
        a[n] for n in ("x_prompt", "x_sample", "w_in", "w_out", "w_mem_k", "w_mem_v", "w_k", "w_v",
                       "w_mlp1", "w_mlp2", "w_pool"))

    def w_mlp(l):
        up, down = _units(w_mlp1[l]), w_mlp2[l].reshape(BLOCKS, D, D)
        return [m for b in range(BLOCKS) for m in (up[KT * b:KT * b + KT], _units(down[b]))]

    pool_units = np.zeros((MIXT, P, D), np.float32)
    for pair in range(2):
        block = np.zeros((384, 384), np.float32)
        block[:192, :192], block[192:, 192:] = w_pool[0, 2 * pair], w_pool[0, 2 * pair + 1]
        pool_units[3 * pair:3 * pair + 3, :, :POOL_COLS] = _units(block)
    weights = np.concatenate(
        [_units(w_mem_k[0]), _units(w_mem_k[1]), _units(w_mem_v[0]), _units(w_mem_v[1]),
         _units(w_in[0])[IN_ORDER[0]], pool_units[POOL_OUT], _units(w_out[0]), *w_mlp(0),
         _units(w_in[1])[IN_ORDER[1]], _units(w_k), _units(w_v), _units(w_out[1]), *w_mlp(1)])

    tile = lambda v: v.reshape(-1, P).T
    lam = np.concatenate([a[n][0] for n in ("lambda_q1", "lambda_k1", "lambda_q2", "lambda_k2")])
    params = np.concatenate(
        [tile(v) for v in (a["mem_norm"], a["norm1"][0], a["norm2"][0], a["norm1"][1], a["kv_norm"],
                           a["norm2"][1], a["final_norm"], a["pool_scale"][0], a["subln"][0])]
        + [np.broadcast_to(lam, (P, 256))], axis=1)
    tokens = np.concatenate([x_prompt[0], x_sample.reshape(SAMPLE, D)])
    mem_k = a["cache_mem_k"].reshape(2, 4, 2, MEM, 2, 2, HD).transpose(0, 1, 5, 6, 2, 4, 3).reshape(2, 4, P, D)
    mem_v = a["cache_mem_v"].reshape(2, 4, 2, 2, P, 256).transpose(0, 1, 4, 2, 3, 5).reshape(2, 4, P, D)
    n_pool = a["cache_k"].shape[0]
    ins = {
        "x": _lanes(tokens), "mem": _lanes(a["mem_prompt"][0]),
        "hist": a["state_pool"][0].transpose(2, 0, 1).reshape(MIXT, P, REQS, HIST).transpose(1, 0, 2, 3),
        "params": params, "consts": _constants(), "angles": _angles(), "weights": weights,
        "mem_k": mem_k, "mem_v": mem_v,
        "page_k": a["cache_k"].transpose(0, 3, 4, 2, 1).reshape(n_pool, P, 768),
        "page_v": a["cache_v"].reshape(n_pool, P, 768),
        "page_table": a["page_table"].reshape(1, 16),
    }
    outs = {"y": (P, KT, TOK), "pool_prompt": (P, MIXT, HIST), "mem_k_prompt": (P, 2, 2, MEM),
            "mem_v_prompt": (P, 2, 2, MEM), "k": (P, HEADS, TOK), "v_prompt": (P, QT, 768),
            "pool_sample": (P, MIXT, REQS, HIST), "v_sample": (SAMPLE, 768)}
    nc = bacc.Bacc("TRN2", target_bir_lowering=False, num_devices=1)
    arrays = {f"in_{k}": f(v) for k, v in ins.items()}
    args = [nc.dram_tensor(k, v.shape, mybir.dt.from_np(v.dtype), kind="ExternalInput").ap() for k, v in arrays.items()]
    args += [nc.dram_tensor(f"out_{k}", s, mybir.dt.float32, kind="ExternalOutput").ap() for k, s in outs.items()]
    build(nc, *args)
    r = run_bass_kernel_spmd(nc, [arrays], core_ids=[0]).results[0]
    got = {k: np.asarray(r[f"out_{k}"]) for k in outs}

    rows = lambda v: v.transpose(2, 1, 0).reshape(v.shape[2], -1)
    y, k = rows(got["y"]), rows(got["k"])
    mk = got["mem_k_prompt"].transpose(1, 3, 2, 0).reshape(2, 1, MEM, 4, HD)
    mv = got["mem_v_prompt"].transpose(1, 2, 0, 3).reshape(2, 1, MEM, 4, HD)
    ps = got["pool_sample"].transpose(2, 3, 1, 0).reshape(1, REQS, HIST, 768)
    return (f(y[:PROMPT]).reshape(1, PROMPT, D), f(y[PROMPT:]).reshape(REQS, STEPS, D),
            f(rows(got["pool_prompt"])).reshape(1, 1, HIST, 768), f(mk), f(mv),
            f(k[:PROMPT]).reshape(1, PROMPT, HEADS, 2, HD),
            f(got["v_prompt"].transpose(1, 0, 2)).reshape(1, PROMPT, HEADS, 2 * HD), f(ps),
            f(k[PROMPT:]).reshape(REQS, STEPS, HEADS, 2, HD),
            f(got["v_sample"]).reshape(REQS, STEPS, HEADS, 2 * HD))
```
